# Optimizing a Trainium2 kernel written in Bass

```python
import math
import jax, jax.numpy as jnp
from jax import lax
import numpy as np

D_MODEL = 1024
BATCH = 1
SEQ = 256
DEPTH = 2

HEAD_DIM = 64
EPS = 1e-6
DA_HEADS = 4
DA_QK = HEAD_DIM
DA_V = 2 * HEAD_DIM
DA_WIDTH = DA_HEADS * DA_V
Q_BLOCK = 128
ROPE_THETA = 500000.0
ROT_DIM = HEAD_DIM // 4
SC_WIDTH = 256
SC_GROUPS = 4
CONV_W = 3
GLA_HEADS = 4
GLA_DK = 32
GLA_DV = 64
GLA_KW = GLA_HEADS * GLA_DK
GLA_VW = GLA_HEADS * GLA_DV
GLA_GATE_RANK = 16
GLA_GATE_TEMP = 16.0
GLA_CHUNK = 64
MIX_WIDTH = DA_WIDTH + SC_WIDTH + GLA_VW
IN_SIZES = (DA_HEADS * 2 * DA_QK, DA_HEADS * 2 * DA_QK, DA_WIDTH,
            SC_WIDTH, SC_WIDTH, SC_WIDTH,
            GLA_KW, GLA_KW, GLA_VW, GLA_VW, GLA_GATE_RANK)
IN_WIDTH = 3088
PEER_HEADS = 8
PEER_NKEYS = 128
PEER_EXPERTS = PEER_NKEYS * PEER_NKEYS
PEER_HALF = 128
PEER_QDIM = 2 * PEER_HALF
PEER_TOPK = 16
PEER_TOKEN_BLOCK = 128


def rmsnorm(x, g):
    xf = x.astype(jnp.float32)
    y = xf * lax.rsqrt(jnp.mean(xf * xf, axis=-1, keepdims=True) + EPS)
    return (y * g.astype(jnp.float32)).astype(x.dtype)

def rope_tables(positions):
    inv = ROPE_THETA ** (-jnp.arange(0, ROT_DIM, 2, dtype=jnp.float32) / ROT_DIM)
    ang = positions.astype(jnp.float32)[..., None] * inv
    return jnp.cos(ang), jnp.sin(ang)

def apply_partial_rope(t, cos, sin):
    rot, rest = t[..., :ROT_DIM], t[..., ROT_DIM:]
    r1, r2 = rot[..., :ROT_DIM // 2], rot[..., ROT_DIM // 2:]
    c = cos[:, :, None, None, :].astype(t.dtype)
    s = sin[:, :, None, None, :].astype(t.dtype)
    return jnp.concatenate([r1 * c - r2 * s, r1 * s + r2 * c, rest], axis=-1)

def diff_attention(q, k, v, lam, out_scale, gain):
    B, S = q.shape[0], q.shape[1]
    nblk = S // Q_BLOCK
    qb = q.reshape(B, nblk, Q_BLOCK, DA_HEADS, 2, DA_QK).transpose(1, 0, 2, 3, 4, 5)
    kpos = jnp.arange(S)
    scale = DA_QK ** -0.5

    def block(args):
        qi, bi = args
        s = jnp.einsum('bqhmd,bkhmd->bhmqk', qi, k).astype(jnp.float32) * scale
        qpos = bi * Q_BLOCK + jnp.arange(Q_BLOCK)
        mask = kpos[None, :] <= qpos[:, None]
        p = jax.nn.softmax(jnp.where(mask, s, -jnp.inf), axis=-1)
        a = p[:, :, 0] - lam * p[:, :, 1]
        return jnp.einsum('bhqk,bkhe->bqhe', a.astype(v.dtype), v)

    o = lax.map(block, (qb, jnp.arange(nblk)))
    o = o.transpose(1, 0, 2, 3, 4).reshape(B, S, DA_HEADS, DA_V)
    o = rmsnorm(o, gain) * out_scale
    return o.reshape(B, S, DA_WIDTH)

def short_conv(b_gate, c_gate, h_in, w):
    z = c_gate * h_in
    S = z.shape[1]
    zp = jnp.pad(z, ((0, 0), (CONV_W - 1, 0), (0, 0)))
    y = w[0] * zp[:, 0:S]
    for j in range(1, CONV_W):
        y = y + w[j] * zp[:, j:j + S]
    return b_gate * y

def gla(q, k, v, log_a):
    B, S = q.shape[0], q.shape[1]
    nc = S // GLA_CHUNK

    def chunks(t):
        return t.astype(jnp.float32).reshape(B, nc, GLA_CHUNK, GLA_HEADS, t.shape[-1]).transpose(1, 0, 3, 2, 4)

    qc, kc, vc, ac = chunks(q * (GLA_DK ** -0.5)), chunks(k), chunks(v), chunks(log_a)
    causal = jnp.tril(jnp.ones((GLA_CHUNK, GLA_CHUNK), dtype=bool))

    def step(state, inp):
        qi, ki, vi, ai = inp
        b = lax.cumsum(ai, axis=2)
        diff = b[:, :, :, None, :] - b[:, :, None, :, :]
        decay = jnp.exp(jnp.where(causal[:, :, None], diff, -jnp.inf))
        attn = jnp.sum(qi[:, :, :, None, :] * ki[:, :, None, :, :] * decay, axis=-1)
        o = jnp.einsum('bhij,bhje->bhie', attn, vi) + jnp.einsum('bhid,bhde->bhie', qi * jnp.exp(b), state)
        b_last = b[:, :, -1:, :]
        state = jnp.exp(b_last[:, :, 0, :, None]) * state + jnp.einsum(
            'bhjd,bhje->bhde', ki * jnp.exp(b_last - b), vi)
        return state, o

    state0 = jnp.zeros((B, GLA_HEADS, GLA_DK, GLA_DV), jnp.float32)
    _, o = lax.scan(step, state0, (qc, kc, vc, ac))
    o = o.transpose(1, 0, 3, 2, 4).reshape(B, S, GLA_HEADS, GLA_DV)
    return o.astype(v.dtype)

def peer(xn, w_q, keys1, keys2, u, v):
    B, S, D = xn.shape
    T = B * S
    xt = xn.reshape(T, D)
    q = (xt @ w_q).reshape(T, PEER_HEADS, 2, PEER_HALF)
    s1 = jnp.einsum('thd,nd->thn', q[:, :, 0], keys1).astype(jnp.float32)
    s2 = jnp.einsum('thd,nd->thn', q[:, :, 1], keys2).astype(jnp.float32)
    v1, i1 = lax.top_k(s1, PEER_TOPK)
    v2, i2 = lax.top_k(s2, PEER_TOPK)
    cand = (v1[..., :, None] + v2[..., None, :]).reshape(T, PEER_HEADS, PEER_TOPK * PEER_TOPK)
    sc, ci = lax.top_k(cand, PEER_TOPK)
    e1 = jnp.take_along_axis(i1, ci // PEER_TOPK, axis=-1)
    e2 = jnp.take_along_axis(i2, ci % PEER_TOPK, axis=-1)
    hk = PEER_HEADS * PEER_TOPK
    experts = (e1 * PEER_NKEYS + e2).reshape(T, hk)
    gates = jax.nn.softmax(sc, axis=-1).reshape(T, hk).astype(xn.dtype)
    nb = T // PEER_TOKEN_BLOCK

    def block(args):
        xb, eb, gb = args
        ub = jnp.take(u, eb, axis=0)
        hb = jax.nn.gelu(jnp.einsum('tkd,td->tk', ub, xb), approximate=False)
        vb = jnp.take(v, eb, axis=0)
        return jnp.einsum('tk,tkd->td', gb * hb, vb)

    out = lax.map(block, (xt.reshape(nb, PEER_TOKEN_BLOCK, D),
                          experts.reshape(nb, PEER_TOKEN_BLOCK, hk),
                          gates.reshape(nb, PEER_TOKEN_BLOCK, hk)))
    return out.reshape(B, S, D)

def first_inputs(seed: int = 0) -> dict:
    key = jax.random.key(seed)
    ks = jax.random.split(key, 24)
    f32 = jnp.float32
    L, D = DEPTH, D_MODEL
    nrm = lambda k, shape, s: jax.random.normal(k, shape, f32) * s
    return {
        "x": jax.random.normal(ks[0], (BATCH, SEQ, D), f32),
        "positions": jnp.broadcast_to(jnp.arange(SEQ, dtype=jnp.int32), (BATCH, SEQ)),
        "norm_mix": 1.0 + nrm(ks[1], (L, D), 0.02),
        "w_in": nrm(ks[2], (L, D, IN_WIDTH), D ** -0.5),
        "lam_q1": nrm(ks[3], (L, DA_QK), 0.1),
        "lam_k1": nrm(ks[4], (L, DA_QK), 0.1),
        "lam_q2": nrm(ks[5], (L, DA_QK), 0.1),
        "lam_k2": nrm(ks[6], (L, DA_QK), 0.1),
        "diff_norm": 1.0 + nrm(ks[7], (L, DA_V), 0.02),
        "conv_w": nrm(ks[8], (L, CONV_W, SC_WIDTH), CONV_W ** -0.5),
        "gla_w_gate2": nrm(ks[9], (L, GLA_GATE_RANK, GLA_KW), GLA_GATE_RANK ** -0.5),
        "gla_b_gate": nrm(ks[10], (L, GLA_KW), 0.1),
        "gla_norm": 1.0 + nrm(ks[11], (L, GLA_DV), 0.02),
        "w_out": nrm(ks[12], (L, MIX_WIDTH, D), MIX_WIDTH ** -0.5),
        "norm_ffn": 1.0 + nrm(ks[13], (L, D), 0.02),
        "peer_w_q": nrm(ks[14], (L, D, PEER_HEADS * PEER_QDIM), D ** -0.5),
        "peer_keys1": nrm(ks[15], (L, PEER_NKEYS, PEER_HALF), PEER_HALF ** -0.5),
        "peer_keys2": nrm(ks[16], (L, PEER_NKEYS, PEER_HALF), PEER_HALF ** -0.5),
        "peer_u": nrm(ks[17], (L, PEER_EXPERTS, D), D ** -0.5),
        "peer_v": nrm(ks[18], (L, PEER_EXPERTS, D), (PEER_HEADS * PEER_TOPK) ** -0.5),
        "norm_final": 1.0 + nrm(ks[19], (D,), 0.02),
    }

def first_block(x, positions, norm_mix, w_in, lam_q1, lam_k1, lam_q2, lam_k2, diff_norm,
              conv_w, gla_w_gate2, gla_b_gate, gla_norm, w_out, norm_ffn, peer_w_q,
              peer_keys1, peer_keys2, peer_u, peer_v, norm_final):
    B, S, _ = x.shape
    cos, sin = rope_tables(positions)
    split_points = [int(p) for p in np.cumsum(IN_SIZES)[:-1]]
    for i in range(DEPTH):
        h = rmsnorm(x, norm_mix[i])
        proj = h @ w_in[i]
        (da_q, da_k, da_v, sc_b, sc_c, sc_h,
         g_q, g_k, g_v, g_r, g_lr) = jnp.split(proj, split_points, axis=-1)

        lam_init = 0.8 - 0.6 * math.exp(-0.3 * i)
        lam = (jnp.exp(jnp.sum(lam_q1[i].astype(jnp.float32) * lam_k1[i].astype(jnp.float32)))
               - jnp.exp(jnp.sum(lam_q2[i].astype(jnp.float32) * lam_k2[i].astype(jnp.float32)))
               + lam_init)
        q = apply_partial_rope(da_q.reshape(B, S, DA_HEADS, 2, DA_QK), cos, sin)
        k = apply_partial_rope(da_k.reshape(B, S, DA_HEADS, 2, DA_QK), cos, sin)
        o_da = diff_attention(q, k, da_v.reshape(B, S, DA_HEADS, DA_V), lam,
                              1.0 - lam_init, diff_norm[i])

        o_sc = short_conv(sc_b, sc_c, sc_h, conv_w[i])

        log_a = jax.nn.log_sigmoid((g_lr @ gla_w_gate2[i] + gla_b_gate[i]).astype(jnp.float32)) / GLA_GATE_TEMP
        o_g = gla(g_q.reshape(B, S, GLA_HEADS, GLA_DK), g_k.reshape(B, S, GLA_HEADS, GLA_DK),
                  g_v.reshape(B, S, GLA_HEADS, GLA_DV), log_a.reshape(B, S, GLA_HEADS, GLA_DK))
        o_g = rmsnorm(o_g, gla_norm[i]) * jax.nn.silu(g_r.reshape(B, S, GLA_HEADS, GLA_DV))
        o_g = o_g.reshape(B, S, GLA_VW)

        mixed = jnp.concatenate([o_da, o_sc, o_g], axis=-1)
        x = x + mixed @ w_out[i]

        x = x + peer(rmsnorm(x, norm_ffn[i]), peer_w_q[i], peer_keys1[i], peer_keys2[i],
                     peer_u[i], peer_v[i])
    return rmsnorm(x, norm_final)


N_MIXERS = 2
N_ATTN_LAYERS = (DEPTH + 1) // 2
N_RET_LAYERS = DEPTH // 2
NORM_EPS = 1e-6
N_NORMS = 6

D_FF = 2816

DILATED_GROUPS = ((128, 1), (512, 4), (2048, 16))
N_GROUPS = len(DILATED_GROUPS)
H_A = 16
DH_A = 64
D_A = H_A * DH_A
ATTN_IN_COLS = N_GROUPS * 3 * D_A
BLK = 64
NEG_INF = -1e30

NUM_BUCKETS = 32
REL_MAX_DISTANCE = 1024

H_R = 4
DK_R = D_MODEL // H_R
DV_R = 2 * D_MODEL // H_R
D_V = H_R * DV_R
RET_IN_COLS = 2 * H_R * DK_R + 3 * D_V
RET_CHUNK = 128
ROPE_BASE = 10000.0


def rms_norm(x, g):
    xf = x.astype(jnp.float32)
    y = xf * lax.rsqrt(jnp.mean(xf * xf, axis=-1, keepdims=True) + NORM_EPS)
    return (y * g.astype(jnp.float32)).astype(x.dtype)

def swiglu(h, w_gate, w_up, w_down):
    return (jax.nn.silu(h @ w_gate) * (h @ w_up)) @ w_down

def t5_buckets(rel):
    half = NUM_BUCKETS // 2
    max_exact = half // 2
    n = np.abs(rel)
    large = max_exact + (np.log(np.maximum(n, 1) / max_exact)
                         / np.log(REL_MAX_DISTANCE / max_exact) * (half - max_exact)).astype(np.int64)
    large = np.minimum(large, half - 1)
    return ((rel > 0) * half + np.where(n < max_exact, n, large)).astype(np.int32)

def banded_attention(q, k, v, bias, radius):
    N, L, H, dh = q.shape
    nb = -(-L // BLK)
    Lp = nb * BLK
    qb = jnp.pad(q, ((0, 0), (0, Lp - L), (0, 0), (0, 0))).reshape(N, nb, BLK, H, dh)

    def windows(t):
        tp = jnp.pad(t, ((0, 0), (BLK, Lp - L + BLK), (0, 0), (0, 0))).reshape(N, nb + 2, BLK, H, dh)
        return jnp.concatenate([tp[:, :-2], tp[:, 1:-1], tp[:, 2:]], axis=2)

    kw, vw = windows(k), windows(v)
    a = np.arange(BLK)[:, None]
    c = np.arange(3 * BLK)[None, :]
    off = c - BLK - a
    key_pos = np.arange(nb)[:, None, None] * BLK - BLK + c[None]
    valid = (np.abs(off) <= radius)[None] & (key_pos >= 0) & (key_pos < L)
    bias_blk = bias[:, np.clip(off + radius, 0, 2 * radius)].astype(jnp.float32)

    s = jnp.einsum('nbqhd,nbkhd->nbhqk', qb, kw).astype(jnp.float32) * (dh ** -0.5) + bias_blk
    s = jnp.where(valid[None, :, None], s, NEG_INF)
    smax = jnp.max(s, axis=-1, keepdims=True)
    p = jnp.exp(s - smax)
    denom = jnp.sum(p, axis=-1, keepdims=True)
    o = jnp.einsum('nbhqk,nbkhd->nbqhd', (p / denom).astype(v.dtype), vw)
    lse = (smax + jnp.log(denom))[..., 0]
    o = o.reshape(N, Lp, H, dh)[:, :L]
    lse = lse.transpose(0, 1, 3, 2).reshape(N, Lp, H)[:, :L]
    return o, lse

def dilated_group(q, k, v, bias, dilation, radius):
    B, S, H, dh = q.shape
    Ls = S // dilation

    def split(t):
        return t.reshape(B, Ls, dilation, H, dh).transpose(0, 2, 1, 3, 4).reshape(B * dilation, Ls, H, dh)

    o, lse = banded_attention(split(q), split(k), split(v), bias, radius)
    o = o.reshape(B, dilation, Ls, H, dh).transpose(0, 2, 1, 3, 4).reshape(B, S, H, dh)
    lse = lse.reshape(B, dilation, Ls, H).transpose(0, 2, 1, 3).reshape(B, S, H)
    return o, lse

def dilated_attention(h, w_in, w_out, rel_bias):
    B, S, _ = h.shape
    proj = (h @ w_in).reshape(B, S, N_GROUPS, 3, H_A, DH_A)
    outs, lses = [], []
    for g, (window, dilation) in enumerate(DILATED_GROUPS):
        radius = window // (2 * dilation)
        buckets = t5_buckets(np.arange(-radius, radius + 1) * dilation)
        bias_g = rel_bias[g * H_A:(g + 1) * H_A][:, buckets]
        o, lse = dilated_group(proj[:, :, g, 0], proj[:, :, g, 1], proj[:, :, g, 2],
                               bias_g, dilation, radius)
        outs.append(o)
        lses.append(lse)
    wts = jax.nn.softmax(jnp.stack(lses, axis=0), axis=0)
    o = jnp.einsum('gbsh,gbshd->bshd', wts.astype(h.dtype), jnp.stack(outs, axis=0))
    return o.reshape(B, S, D_A) @ w_out

def rotary(t, pos):
    half = t.shape[-1] // 2
    inv_freq = 1.0 / (ROPE_BASE ** jnp.linspace(0.0, 1.0, half, dtype=jnp.float32))
    ang = pos[:, None] * inv_freq[None, :]
    cos = jnp.cos(ang)[None, :, None, :]
    sin = jnp.sin(ang)[None, :, None, :]
    t1, t2 = t[..., :half], t[..., half:]
    return jnp.concatenate([t1 * cos - t2 * sin, t1 * sin + t2 * cos], axis=-1)

def chunk_retention(q, k, v, log_gamma):
    B, S, H, dk = q.shape
    dv = v.shape[-1]
    C = RET_CHUNK
    n = S // C

    def to_chunks(t):
        return t.reshape(B, n, C, H, t.shape[-1]).transpose(1, 0, 3, 2, 4)

    qc, kc, vc = to_chunks(q), to_chunks(k), to_chunks(v)
    i = jnp.arange(C, dtype=jnp.float32)
    rel = i[:, None] - i[None, :]
    dmat = jnp.where(rel >= 0, jnp.exp(log_gamma[:, None, None] * jnp.maximum(rel, 0.0)), 0.0)
    inner = jnp.einsum('nbhid,nbhjd->nbhij', qc, kc) * dmat
    inner = jnp.einsum('nbhij,nbhje->nbhie', inner, vc)
    q_decay = jnp.exp(log_gamma[:, None] * (i + 1.0))[None, :, :, None]
    k_decay = jnp.exp(log_gamma[:, None] * (C - 1.0 - i))[None, :, :, None]
    chunk_decay = jnp.exp(log_gamma * C)[None, :, None, None]

    def step(state, xs):
        qi, ki, vi = xs
        cross = jnp.einsum('bhid,bhde->bhie', qi, state) * q_decay
        state = state * chunk_decay + jnp.einsum('bhjd,bhje->bhde', ki * k_decay, vi)
        return state, cross

    _, cross = lax.scan(step, jnp.zeros((B, H, dk, dv), jnp.float32), (qc, kc, vc))
    y = inner + cross
    return y.transpose(1, 0, 3, 2, 4).reshape(B, S, H, dv)

def head_group_norm(y):
    mu = jnp.mean(y, axis=-1, keepdims=True)
    var = jnp.mean(jnp.square(y - mu), axis=-1, keepdims=True)
    return (y - mu) * lax.rsqrt(var + NORM_EPS)

def retention(h, w_in, w_out, decay_logit):
    B, S, _ = h.shape
    proj = (h @ w_in).astype(jnp.float32)
    dq = H_R * DK_R
    q = proj[..., :dq].reshape(B, S, H_R, DK_R)
    k = proj[..., dq:2 * dq].reshape(B, S, H_R, DK_R)
    v = proj[..., 2 * dq:2 * dq + D_V].reshape(B, S, H_R, DV_R)
    g_f = proj[..., 2 * dq + D_V:2 * dq + 2 * D_V].reshape(B, S, H_R, DV_R)
    g_b = proj[..., 2 * dq + 2 * D_V:].reshape(B, S, H_R, DV_R)
    pos = jnp.arange(S, dtype=jnp.float32)
    q = rotary(q, pos)
    k = rotary(k, pos) * (DK_R ** -0.5)
    log_gamma = jnp.log1p(-jnp.exp(decay_logit.astype(jnp.float32)))
    y_f = chunk_retention(q, k, v, log_gamma[0])
    y_b = jnp.flip(chunk_retention(jnp.flip(q, 1), jnp.flip(k, 1), jnp.flip(v, 1), log_gamma[1]), 1)
    y = jax.nn.silu(g_f) * head_group_norm(y_f) + jax.nn.silu(g_b) * head_group_norm(y_b)
    return y.reshape(B, S, D_V).astype(h.dtype) @ w_out

def second_inputs(seed: int = 0) -> dict:
    key = jax.random.key(seed)
    ks = jax.random.split(key, 12)
    f32 = jnp.float32
    x = jax.random.normal(ks[0], (BATCH, SEQ, D_MODEL), f32)
    norm_gains = 1.0 + 0.05 * jax.random.normal(ks[1], (DEPTH, N_NORMS, D_MODEL), f32)
    ffn_w_gate = jax.random.normal(ks[2], (DEPTH, 2, D_MODEL, D_FF), f32) * D_MODEL ** -0.5
    ffn_w_up = jax.random.normal(ks[3], (DEPTH, 2, D_MODEL, D_FF), f32) * D_MODEL ** -0.5
    ffn_w_down = jax.random.normal(ks[4], (DEPTH, 2, D_FF, D_MODEL), f32) * D_FF ** -0.5
    attn_w_in = jax.random.normal(ks[5], (N_ATTN_LAYERS, D_MODEL, ATTN_IN_COLS), f32) * D_MODEL ** -0.5
    attn_w_out = jax.random.normal(ks[6], (N_ATTN_LAYERS, D_A, D_MODEL), f32) * D_A ** -0.5
    rel_bias = 0.5 * jax.random.normal(ks[7], (N_GROUPS * H_A, NUM_BUCKETS), f32)
    ret_w_in = jax.random.normal(ks[8], (N_RET_LAYERS, D_MODEL, RET_IN_COLS), f32) * D_MODEL ** -0.5
    ret_w_out = jax.random.normal(ks[9], (N_RET_LAYERS, D_V, D_MODEL), f32) * D_V ** -0.5
    base = -(5.0 + jnp.arange(H_R, dtype=f32)) * math.log(2.0)
    ret_decay_logit = base[None, None, :] + 0.1 * jax.random.normal(ks[10], (N_RET_LAYERS, 2, H_R), f32)
    return {"x": x, "norm_gains": norm_gains, "ffn_w_gate": ffn_w_gate, "ffn_w_up": ffn_w_up,
            "ffn_w_down": ffn_w_down, "attn_w_in": attn_w_in, "attn_w_out": attn_w_out,
            "rel_bias": rel_bias, "ret_w_in": ret_w_in, "ret_w_out": ret_w_out,
            "ret_decay_logit": ret_decay_logit}

def second_block(x, norm_gains, ffn_w_gate, ffn_w_up, ffn_w_down, attn_w_in, attn_w_out,
              rel_bias, ret_w_in, ret_w_out, ret_decay_logit):
    for i in range(DEPTH):
        g = norm_gains[i]
        h = swiglu(rms_norm(x, g[0]), ffn_w_gate[i, 0], ffn_w_up[i, 0], ffn_w_down[i, 0])
        x = x + 0.5 * rms_norm(h, g[1])
        hm = rms_norm(x, g[2])
        if i % N_MIXERS == 0:
            j = i // N_MIXERS
            m = dilated_attention(hm, attn_w_in[j], attn_w_out[j], rel_bias)
        else:
            j = i // N_MIXERS
            m = retention(hm, ret_w_in[j], ret_w_out[j], ret_decay_logit[j])
        x = x + rms_norm(m, g[3])
        h = swiglu(rms_norm(x, g[4]), ffn_w_gate[i, 1], ffn_w_up[i, 1], ffn_w_down[i, 1])
        x = x + 0.5 * rms_norm(h, g[5])
    return x


def setup_inputs(seed=0):
    out = dict(first_inputs(seed))
    for name, value in second_inputs(seed + 1).items():
        if name != "x":
            out[name + "_2"] = value
    return out


def reference(
    x, positions, norm_mix, w_in, lam_q1, lam_k1, lam_q2, lam_k2, diff_norm, conv_w,
    gla_w_gate2, gla_b_gate, gla_norm, w_out, norm_ffn, peer_w_q, peer_keys1, peer_keys2,
    peer_u, peer_v, norm_final, norm_gains_2, ffn_w_gate_2, ffn_w_up_2, ffn_w_down_2,
    attn_w_in_2, attn_w_out_2, rel_bias_2, ret_w_in_2, ret_w_out_2, ret_decay_logit_2,
):
    x = first_block(
        x, positions, norm_mix, w_in, lam_q1, lam_k1, lam_q2, lam_k2, diff_norm, conv_w,
        gla_w_gate2, gla_b_gate, gla_norm, w_out, norm_ffn, peer_w_q, peer_keys1, peer_keys2,
        peer_u, peer_v, norm_final,
    )
    return second_block(
        x, norm_gains_2, ffn_w_gate_2, ffn_w_up_2, ffn_w_down_2, attn_w_in_2, attn_w_out_2,
        rel_bias_2, ret_w_in_2, ret_w_out_2, ret_decay_logit_2,
    )


_drawn_inputs = setup_inputs


def setup_inputs(seed=0):
    import zlib

    import numpy as np

    out = dict(_drawn_inputs(seed))
    spreads = {}
    factors = {'gla_norm': 3.687, 'norm_ffn': 3.923}
    for name, (base, spread) in spreads.items():
        noise = np.random.default_rng([zlib.crc32(name.encode()), seed]).standard_normal(out[name].shape)
        drawn = base * np.exp(spread * noise) if base else spread * noise
        out[name] = __import__('jax').numpy.asarray(drawn.astype(out[name].dtype))
    for name, factor in factors.items():
        out[name] = (out[name] * factor).astype(out[name].dtype)
    return out
```

```python
import concourse.bass as bass
from concourse import mybir
from concourse.alu_op_type import AluOpType as ALU
from contextlib import ExitStack, contextmanager
import math
import numpy as np

f32 = mybir.dt.float32
u32 = mybir.dt.uint32
i32 = mybir.dt.int32
ACT = mybir.ActivationFunctionType
AX = mybir.AxisListType.X

P = 128
SEQ = 256
NT = SEQ // P
D = 1024
KD = D // P
DEPTH = 2
EPS = 1e-6

QH = 4
QK = 64
COL_Q, COL_K, COL_V, COL_B, COL_C, COL_H, COL_GQ, COL_GK, COL_GV, COL_GR, COL_LR = (
    0, 512, 1024, 1536, 1792, 2048, 2304, 2432, 2560, 2816, 3072)
IN_W = 3088
RANK = IN_W - COL_LR
ROT = 8
CHUNK = 64
NCH = SEQ // CHUNK
GH, GDK, GDV = 4, 32, 64
PH = 8
NKEY = 128
TOPK = 16
RING = 8

FF = 2816
FP = 256
NPIECE = FF // FP
NG = 3
AH = 16
ADH = 64
DIL = (1, 4, 16)
RADIUS = 64
NEG = -1e30
NBUCKET = 32
RH = 4
RV = 2048

CH = 512
SLOT = KD * CH

C_ID, C_MASK, C_SEL, C_BD, C_IOTA, C_INV = 0, 128, 384, 388, 644, 660
C_N = 668
R_COS, R_SIN, R_RELF, R_MF, R_RELB, R_MB = 0, 256, 512, 1024, 1536, 2048
R_N = 2560
TOEP = 2 * SEQ - 1
TOEPW = 512
HANK = 3 * P


def constants():
    c = np.zeros((P, C_N), np.float32)
    c[:, C_ID:C_ID + P] = np.eye(P)
    q, k = np.arange(P)[:, None], np.arange(P)[None]
    c[:, C_MASK + P:C_MASK + 2 * P] = np.where(k <= q, 0.0, NEG)
    c[:, C_SEL:C_SEL + GH] = (q // GDK == np.arange(GH)[None]) * np.float32(GDK ** -0.5)
    c[:, C_BD:C_BD + SEQ] = (q // GDK == np.arange(GH * GDV)[None] // GDV)
    c[:, C_IOTA:C_IOTA + TOPK] = np.arange(TOPK)
    c[:, C_INV:C_INV + ROT] = np.float32(500000.0) ** (-np.arange(0, 2 * ROT, 2, dtype=np.float32) / np.float32(2 * ROT))
    r = np.zeros((P, R_N), np.float32)
    inv = (1.0 / (10000.0 ** np.linspace(0.0, 1.0, P, dtype=np.float32))).astype(np.float32)
    ang = inv[:, None] * np.arange(SEQ, dtype=np.float32)[None]
    r[:, R_COS:R_COS + SEQ] = np.cos(ang)
    r[:, R_SIN:R_SIN + SEQ] = np.sin(ang)
    for jt in range(NT):
        rel = np.arange(SEQ)[None] - (jt * P + np.arange(P)[:, None])
        s = slice(jt * SEQ, (jt + 1) * SEQ)
        r[:, R_RELF:R_MF][:, s] = np.maximum(rel, 0)
        r[:, R_MF:R_RELB][:, s] = rel >= 0
        r[:, R_RELB:R_MB][:, s] = np.maximum(-rel, 0)
        r[:, R_MB:R_N][:, s] = rel <= 0
    oh = np.zeros((NBUCKET + 1, NG, TOEPW), np.float32)
    for g, dil in enumerate(DIL):
        rel = SEQ - 1 - np.arange(TOEP)
        half, exact = NBUCKET // 2, NBUCKET // 4
        n = np.abs(rel)
        large = exact + (np.log(np.maximum(n, 1) / exact) / np.log(1024 / exact) * (half - exact)).astype(np.int64)
        large = np.minimum(large, half - 1)
        b = (rel > 0) * half + np.where(n < exact, n, large)
        b = np.where((rel % dil == 0) & (n <= RADIUS * dil), b, NBUCKET)
        oh[b, g, np.arange(TOEP)] = 1.0
    return {"tables": c, "ret_tables": r, "bucket_onehot": oh.reshape(NBUCKET + 1, NG * TOEPW)}


class Tally:

    def __init__(self, n=0):
        self.n, self.turns = n, []

    def at(self):
        v = self.n
        for reg, per in self.turns:
            v = reg * per + v
        return v

    def add(self, k=1):
        self.n += k
        return self.at()

    def one(self):
        self.n += 1
        return 1


@contextmanager
def turns(eng, trips, counted):
    with eng.Fori(0, trips) as i:
        before = {t: t.n for t in counted}
        for t, per in counted.items():
            t.turns.append((i, per))
        yield i
        for t, per in counted.items():
            assert t.n - before[t] == per, (t.n - before[t], per)
            t.turns.pop()
            t.n = before[t] + trips * per



PLAN = [("mixer", 0), ("experts", 0), ("mixer", 1), ("experts", 1), ("final", 0),
        ("swiglu", 0), ("dilated", 0), ("swiglu", 1), ("swiglu", 2), ("retention", 0), ("swiglu", 3)]
ROUTE_STEPS = 28


def program(nc, a, out, scratch, plan):
    ctx = ExitStack()
    with ctx:
        def sb(name, shape, dt=f32):
            return ctx.enter_context(nc.sbuf_tensor(name, shape, dt))

        def sem(name):
            return ctx.enter_context(nc.semaphore(name))

        x = sb("x", [P, NT, D])
        xn = sb("xn", [P, NT, D])
        hT = sb("hT", [P, KD, SEQ])
        w = sb("w", [P, 2, SLOT])
        wd = sb("wd", [P, 2, 2, D])
        grow = sb("grow", [P, 2, D])
        tab = sb("tab", [P, C_N])
        ident = tab[:, C_ID:C_ID + P]
        mask2 = tab[:, C_MASK:C_MASK + SEQ]
        zero = sb("zero", [1, CH])
        ones = sb("ones", [P, CHUNK])
        mhalf = sb("mhalf", [P, 16])
        st = sb("st", [P, 64])
        junk = sb("junk", [P, D])
        ARENA = 29700
        arena = sb("arena", [P, ARENA])
        pos = [0]

        def part(*shape, at=None):
            if at is not None:
                pos[0] = at
            n = math.prod(shape)
            v = arena[:, pos[0]:pos[0] + n]
            pos[0] += n
            assert pos[0] <= ARENA, pos
            if len(shape) == 1:
                return v
            names = "abcde"[:len(shape)]
            return v.rearrange(f"p ({' '.join(names)}) -> p {' '.join(names)}", **dict(zip(names, shape)))

        lamrow = part(DEPTH, 4, QK, at=0)
        gainrow = part(DEPTH, P)
        glarow = part(DEPTH, GDV)
        convw = part(DEPTH, 2, 3)
        gatew = part(DEPTH, P)
        gateb = part(DEPTH)
        keyn = part(DEPTH, 2, P)
        wtail = part(DEPTH, KD, RANK)
        keyT = part(2, P)
        trig = part(6, NT, ROT)
        posf = part(NT)
        posi = part(NT).bitcast(i32)
        kint = part(NT, ROT).bitcast(i32)
        lrT = part(SEQ)
        mixer = pos[0]
        proj = part(NT, COL_LR)
        tT = part(14, SEQ)
        rt = part(4, NT, 16, ROT)
        sS = part(2, 2, SEQ)
        aN = part(2, SEQ)
        aT = part(SEQ)
        oda = part(NT, QH, P)
        og = part(NT, GH, GDV)
        sgr = part(NT, GH, GDV)
        zg, lg, cb, eb, qb, kd = (part(SEQ) for _ in range(6))
        M = part(2, CHUNK, CHUNK)
        qsel = part(2, CHUNK, GH)
        atT = part(NT, GH, CHUNK)
        kdn = part(NT, P)
        stt = part(NCH, SEQ)
        stu = part(SEQ)
        cy = part(SEQ)
        score = part(NT, PH, 2, NKEY, at=mixer)
        urow = part(RING, D)
        pq = arena[:, pos[0]:pos[0] + 16 * SEQ].rearrange("p (b s) -> p b s", b=16)
        vrow = part(RING, D)
        xcur = part(D)
        junk2 = part(D)
        diag = part(4, P)
        rsv = part(2, NKEY)
        rs2 = part(2, NKEY)
        rv = part(2, TOPK)
        rif = part(2, TOPK)
        cand = part(TOPK, TOPK)
        cand2 = part(TOPK * TOPK)
        csc = part(4, TOPK)
        caf = part(2, TOPK)
        oh = part(2, TOPK, TOPK)
        ef = part(2, TOPK)
        eidf = part(TOPK)
        hdot = part(4, TOPK)
        gel = part(4, TOPK)
        gex = part(4, TOPK)
        wgt = part(4, TOPK)
        rsm = part(4, 4)
        ri = part(2, TOPK).bitcast(u32)
        ci = part(TOPK).bitcast(u32)
        cab = part(2, TOPK).bitcast(u32)
        eid = part(4, TOPK).bitcast(u32)

        ptmp = part(2, CH, at=0)
        second = pos[0]
        ffh = part(2, 2, SEQ)
        ffs = part(2, 2, SEQ)
        qT2 = part(3 * KD, SEQ, at=second)
        kT2 = part(3 * KD, SEQ)
        v2 = part(NT, NG * D)
        bias = part(2, NG, HANK)
        ssc = part(2, NG, SEQ)
        pT2 = part(NG * NT, P)
        o2 = part(NT, D)
        rtab = part(R_N, at=second)
        rq = part(KD, SEQ)
        rk = part(KD, SEQ)
        rg = part(NT, 3 * RV)
        dlg = part(8, 2 * RH)
        bns = part(4, 6)
        mv = part(4, 2)
        dec = part(4, SEQ)
        rotating = pos[0]
        rtmp = part(4, RH, SEQ)
        rtk = part(4, RH, SEQ)
        rn = part(4, CH, at=rotating)
        rp = part(2, 4, SEQ, at=rotating + 4 * RH * SEQ)
        hTflat = hT[:, :, :].rearrange("p k s -> p (k s)")
        xnflat = xn[:, :, :].rearrange("p t n -> p (t n)")
        xnT = xnflat.rearrange("p (k s) -> p k s", k=KD)
        ajunk = sb("ajunk", [P, 4])
        cells = sb("cells", [P, 4])

        pb = ctx.enter_context(nc.psum_tensor("pb", [P, 8, CH], f32))
        pflat = pb[:, :, :].rearrange("p b n -> p (b n)")

        filled = [sem("bank_filled_for_act"), sem("bank_filled_for_dve")]
        took = [sem("bank_taken_by_act"), sem("bank_taken_by_dve")]
        w_ready = [sem("weights_ready_0"), sem("weights_ready_1")]
        w_free = [sem("weights_free_0"), sem("weights_free_1")]
        wd_ready = [sem("down_weights_ready_0"), sem("down_weights_ready_1")]
        wd_free = [sem("down_weights_free_0"), sem("down_weights_free_1")]
        tab_ready, x_ready, par_ready = sem("tables_ready"), sem("x_ready"), sem("parameters_ready")
        grow_ready = [sem("gains_ready_0"), sem("gains_ready_1")]
        onehot_ready, toep_stored, rtab_ready = sem("onehot_ready"), sem("bias_rows_stored"), sem("ret_tables_ready")
        dve_pe, act_pe = sem("dve_wrote_for_pe"), sem("act_wrote_for_pe")
        dve_act, act_dve = sem("dve_wrote_for_act"), sem("act_wrote_for_dve")
        dve_pool, pool_dve = sem("dve_wrote_for_pool"), sem("pool_wrote_for_dve")
        pool_act, act_pool = sem("pool_wrote_for_act"), sem("act_wrote_for_pool")
        pe_dve, pe_act = sem("pe_summed_for_dve"), sem("pe_summed_for_act")
        pool_set = sem("pool_set_constants")
        own_dve, own_act, own_pool = sem("own_dve"), sem("own_act"), sem("own_pool")
        u_ready = [sem(f"u_row_ready_{r}") for r in range(RING)]
        v_ready = [sem(f"v_row_ready_{r}") for r in range(RING)]
        u_used, v_used, diag_ready = sem("u_rows_used"), sem("v_rows_used"), sem("diagonals_ready")
        bias_ready = [sem("bias_ready_0"), sem("bias_ready_1")]
        bias_used = sem("bias_used")
        scores_read = sem("scores_read_by_dve")
        x_done = sem("x_done")
        stored = sem("output_stored")
        mark = {}

        block = ctx.enter_context(nc.Block())

        passed = sem("waits_passed")

        gains = []
        for stage, n in plan:
            g2 = a["norm_gains_2"]
            gains += {
                "mixer": lambda: [a["norm_mix"][n]], "experts": lambda: [a["norm_ffn"][n]],
                "final": lambda: [a["norm_final"]],
                "swiglu": lambda: [g2[n // 2, 4 * (n % 2)], g2[n // 2, 4 * (n % 2) + 1]],
                "dilated": lambda: [g2[0, 2], g2[0, 3]], "retention": lambda: [g2[1, 2], g2[1, 3]],
            }[stage]()
        n_norms = len(gains)
        params = [(a["positions"].rearrange("o (t p) -> p (o t)", p=P), posi)]
        for l in range(DEPTH):
            for n, name in enumerate(("lam_q1", "lam_k1", "lam_q2", "lam_k2")):
                params.append((a[name][l].partition_broadcast(P), lamrow[:, l, n, :]))
            params += [
                (a["diff_norm"][l].partition_broadcast(P), gainrow[:, l, :]),
                (a["gla_norm"][l].partition_broadcast(P), glarow[:, l, :]),
                (a["gla_w_gate2"][l], gatew[0:RANK, l, :]),
                (a["gla_b_gate"][l].rearrange("(p o) -> p o", o=1), gateb[:, l:l + 1]),
                (a["peer_keys1"][l], keyn[:, l, 0, :]),
                (a["peer_keys2"][l], keyn[:, l, 1, :]),
                (a["w_in"][l].rearrange("(k p) n -> p k n", p=P)[:, :, COL_LR:IN_W], wtail[:, l, :, :]),
            ]
            for b in range(2):
                params.append((a["conv_w"][l][:, b * P:(b + 1) * P].rearrange("j p -> p j"), convw[:, l, b, :]))
        PAR = 16 * len(params)

        @block.tensor
        def _(pe):
            given = [Tally(), Tally()]
            from_dve, from_act = Tally(), Tally()
            filledw = [Tally(), Tally()]
            slot, spent = [0], [1]

            def ring(e):
                return pb[:, 4 + e + 2 * ((given[e].n - 1) % 2), :]

            def next_slot():
                slot[0] ^= 1
                return slot[0] ^ 1

            def release(ins):
                if spent[0] is not None:
                    ins.then_inc(w_free[spent[0]], 1)
                    spent[0] = None

            def chunk_natural(src, readers, banks=None, first=True, last=True):
                s = next_slot()
                pe.wait_ge(w_ready[s], filledw[s].add(16))
                wk = w[:, s, :].rearrange("p (k n) -> p k n", k=KD)
                for t in range(NT):
                    if banks is None:
                        pe.wait_ge(took[readers[t]], given[readers[t]].add(1))
                        o = ring(readers[t])
                    else:
                        o = pb[:, banks[t], :]
                    for k in range(KD):
                        ins = nc.tensor.matmul(o, src[:, k, t * P:(t + 1) * P], wk[:, k, :],
                                               start=first and k == 0, stop=last and k == KD - 1)
                        if t == 0 and k == 0:
                            release(ins)
                    if banks is None:
                        ins.then_inc(filled[readers[t]], 1)
                spent[0] = s
                return ins

            def chunk_transposed():
                s = next_slot()
                pe.wait_ge(w_ready[s], filledw[s].add(16))
                wk = w[:, s, :].rearrange("p (k n) -> p k n", k=KD)
                for m in range(CH // P):
                    pe.wait_ge(took[m % 2], given[m % 2].add(1))
                    o = ring(m % 2)
                    for k in range(KD):
                        ins = nc.tensor.matmul(o[:, 0:SEQ], wk[:, k, m * P:(m + 1) * P], hT[:, k, :],
                                               start=k == 0, stop=k == KD - 1)
                        if m == 0 and k == 0:
                            release(ins)
                    ins.then_inc(filled[m % 2], 1)
                spent[0] = s

            sums, filledwd = Tally(), [Tally(), Tally()]

            def transpose_into(e, ins_):
                pe.wait_ge(took[e], given[e].add(1))
                o = ring(e)
                for j, tile in enumerate(ins_):
                    ins = nc.tensor.transpose(o[:, j * P:(j + 1) * P], tile, ident)
                ins.then_inc(filled[e], 1)

            def natural_to_hT(src):
                pe.wait_ge(dve_pe, from_dve.add(NT))
                for c in range(KD // 2):
                    transpose_into(c % 2, [src[:, t, (2 * c + b) * P:(2 * c + b + 1) * P]
                                           for b in range(2) for t in range(NT)])
                pe.wait_ge(took[0], given[0].at() + 2)
                pe.wait_ge(took[1], given[1].at() + 2)

            def mixer(L):
                natural_to_hT(xn)
                pe.wait_ge(took[1], given[1].add(1))
                o = ring(1)
                for k in range(KD):
                    ins = nc.tensor.matmul(o[0:RANK, 0:SEQ], wtail[:, L, k, :], hT[:, k, :],
                                           start=k == 0, stop=k == KD - 1)
                ins.then_inc(filled[1], 1)
                with turns(pe, 3, {given[0]: 2, given[1]: 2, filledw[0]: 16, filledw[1]: 16}):
                    for _ in range(2):
                        chunk_natural(hT, (0, 1))
                pe.wait_ge(took[0], given[0].at() + 2)
                pe.wait_ge(took[1], given[1].at() + 2)
                mark["proj", L] = given[0].n
                pe.wait_ge(took[1], given[1].add(1))
                o = ring(1)
                nc.tensor.matmul(o[:, 0:SEQ], gatew[0:RANK, L, :], lrT[0:RANK, :],
                                 start=True, stop=True).then_inc(filled[1], 1)
                cols = [COL_GQ, COL_GK] + [COL_Q + P * b for b in range(4)] + [COL_K + P * b for b in range(4)]
                cols += [COL_B, COL_B + P, COL_C, COL_C + P]
                for n in range(7):
                    if n == 1:
                        pe.wait_ge(dve_pe, from_dve.add(1))
                    transpose_into(n % 2, [proj[:, t, cols[2 * n + b]:cols[2 * n + b] + P]
                                           for b in range(2) for t in range(NT)])
                mark["tT", L] = given[0].n
                pe.wait_ge(took[0], given[0].at() + 2)
                pe.wait_ge(took[1], given[1].at() + 2)
                pe.wait_ge(dve_pe, from_dve.add(1))
                transpose_into(0, [kd[:, t * P:(t + 1) * P] for t in range(NT)])

                units = [(t, h) for t in range(NT) for h in range(QH)]

                def scores(t, h):
                    for m in range(2):
                        r = slice(m * QK, (m + 1) * QK)
                        pe.wait_ge(took[1], given[1].add(1))
                        nc.tensor.matmul(ring(1)[:, 0:(t + 1) * P],
                                         tT[r, 2 + h, t * P:(t + 1) * P], tT[r, 6 + h, 0:(t + 1) * P],
                                         start=True, stop=True).then_inc(filled[1], 1)

                scores(*units[0])
                for u, (t, h) in enumerate(units):
                    if u + 1 < len(units):
                        scores(*units[u + 1])
                    pe.wait_ge(dve_pe, from_dve.add(1))
                    transpose_into(0, [aN[:, u % 2, j * P:(j + 1) * P] for j in range(t + 1)])
                    pe.wait_ge(took[0], given[0].at() + 2)
                    pe.wait_ge(took[1], given[1].add(1))
                    o = ring(1)
                    for j in range(t + 1):
                        ins = nc.tensor.matmul(o[:, 0:P], aT[:, j * P:(j + 1) * P],
                                               proj[:, j, COL_V + h * P:COL_V + (h + 1) * P],
                                               start=j == 0, stop=j == t)
                    ins.then_inc(filled[1], 1)

                with turns(pe, NT, {from_dve: 2, from_act: 1}):
                    for c in range(2):
                        pe.wait_ge(dve_pe, from_dve.add(1))
                        if c == 0:
                            pe.wait_ge(act_pe, from_act.add(1))
                        for i in range(CHUNK):
                            ins = nc.tensor.matmul(pb[c * CHUNK:(c + 1) * CHUNK, 0, i * GH:(i + 1) * GH],
                                                   M[:, c, i, :], qsel[:, c, i, :], start=True, stop=True)
                    ins.then_inc(pe_act, 1)
                pe.wait_ge(act_pe, from_act.add(1))
                for c in range(NCH - 1):
                    t, r = c // 2, slice((c % 2) * CHUNK, (c % 2 + 1) * CHUNK)
                    pe.wait_ge(took[1], given[1].add(1))
                    o = ring(1)
                    nc.tensor.matmul(o[:, 0:SEQ], kdn[r, t, :], proj[r, t, COL_GV:COL_GV + SEQ],
                                     start=True, stop=True).then_inc(filled[1], 1)
                for t in range(NT):
                    pe.wait_ge(took[1], given[1].add(1))
                    o = ring(1)
                    for c in (2 * t, 2 * t + 1):
                        r = slice((c % 2) * CHUNK, (c % 2 + 1) * CHUNK)
                        for h in range(GH):
                            ins = nc.tensor.matmul(o[r, h * GDV:(h + 1) * GDV], atT[r, t, h, :],
                                                   proj[r, t, COL_GV + h * GDV:COL_GV + (h + 1) * GDV],
                                                   start=True, stop=True)
                    ins.then_inc(filled[1], 1)
                pe.wait_ge(dve_pe, from_dve.add(1))
                for t in range(NT):
                    pe.wait_ge(took[1], given[1].add(1))
                    o = ring(1)
                    for c in (2 * t, 2 * t + 1):
                        r = slice((c % 2) * CHUNK, (c % 2 + 1) * CHUNK)
                        ins = nc.tensor.matmul(o[r, 0:SEQ], qb[:, c * CHUNK:(c + 1) * CHUNK], stt[:, c, :],
                                               start=True, stop=True)
                    ins.then_inc(filled[1], 1)

                pe.wait_ge(dve_pe, from_dve.add(1))
                outs = [oda[:, :, h, :] for h in range(QH)] + [
                    og[:, :, 2 * b:2 * b + 2, :].rearrange("p t h e -> p t (h e)") for b in range(2)]
                for n in range(3):
                    transpose_into(n % 2, [outs[2 * n + b][:, t, :] for b in range(2) for t in range(NT)])
                pe.wait_ge(took[0], given[0].at() + 2)
                pe.wait_ge(took[1], given[1].at() + 2)
                for _ in range(2):
                    chunk_natural(hT, (1, 1))

            def experts(L):
                natural_to_hT(xn)
                transpose_into(0, [keyn[:, L, b, :] for b in range(2)])
                with turns(pe, 2, {given[0]: 4, given[1]: 4, filledw[0]: 16, filledw[1]: 16}):
                    for _ in range(2):
                        chunk_transposed()
                pe.wait_ge(took[0], given[0].at() + 2)
                pe.wait_ge(took[1], given[1].at() + 2)
                for t in range(NT):
                    for g in range(4):
                        pe.wait_ge(took[g % 2], given[g % 2].add(1))
                        o = ring(g % 2)
                        for j in range(4):
                            b = 4 * g + j
                            ins = nc.tensor.matmul(o[:, j * P:(j + 1) * P], pq[:, b, t * P:(t + 1) * P],
                                                   keyT[:, b % 2, :], start=True, stop=True)
                        ins.then_inc(filled[g % 2], 1)
                mark["score", L] = given[0].n
                for b in range(4):
                    nc.tensor.matmul(pb[:, b, :], zero[0:1, 0:P], zero[0:1, :], start=True, stop=False)
                with turns(pe, NT, {diags: 8 * TOPK, **{vrows[r]: 16 * 16 for r in range(RING)}}) as t:
                    with turns(pe, 2, {diags: 4 * TOPK, **{vrows[r]: 16 * 8 for r in range(RING)}}):
                        for u in range(4):
                            for k in range(TOPK):
                                pe.wait_ge(diag_ready, diags.add(1))
                                pe.wait_ge(v_ready[k % RING], vrows[k % RING].add(16))
                                for half in range(2):
                                    ins = nc.tensor.matmul(pflat[:, bass.ds(t * D + half * CH, CH)],
                                                           diag[:, k % 4, :],
                                                           vrow[:, k % RING, half * CH:(half + 1) * CH],
                                                           start=False, stop=False, skip_group_check=True)
                                ins.then_inc(v_used, 1)
                for b in range(4):
                    ins = nc.tensor.matmul(pb[:, b, :], zero[0:1, 0:P], zero[0:1, :], start=False, stop=True)
                ins.then_inc(pe_dve, sums.one())

            diags, vrows = Tally(), [Tally() for _ in range(RING)]

            def swiglu():
                natural_to_hT(xn)
                def gate_up(j):
                    s = next_slot()
                    pe.wait_ge(w_ready[s], filledw[s].add(32))
                    wk = w[:, s, :].rearrange("p (a k n) -> p a k n", a=2, k=KD)
                    for m in range(2):
                        o = pb[:, 4 + 2 * (j % 2) + m, :]
                        for g in range(2):
                            for k in range(KD):
                                ins = nc.tensor.matmul(o[:, g * SEQ:(g + 1) * SEQ],
                                                       wk[:, g, k, m * P:(m + 1) * P], hT[:, k, :],
                                                       start=k == 0, stop=k == KD - 1)
                                if m == 0 and g == 0 and k == 0:
                                    release(ins)
                        ins.then_inc(pe_act, 1)
                    spent[0] = s

                def down(j, free_w=True, last=False):
                    s = j % 2
                    pe.wait_ge(wd_ready[s], filledwd[s].add(16))
                    pe.wait_ge(dve_pe, from_dve.add(2))
                    for m in range(2):
                        for t in range(NT):
                            for half in range(2):
                                ins = nc.tensor.matmul(pb[:, 2 * t + half, :], ffh[:, s, m, t * P:(t + 1) * P],
                                                       wd[:, s, m, half * CH:(half + 1) * CH],
                                                       start=j == 0 and m == 0, stop=last and m == 1,
                                                       skip_group_check=True)
                                if free_w:
                                    release(ins)
                    if last:
                        ins.then_inc(pe_dve, sums.one())
                        mark.setdefault("sums", []).append(sums.n)
                    else:
                        ins.then_inc(wd_free[s], 1)

                gate_up(0)
                gate_up(1)
                down(0)
                with turns(pe, (NPIECE - 3) // 2, {filledw[0]: 32, filledw[1]: 32, filledwd[0]: 16, filledwd[1]: 16,
                                                   from_dve: 4}):
                    gate_up(2)
                    down(1)
                    gate_up(3)
                    down(2)
                gate_up(NPIECE - 1)
                down(NPIECE - 2, free_w=False)
                down(NPIECE - 1, free_w=False, last=True)

            def dilated():
                natural_to_hT(xn)
                with turns(pe, NG, {given[0]: 10, given[1]: 10, filledw[0]: 48, filledw[1]: 48}):
                    for _ in range(4):
                        chunk_transposed()
                    for _ in range(2):
                        chunk_natural(hT, (0, 1))
                pe.wait_ge(took[0], given[0].at() + 2)
                pe.wait_ge(took[1], given[1].at() + 2)
                units = [(h, t) for h in range(AH) for t in range(NT)]

                def scores(u):
                    h, t = units[u]
                    r = slice((h % 2) * ADH, (h % 2 + 1) * ADH)
                    if u >= 2:
                        pe.wait_ge(scores_read, u - 1)
                    for g in range(NG):
                        o = pflat[:, (u % 2) * D + g * SEQ:(u % 2) * D + (g + 1) * SEQ]
                        ins = nc.tensor.matmul(o, qT2[r, g * KD + h // 2, t * P:(t + 1) * P],
                                               kT2[r, g * KD + h // 2, :], start=True, stop=True)
                    ins.then_inc(pe_dve, sums.one())

                scores(0)
                for u, (h, t) in enumerate(units):
                    if u + 1 < len(units):
                        scores(u + 1)
                    pe.wait_ge(act_pe, from_act.add(1))
                    flat = ssc[:, u % 2, :, :].rearrange("p g k -> p (g k)")
                    transpose_into(0, [flat[:, j * P:(j + 1) * P] for j in range(4)])
                    transpose_into(1, [flat[:, j * P:(j + 1) * P] for j in range(4, 6)])
                    pe.wait_ge(took[0], given[0].at() + 2)
                    pe.wait_ge(took[1], given[1].at() + 2)
                    pe.wait_ge(took[1], given[1].add(1))
                    o = ring(1)
                    for j in range(6):
                        g, kt = j // 2, j % 2
                        ins = nc.tensor.matmul(o[:, 0:ADH], pT2[:, j, :],
                                               v2[:, kt, g * D + h * ADH:g * D + (h + 1) * ADH],
                                               start=j == 0, stop=j == 5)
                    ins.then_inc(filled[1], 1)
                natural_to_hT(o2)
                for c in range(2):
                    ins = chunk_natural(hT, None, banks=(c, 2 + c))
                ins.then_inc(pe_dve, sums.one())
                mark.setdefault("sums", []).append(sums.n)

            def retention():
                natural_to_hT(xn)
                for _ in range(4):
                    chunk_transposed()
                mark["qk"] = given[0].n
                with turns(pe, 6, {given[0]: 2, given[1]: 2, filledw[0]: 16, filledw[1]: 16}):
                    for _ in range(2):
                        chunk_natural(hT, (0, 1))
                pe.wait_ge(took[0], given[0].at() + 2)
                pe.wait_ge(took[1], given[1].at() + 2)
                mark["vg"] = given[0].n
                pe.wait_ge(dve_pe, from_dve.add(1))
                for h in range(RH):
                    pe.wait_ge(took[1], given[1].add(1))
                    o = ring(1)
                    for jt in range(NT):
                        for kt in range(2):
                            ins = nc.tensor.matmul(o[:, jt * SEQ:(jt + 1) * SEQ],
                                                   rk[:, 2 * h + kt, jt * P:(jt + 1) * P], rq[:, 2 * h + kt, :],
                                                   start=kt == 0, stop=kt == 1)
                    ins.then_inc(filled[1], 1)
                    pe.wait_ge(dve_pe, from_dve.add(1))
                    for d, t in ((0, 0), (0, 1), (1, 0), (1, 1)):
                        js = range(t + 1) if d == 0 else range(t, NT)
                        for j in js:
                            ins = nc.tensor.matmul(pb[:, 2 * d + t, :], rp[:, h % 2, 2 * d + j, t * P:(t + 1) * P],
                                                   rg[:, j, h * CH:(h + 1) * CH],
                                                   start=j == js[0], stop=j == js[-1])
                        ins.then_inc(pe_dve, sums.one())
                pe.wait_ge(dve_pe, from_dve.add(2))
                for r, dst in enumerate((hT, xn)):
                    for c in range(KD // 2):
                        base = RV + r * D + 2 * c * P
                        transpose_into(c % 2, [rg[:, t, base + b * P:base + (b + 1) * P]
                                               for b in range(2) for t in range(NT)])
                pe.wait_ge(took[0], given[0].at() + 2)
                pe.wait_ge(took[1], given[1].at() + 2)
                xnT = xn[:, :, :].rearrange("p t n -> p (t n)").rearrange("p (k s) -> p k s", k=KD)
                for r, src in enumerate((hT, xnT)):
                    for c in range(2):
                        ins = chunk_natural(src, None, banks=(c, 2 + c), first=r == 0, last=r == 1)
                ins.then_inc(pe_dve, sums.one())
                mark.setdefault("sums", []).append(sums.n)

            pe.sem_inc(w_free[0], 1)
            pe.sem_inc(wd_free[1], 1)
            pe.sem_inc(v_used, 4 * TOPK + RING)
            pe.wait_ge(tab_ready, 16)
            pe.wait_ge(pool_set, 3)
            pe.wait_ge(dve_pe, from_dve.add(1))
            pe.wait_ge(onehot_ready, 32)
            for g in range(NG):
                pe.wait_ge(took[1], given[1].add(1))
                o = ring(1)
                nc.tensor.matmul(o[0:AH, :], junk[0:NBUCKET + 1, g * AH:(g + 1) * AH],
                                 hTflat[0:NBUCKET + 1, g * TOEPW:(g + 1) * TOEPW],
                                 start=True, stop=True).then_inc(filled[1], 1)
            pe.wait_ge(par_ready, PAR)
            for stage, L in plan:
                {"mixer": mixer, "experts": experts}[stage](L) if stage in ("mixer", "experts") else \
                    {"swiglu": swiglu, "dilated": dilated, "retention": retention, "final": lambda: None}[stage]()

        @block.vector
        def _(dve):
            V = nc.vector
            own = Tally()
            got = Tally()
            from_act, from_pool, from_pe = Tally(), Tally(), Tally()
            norms, cell = [0], [0]

            def bank():
                return pb[:, 5 + 2 * ((got.n - 1) % 2), :]

            def told():
                cell[0] = (cell[0] + 1) % 4
                return V.tensor_copy(cells[:, cell[0]:cell[0] + 1], tab[:, 0:1])

            def gains_row():
                n = norms[0]
                norms[0] += 1
                dve.wait_ge(grow_ready[n % 2], 16 * (n // 2 + 1))
                return grow[:, n % 2, :]

            def norm(dst=None, signal=True):
                for t in range(NT):
                    V.tensor_tensor_reduce(out=xn[:, t, :], in0=x[:, t, :], in1=x[:, t, :], scale=1.0, scalar=0.0,
                                                op0=ALU.mult, op1=ALU.add, accum_out=st[:, t:t + 1]).then_inc(own_dve, own.one())
                dve.wait_ge(own_dve, own.at())
                V.tensor_scalar(st[:, 2:4], st[:, 0:2], 1.0 / D, EPS, ALU.mult, ALU.add).then_inc(dve_pool, 1)
                g = gains_row()
                dve.wait_ge(pool_dve, from_pool.add(1))
                for t in range(NT):
                    ins = V.scalar_tensor_tensor(out=(xn if dst is None else dst)[:, t, :], in0=x[:, t, :],
                                                 scalar=st[:, 4 + t:5 + t], in1=g, op0=ALU.mult, op1=ALU.mult)
                    if signal:
                        ins.then_inc(dve_pe, 1)
                    else:
                        ins.then_inc(own_dve, own.one())
                        dve.wait_ge(own_dve, own.at())

            def hT_banks():
                for c in (1, 3):
                    dve.wait_ge(filled[1], got.add(1))
                    V.tensor_copy(hT[:, 2 * c:2 * c + 2, :], two(bank())).then_inc(took[1], 1)

            def two(b):
                return b.rearrange("p (a s) -> p a s", a=2)

            def post_norm(factor):
                dve.wait_ge(act_dve, from_act.add(1))
                V.tensor_tensor(st[:, 12:14], st[:, 8:12].rearrange("p (t h) -> p t h", t=2)[:, :, 0],
                                     st[:, 8:12].rearrange("p (t h) -> p t h", t=2)[:, :, 1], ALU.add).then_inc(own_dve, own.one())
                dve.wait_ge(own_dve, own.at())
                V.tensor_scalar(st[:, 2:4], st[:, 12:14], 1.0 / D, EPS, ALU.mult, ALU.add).then_inc(dve_pool, 1)
                g = gains_row()
                dve.wait_ge(pool_dve, from_pool.add(1))
                for t in range(NT):
                    for h in range(2):
                        cols = slice(h * CH, (h + 1) * CH)
                        V.scalar_tensor_tensor(out=ptmp[:, h, :], in0=pb[:, 2 * t + h, :],
                                                    scalar=st[:, 4 + t:5 + t], in1=g[:, cols],
                                                    op0=ALU.mult, op1=ALU.mult).then_inc(own_dve, own.one())
                    dve.wait_ge(own_dve, own.at())
                    for h in range(2):
                        cols = slice(h * CH, (h + 1) * CH)
                        V.scalar_tensor_tensor(out=x[:, t, cols], in0=ptmp[:, h, :], scalar=factor,
                                                    in1=x[:, t, cols], op0=ALU.mult, op1=ALU.add).then_inc(own_dve, own.one())
                    dve.wait_ge(own_dve, own.at())

            def mixer(L):
                lam_init = 0.8 - 0.6 * math.exp(-0.3 * L)
                norm()
                hT_banks()
                dve.wait_ge(filled[1], got.add(1))
                V.tensor_copy(lrT[0:RANK, :], bank()[0:RANK, 0:SEQ]).then_inc(took[1], 1)
                with turns(dve, 3, {got: 2}) as i:
                    for s in range(2):
                        dve.wait_ge(filled[1], got.add(1))
                        V.tensor_copy(proj[:, 1, bass.ds(i * 2 * CH + s * CH, CH)], bank()).then_inc(took[1], 1)
                dve.wait_ge(filled[1], got.add(1))
                V.tensor_scalar(zg[:], bank()[:, 0:SEQ], gateb[:, L:L + 1], None, ALU.add).then_inc(took[1], 1)
                dve.wait_ge(took[0], mark["proj", L] + 2)
                dve.wait_ge(took[1], got.at() + 2)
                V.tensor_scalar(lg[:], zg[:], 0.0, None, ALU.min).then_inc(dve_act, 1)
                qk = proj[:, :, 0:2 * CH].rearrange("p t (b e) -> p t b e", b=16)
                for t in range(NT):
                    r1, r2 = qk[:, t, :, 0:ROT], qk[:, t, :, ROT:2 * ROT]
                    c = trig[:, 0, t, :].unsqueeze(1).broadcast_to([P, 16, ROT])
                    s = trig[:, 1, t, :].unsqueeze(1).broadcast_to([P, 16, ROT])
                    V.tensor_tensor(rt[:, 0, t], r1, c, ALU.mult).then_inc(own_dve, own.one())
                    V.tensor_tensor(rt[:, 1, t], r2, s, ALU.mult).then_inc(own_dve, own.one())
                    V.tensor_tensor(rt[:, 2, t], r1, s, ALU.mult).then_inc(own_dve, own.one())
                    V.tensor_tensor(rt[:, 3, t], r2, c, ALU.mult).then_inc(own_dve, own.one())
                    dve.wait_ge(own_dve, own.at())
                    V.tensor_tensor(r1, rt[:, 0, t], rt[:, 1, t], ALU.subtract).then_inc(own_dve, own.one())
                    V.tensor_tensor(r2, rt[:, 2, t], rt[:, 3, t], ALU.add).then_inc(own_dve, own.one())
                V.tensor_tensor(proj[:, :, COL_C:COL_C + SEQ], proj[:, :, COL_C:COL_C + SEQ],
                                     proj[:, :, COL_H:COL_H + SEQ], ALU.mult).then_inc(own_dve, own.one())
                dve.wait_ge(own_dve, own.at())
                told().then_inc(dve_pe, 1)
                for n in (1, 3, 5):
                    dve.wait_ge(filled[1], got.add(1))
                    V.tensor_copy(tT[:, 2 * n:2 * n + 2, :], two(bank())).then_inc(took[1], 1)
                for m in range(2):
                    V.tensor_tensor_reduce(out=junk[:, m * QK:(m + 1) * QK], in0=lamrow[:, L, 2 * m, :],
                                                in1=lamrow[:, L, 2 * m + 1, :], scale=1.0, scalar=0.0,
                                                op0=ALU.mult, op1=ALU.add, accum_out=st[:, 16 + m:17 + m]).then_inc(own_dve, own.one())
                dve.wait_ge(own_dve, own.at())
                told().then_inc(dve_act, 1)
                dve.wait_ge(act_dve, from_act.add(1))
                V.tensor_tensor(lg[:], lg[:], qb[:], ALU.subtract).then_inc(own_dve, own.one())
                dve.wait_ge(own_dve, own.at())
                for c in range(NCH):
                    s = slice(c * CHUNK, (c + 1) * CHUNK)
                    V.tensor_tensor_scan(out=zg[:, s], data0=ones[:], data1=lg[:, s], initial=0.0,
                                              op0=ALU.mult, op1=ALU.add).then_inc(own_dve, own.one())
                dve.wait_ge(own_dve, own.at())
                V.tensor_scalar(cb[:], zg[:], 1.0 / 16.0, None, ALU.mult).then_inc(dve_act, 1)
                dve.wait_ge(act_dve, from_act.add(1))
                V.tensor_tensor(st[:, 22:23], st[:, 21:22], st[:, 20:21], ALU.subtract).then_inc(own_dve, own.one())
                dve.wait_ge(own_dve, own.at())
                V.tensor_scalar(st[:, 23:24], st[:, 22:23], lam_init, None, ALU.subtract).then_inc(own_dve, own.one())
                dve.wait_ge(own_dve, own.at())
                dve.wait_ge(act_dve, from_act.add(1))
                dve.wait_ge(took[0], mark["tT", L] + 2)
                V.scalar_tensor_tensor(out=qb[:], in0=tT[:, 0, :], scalar=GDK ** -0.5, in1=eb[:],
                                            op0=ALU.mult, op1=ALU.mult).then_inc(own_dve, own.one())
                V.tensor_tensor(kd[:], kd[:], tT[:, 1, :], ALU.mult).then_inc(own_dve, own.one())
                dve.wait_ge(own_dve, own.at())
                told().then_inc(dve_pe, 1)

                units = [(t, h) for t in range(NT) for h in range(QH)]

                def scores(u):
                    t, h = units[u]
                    k = (t + 1) * P
                    s = sS[:, u % 2, :, 0:k]
                    for m in range(2):
                        dve.wait_ge(filled[1], got.add(1))
                        V.tensor_tensor(s[:, m, :], bank()[:, 0:k], mask2[:, SEQ - k:SEQ], ALU.add).then_inc(took[1], 1)
                    dve.wait_ge(took[1], got.at() + 2)
                    c = 24 + 4 * (u % 2)
                    V.reduce_max(st[:, c:c + 2], s, AX).then_inc(own_dve, own.one())
                    dve.wait_ge(own_dve, own.at())
                    V.tensor_scalar(st[:, c + 2:c + 4], st[:, c:c + 2], -QK ** -0.5, None,
                                    ALU.mult).then_inc(dve_act, 1)

                def output(u):
                    t, h = units[u]
                    dve.wait_ge(filled[1], got.add(1))
                    V.tensor_copy(oda[:, t, h, :], bank()[:, 0:P]).then_inc(took[1], 1)

                scores(0)
                for u, (t, h) in enumerate(units):
                    if u:
                        output(u - 1)
                    if u + 1 < len(units):
                        scores(u + 1)
                    dve.wait_ge(act_dve, from_act.add(1))
                    k = (t + 1) * P
                    c = 32 + 2 * (u % 2)
                    V.reciprocal(st[:, 36:38], st[:, c:c + 2]).then_inc(own_dve, own.one())
                    dve.wait_ge(own_dve, own.at())
                    V.tensor_scalar(st[:, 38:39], st[:, 37:38], st[:, 23:24], None, ALU.mult).then_inc(own_dve, own.one())
                    dve.wait_ge(own_dve, own.at())
                    V.tensor_scalar(sS[:, u % 2, 0, 0:k], sS[:, u % 2, 0, 0:k], st[:, 36:37], None, ALU.mult).then_inc(own_dve, own.one())
                    dve.wait_ge(own_dve, own.at())
                    V.scalar_tensor_tensor(out=aN[:, u % 2, 0:k], in0=sS[:, u % 2, 1, 0:k], scalar=st[:, 38:39],
                                           in1=sS[:, u % 2, 0, 0:k], op0=ALU.mult,
                                           op1=ALU.add).then_inc(dve_pe, 1)
                output(len(units) - 1)

                sel = tab[:, C_SEL:C_SEL + GH].unsqueeze(1).broadcast_to([P, CHUNK, GH])
                dve.wait_ge(took[1], got.at() + 2)
                with turns(dve, NT, {own: 4, from_act: 1, pe_acts: 1}) as t:
                    for c in range(2):
                        s = bass.ds(t * P + c * CHUNK, CHUNK)
                        bi = cb[:, s].unsqueeze(2).broadcast_to([P, CHUNK, CHUNK])
                        bj = cb[:, s].unsqueeze(1).broadcast_to([P, CHUNK, CHUNK])
                        qi = tT[:, 0, s].unsqueeze(2).broadcast_to([P, CHUNK, GH])
                        V.tensor_tensor(qsel[:, c], qi, sel, ALU.mult).then_inc(own_dve, own.one())
                        V.tensor_tensor(M[:, c], bi, bj, ALU.subtract).then_inc(dve_pool, 1)
                    dve.wait_ge(act_dve, from_act.add(1))
                    for c in range(2):
                        kj = tT[:, 1, bass.ds(t * P + c * CHUNK, CHUNK)].unsqueeze(1).broadcast_to([P, CHUNK, CHUNK])
                        V.tensor_tensor(M[:, c], M[:, c], kj, ALU.mult).then_inc(own_dve, own.one())
                        dve.wait_ge(own_dve, own.at())
                        told().then_inc(dve_pe, 1)
                    dve.wait_ge(pe_act, pe_acts.add(1))
                V.memset(stt[:, 0, :], 0.0).then_inc(own_dve, own.one())
                dve.wait_ge(own_dve, own.at())
                for c in range(NCH - 1):
                    dve.wait_ge(filled[1], got.add(1))
                    V.tensor_tensor(stu[:], bank()[:, 0:SEQ], tab[:, C_BD:C_BD + SEQ], ALU.mult).then_inc(took[1], 1)
                    dve.wait_ge(took[1], got.at() + 2)
                    e = eb[:, (c + 1) * CHUNK - 1:(c + 1) * CHUNK]
                    if c == 0:
                        V.tensor_copy(stt[:, 1, :], stu[:]).then_inc(own_dve, own.one())
                        dve.wait_ge(own_dve, own.at())
                    else:
                        V.scalar_tensor_tensor(out=stt[:, c + 1, :], in0=stt[:, c, :], scalar=e, in1=stu[:],
                                                    op0=ALU.mult, op1=ALU.add).then_inc(own_dve, own.one())
                        dve.wait_ge(own_dve, own.at())
                for t in range(NT):
                    dve.wait_ge(filled[1], got.add(1))
                    V.tensor_copy(og[:, t].rearrange("p h e -> p (h e)"), bank()[:, 0:SEQ]).then_inc(took[1], 1)
                dve.wait_ge(took[1], got.at() + 2)
                told().then_inc(dve_pe, 1)

                for b in range(2):
                    z, y = tT[:, 12 + b, :], cy[:]
                    cw = convw[:, L, b, :]
                    V.tensor_scalar(y, z, cw[:, 2:3], None, ALU.mult).then_inc(own_dve, own.one())
                    dve.wait_ge(own_dve, own.at())
                    for j in (1, 0):
                        d = 2 - j
                        V.scalar_tensor_tensor(out=y[:, d:SEQ], in0=z[:, 0:SEQ - d], scalar=cw[:, j:j + 1],
                                                    in1=y[:, d:SEQ], op0=ALU.mult, op1=ALU.add).then_inc(own_dve, own.one())
                        dve.wait_ge(own_dve, own.at())
                    V.tensor_tensor(hT[:, 4 + b, :], y, tT[:, 10 + b, :], ALU.mult).then_inc(own_dve, own.one())
                    dve.wait_ge(own_dve, own.at())

                for t in range(NT):
                    o = og[:, t].rearrange("p h e -> p (h e)")
                    dve.wait_ge(filled[1], got.add(1))
                    V.tensor_tensor(o, bank()[:, 0:SEQ], o, ALU.add).then_inc(took[1], 1)
                dve.wait_ge(took[1], got.at() + 2)
                sq = sS[:, :, :, :].rearrange("p u m k -> p (u m k)")
                odf = oda[:, :, :, :].rearrange("p t h e -> p (t h e)")
                V.tensor_tensor(sq, odf, odf, ALU.mult).then_inc(own_dve, own.one())
                dve.wait_ge(own_dve, own.at())
                V.reduce_sum(st[:, 40:48], sq.rearrange("p (b e) -> p b e", b=8), AX).then_inc(own_dve, own.one())
                dve.wait_ge(own_dve, own.at())
                V.tensor_scalar(st[:, 40:48], st[:, 40:48], 1.0 / P, EPS, ALU.mult, ALU.add).then_inc(own_dve, own.one())
                ogf = og[:, :, :, :].rearrange("p t h e -> p (t h e)")
                V.tensor_tensor(sq[:, 0:2 * SEQ], ogf, ogf, ALU.mult).then_inc(own_dve, own.one())
                dve.wait_ge(own_dve, own.at())
                V.reduce_sum(st[:, 48:56], sq[:, 0:2 * SEQ].rearrange("p (b e) -> p b e", b=8), AX).then_inc(own_dve, own.one())
                dve.wait_ge(own_dve, own.at())
                V.tensor_scalar(st[:, 48:56], st[:, 48:56], 1.0 / GDV, EPS, ALU.mult, ALU.add).then_inc(dve_pool, 1)
                dve.wait_ge(pool_dve, from_pool.add(1))
                V.tensor_scalar(junk[:, 0:P], gainrow[:, L, :], 1.0 - lam_init, None, ALU.mult).then_inc(own_dve, own.one())
                dve.wait_ge(own_dve, own.at())
                oda8 = oda[:, :, :, :].rearrange("p t h e -> p (t h) e")
                og8 = og[:, :, :, :].rearrange("p t h e -> p (t h) e")
                sg8 = sgr[:, :, :, :].rearrange("p t h e -> p (t h) e")
                V.tensor_tensor(oda8, oda8, st[:, 40:48].unsqueeze(2).broadcast_to([P, 8, P]), ALU.mult).then_inc(own_dve, own.one())
                V.tensor_tensor(og8, og8, st[:, 48:56].unsqueeze(2).broadcast_to([P, 8, GDV]), ALU.mult).then_inc(own_dve, own.one())
                dve.wait_ge(own_dve, own.at())
                V.tensor_tensor(oda8, oda8, junk[:, 0:P].unsqueeze(1).broadcast_to([P, 8, P]), ALU.mult).then_inc(own_dve, own.one())
                V.tensor_tensor(og8, og8, glarow[:, L, :].unsqueeze(1).broadcast_to([P, 8, GDV]), ALU.mult).then_inc(own_dve, own.one())
                dve.wait_ge(own_dve, own.at())
                V.tensor_tensor(og8, og8, sg8, ALU.mult).then_inc(dve_pe, 1)
                dve.wait_ge(filled[1], got.add(1))
                V.tensor_copy(hT[:, 2:4, :], two(bank())).then_inc(took[1], 1)
                for c in range(2):
                    for t in range(NT):
                        s = slice(c * CH, (c + 1) * CH)
                        dve.wait_ge(filled[1], got.add(1))
                        V.tensor_tensor(x[:, t, s], bank(), x[:, t, s], ALU.add).then_inc(took[1], 1)
                dve.wait_ge(took[1], got.at() + 2)

            def experts(L):
                norm()
                hT_banks()
                with turns(dve, 2, {got: 4}) as i:
                    for s in range(2):
                        for m in (1, 3):
                            dve.wait_ge(filled[1], got.add(1))
                            V.tensor_copy(pq[:, bass.ds(i * 8 + s * 4 + m, 1), :], bank()[:, 0:SEQ].unsqueeze(1)).then_inc(took[1], 1)
                for t in range(NT):
                    for g in (1, 3):
                        dve.wait_ge(filled[1], got.add(1))
                        V.tensor_copy(score[:, t, 2 * g:2 * g + 2, :, :],
                                           bank().rearrange("p (h m n) -> p h m n", h=2, m=2)).then_inc(took[1], 1)
                dve.wait_ge(took[0], mark["score", L] + 2)
                dve.wait_ge(took[1], got.at() + 2)
                sflat = score[:, :, :, :, :].rearrange("p t h m n -> p (t h) m n")
                iota_k = tab[:, C_IOTA:C_IOTA + TOPK].unsqueeze(1).broadcast_to([P, TOPK, TOPK])

                def route(s, j):
                    dve.wait_ge(v_used, groups.at() + (j + 1) * TOPK + RING)
                    dve.sem_inc(passed, 1)
                    V.tensor_copy(rsv[:].unsqueeze(1), sflat[:, s]).then_inc(own_dve, own.one())
                    dve.wait_ge(own_dve, own.at())
                    dve.sem_inc(passed, 1)
                    for m in range(2):
                        V.max(rv[:, m, 0:8], rsv[:, m, :]).then_inc(own_dve, own.one())
                        dve.wait_ge(own_dve, own.at())
                        dve.sem_inc(passed, 1)
                        V.max_index(ri[:, m, 0:8], rv[:, m, 0:8], rsv[:, m, :]).then_inc(own_dve, own.one())
                        V.match_replace(rs2[:, m, :], rv[:, m, 0:8], rsv[:, m, :], -3e38).then_inc(own_dve, own.one())
                        dve.wait_ge(own_dve, own.at())
                        dve.sem_inc(passed, 1)
                        V.max(rv[:, m, 8:16], rs2[:, m, :]).then_inc(own_dve, own.one())
                        dve.wait_ge(own_dve, own.at())
                        dve.sem_inc(passed, 1)
                        V.max_index(ri[:, m, 8:16], rv[:, m, 8:16], rs2[:, m, :]).then_inc(own_dve, own.one())
                    dve.wait_ge(own_dve, own.at())
                    dve.sem_inc(passed, 1)
                    V.tensor_tensor(cand[:], rv[:, 0, :].unsqueeze(2).broadcast_to([P, TOPK, TOPK]),
                                         rv[:, 1, :].unsqueeze(1).broadcast_to([P, TOPK, TOPK]), ALU.add).then_inc(own_dve, own.one())
                    V.tensor_copy(rif[:], ri[:]).then_inc(own_dve, own.one())
                    dve.wait_ge(own_dve, own.at())
                    dve.sem_inc(passed, 1)
                    cf = cand[:, :, :].rearrange("p a b -> p (a b)")
                    V.max(csc[:, j, 0:8], cf).then_inc(own_dve, own.one())
                    dve.wait_ge(own_dve, own.at())
                    dve.sem_inc(passed, 1)
                    V.max_index(ci[:, 0:8], csc[:, j, 0:8], cf).then_inc(own_dve, own.one())
                    V.match_replace(cand2[:], csc[:, j, 0:8], cf, -3e38).then_inc(own_dve, own.one())
                    dve.wait_ge(own_dve, own.at())
                    dve.sem_inc(passed, 1)
                    V.max(csc[:, j, 8:16], cand2[:]).then_inc(own_dve, own.one())
                    dve.wait_ge(own_dve, own.at())
                    dve.sem_inc(passed, 1)
                    V.max_index(ci[:, 8:16], csc[:, j, 8:16], cand2[:]).then_inc(own_dve, own.one())
                    dve.wait_ge(own_dve, own.at())
                    dve.sem_inc(passed, 1)
                    V.tensor_single_scalar(cab[:, 0, :], ci[:], 4, ALU.logical_shift_right).then_inc(own_dve, own.one())
                    V.tensor_single_scalar(cab[:, 1, :], ci[:], 15, ALU.bitwise_and).then_inc(own_dve, own.one())
                    dve.wait_ge(own_dve, own.at())
                    dve.sem_inc(passed, 1)
                    V.tensor_copy(caf[:], cab[:]).then_inc(own_dve, own.one())
                    dve.wait_ge(own_dve, own.at())
                    dve.sem_inc(passed, 1)
                    for m in range(2):
                        V.tensor_tensor(oh[:, m], caf[:, m, :].unsqueeze(2).broadcast_to([P, TOPK, TOPK]),
                                             iota_k, ALU.is_equal).then_inc(own_dve, own.one())
                    dve.wait_ge(own_dve, own.at())
                    dve.sem_inc(passed, 1)
                    for m in range(2):
                        V.tensor_tensor(oh[:, m], oh[:, m], rif[:, m, :].unsqueeze(1).broadcast_to([P, TOPK, TOPK]),
                                             ALU.mult).then_inc(own_dve, own.one())
                    dve.wait_ge(own_dve, own.at())
                    dve.sem_inc(passed, 1)
                    V.reduce_sum(ef[:], oh[:], AX).then_inc(own_dve, own.one())
                    dve.wait_ge(own_dve, own.at())
                    dve.sem_inc(passed, 1)
                    V.scalar_tensor_tensor(out=eidf[:], in0=ef[:, 0, :], scalar=float(NKEY), in1=ef[:, 1, :],
                                                op0=ALU.mult, op1=ALU.add).then_inc(own_dve, own.one())
                    dve.wait_ge(own_dve, own.at())
                    dve.sem_inc(passed, 1)
                    V.tensor_scalar(rsm[:, j, 0:1], csc[:, j, 0:1], -1.0, None, ALU.mult).then_inc(own_dve, own.one())
                    V.tensor_scalar(eid[:, j, :], eidf[:], float(L * NKEY * NKEY), None,
                                    ALU.add).then_inc(dve_pool, 1)

                junks = (junk[:], junk2[:])

                def dots(j):
                    for k in range(TOPK):
                        dve.wait_ge(u_ready[k % RING], urows[k % RING].add(16))
                        dve.wait_ge(u_used, used.at() + k - 1 + RING)
                        V.tensor_tensor_reduce(out=junks[k % 2], in0=urow[:, k % RING, :], in1=xcur[:], scale=1.0,
                                               scalar=0.0, op0=ALU.mult, op1=ALU.add,
                                               accum_out=hdot[:, j, k:k + 1]).then_inc(u_used, 1)
                    used.add(TOPK)
                    dve.wait_ge(u_used, used.at() + RING)
                    V.tensor_copy(rsm[:, j, 3:4], rsm[:, j, 0:1]).then_inc(dve_act, 1)
                    dve.wait_ge(act_dve, from_act.add(1))
                    V.reciprocal(rsm[:, j, 2:3], rsm[:, j, 1:2]).then_inc(own_dve, own.one())
                    dve.wait_ge(own_dve, own.at())
                    V.scalar_tensor_tensor(out=wgt[:, j, :], in0=gel[:, j, :], scalar=rsm[:, j, 2:3],
                                           in1=gex[:, j, :], op0=ALU.mult, op1=ALU.mult).then_inc(dve_act, 1)

                per = {own: ROUTE_STEPS * 4 + 4, used: 4 * TOPK, groups: 4 * TOPK, from_act: 4,
                       **{urows[r]: 8 * 16 for r in range(RING)}}
                outer = {k: 2 * v for k, v in per.items()}
                outer[own] += 1
                with turns(dve, NT, outer) as t:
                    V.tensor_copy(xcur[:].unsqueeze(1), xn[:, bass.ds(t, 1), :]).then_inc(own_dve, own.one())
                    dve.wait_ge(own_dve, own.at())
                    dve.sem_inc(passed, 1)
                    with turns(dve, 2, per) as g:
                        for j in (0, 1):
                            route(bass.ds(t * PH + g * 4 + j, 1), j)
                        for j in range(4):
                            dots(j)
                            if j < 2:
                                route(bass.ds(t * PH + g * 4 + j + 2, 1), j + 2)
                        groups.add(4 * TOPK)
                dve.wait_ge(pe_dve, from_pe.add(1))
                for t in range(NT):
                    for h in range(2):
                        s = slice(h * CH, (h + 1) * CH)
                        V.tensor_tensor(x[:, t, s], pb[:, 2 * t + h, :], x[:, t, s], ALU.add).then_inc(own_dve, own.one())
                dve.wait_ge(own_dve, own.at())

            urows, used, groups, pe_acts = [Tally() for _ in range(RING)], Tally(), Tally(), Tally()

            def swiglu():
                norm()
                hT_banks()

                def hidden(j):
                    for m in range(2):
                        dve.wait_ge(act_dve, from_act.add(1))
                        V.tensor_tensor(ffh[:, j % 2, m, :], ffs[:, j % 2, m, :],
                                        pb[:, 4 + 2 * (j % 2) + m, SEQ:2 * SEQ], ALU.mult).then_inc(dve_pe, 1)

                hidden(0)
                with turns(dve, (NPIECE - 1) // 2, {from_act: 4}):
                    hidden(1)
                    hidden(2)
                dve.wait_ge(pe_dve, from_pe.add(1))
                post_norm(0.5)

            def dilated():
                norm()
                hT_banks()
                with turns(dve, NG, {got: 10}) as g:
                    for dst, c0 in ((qT2, 0), (qT2, 4), (kT2, 0), (kT2, 4)):
                        for m in (1, 3):
                            dve.wait_ge(filled[1], got.add(1))
                            V.tensor_copy(dst[:, bass.ds(g * KD + c0 + m, 1), :], bank()[:, 0:SEQ].unsqueeze(1)).then_inc(took[1], 1)
                    for c in range(2):
                        dve.wait_ge(filled[1], got.add(1))
                        V.tensor_copy(v2[:, 1, bass.ds(g * D + c * CH, CH)], bank()).then_inc(took[1], 1)
                units = [(h, t) for h in range(AH) for t in range(NT)]

                def scores(u):
                    h, t = units[u]
                    if t == 0:
                        dve.wait_ge(bias_ready[h % 2], 16 * (h // 2 + 1))
                    dve.wait_ge(pe_dve, from_pe.add(1))
                    s = ssc[:, u % 2]
                    o = pflat[:, (u % 2) * D:(u % 2) * D + NG * SEQ].rearrange("p (g k) -> p g k", g=NG)
                    c0 = P * t
                    V.scalar_tensor_tensor(out=s, in0=o, scalar=ADH ** -0.5, in1=bias[:, h % 2, :, c0:c0 + SEQ][:, :, ::-1],
                                           op0=ALU.mult, op1=ALU.add).then_inc(scores_read, 1)
                    dve.wait_ge(scores_read, u + 1)
                    c = 56 + u % 2
                    V.reduce_max(st[:, c:c + 1], s.rearrange("p g k -> p (g k)"), AX).then_inc(own_dve, own.one())
                    dve.wait_ge(own_dve, own.at())
                    V.tensor_scalar(st[:, c + 2:c + 3], st[:, c:c + 1], -1.0, None, ALU.mult).then_inc(dve_act, 1)

                def output(u):
                    h, t = units[u]
                    dve.wait_ge(act_dve, from_act.add(1))
                    r = st[:, 6 + u % 2:7 + u % 2]
                    V.reciprocal(r, st[:, 60 + u % 2:61 + u % 2]).then_inc(own_dve, own.one())
                    dve.wait_ge(own_dve, own.at())
                    dve.wait_ge(filled[1], got.add(1))
                    V.tensor_scalar(o2[:, t, h * ADH:(h + 1) * ADH], bank()[:, 0:ADH], r, None, ALU.mult).then_inc(took[1], 1)

                scores(0)
                for u in range(len(units)):
                    if u:
                        output(u - 1)
                    if u + 1 < len(units):
                        scores(u + 1)
                    dve.wait_ge(filled[1], got.add(1))
                    V.tensor_copy(pT2[:, 4:6, :], bank()[:, 0:2 * P].rearrange("p (j q) -> p j q", j=2)).then_inc(took[1], 1)
                output(len(units) - 1)
                dve.wait_ge(took[1], got.at() + 2)
                told().then_inc(dve_pe, NT)
                hT_banks()
                dve.wait_ge(pe_dve, from_pe.add(1))
                post_norm(1.0)

            def retention():
                dve.wait_ge(rtab_ready, 32)
                norm()
                hT_banks()
                dve.wait_ge(act_dve, from_act.add(1))
                V.tensor_scalar(dlg[:, 2, :], dlg[:, 1, :], -1.0, 1.0, ALU.mult, ALU.add).then_inc(own_dve, own.one())
                dve.wait_ge(own_dve, own.at())
                told().then_inc(dve_act, 1)
                V.tensor_scalar(dlg[:, 3, :], dlg[:, 2, :], 1.0, None, ALU.subtract).then_inc(own_dve, own.one())
                dve.wait_ge(own_dve, own.at())
                V.tensor_scalar(dlg[:, 4, :], dlg[:, 3, :], 0.0, None, ALU.is_equal).then_inc(own_dve, own.one())
                dve.wait_ge(own_dve, own.at())
                V.tensor_tensor(dlg[:, 3, :], dlg[:, 3, :], dlg[:, 4, :], ALU.add).then_inc(own_dve, own.one())
                dve.wait_ge(own_dve, own.at())
                V.reciprocal(dlg[:, 3, :], dlg[:, 3, :]).then_inc(own_dve, own.one())
                dve.wait_ge(own_dve, own.at())
                dve.wait_ge(act_dve, from_act.add(1))
                V.tensor_tensor(dlg[:, 5, :], dlg[:, 5, :], dlg[:, 4, :], ALU.add).then_inc(own_dve, own.one())
                dve.wait_ge(own_dve, own.at())
                V.tensor_tensor(dlg[:, 5, :], dlg[:, 5, :], dlg[:, 3, :], ALU.mult).then_inc(own_dve, own.one())
                dve.wait_ge(own_dve, own.at())
                V.tensor_tensor(dlg[:, 5, :], dlg[:, 5, :], dlg[:, 1, :], ALU.mult).then_inc(own_dve, own.one())
                dve.wait_ge(own_dve, own.at())
                V.tensor_scalar(dlg[:, 6, :], dlg[:, 5, :], -1.0, None, ALU.mult).then_inc(dve_act, 1)
                for dst, c0 in ((rq, 0), (rq, 4), (rk, 0), (rk, 4)):
                    for m in (1, 3):
                        dve.wait_ge(filled[1], got.add(1))
                        V.tensor_copy(dst[:, c0 + m, :], bank()[:, 0:SEQ]).then_inc(took[1], 1)
                dve.wait_ge(took[0], mark["qk"] + 2)
                dve.wait_ge(took[1], got.at() + 2)
                told().then_inc(dve_pool, 1)
                q4 = rq[:, :, :].rearrange("p (h a) s -> p a h s", a=2)
                cos = rtab[:, R_COS:R_COS + SEQ].unsqueeze(1).broadcast_to([P, RH, SEQ])
                sin = rtab[:, R_SIN:R_SIN + SEQ].unsqueeze(1).broadcast_to([P, RH, SEQ])
                V.tensor_tensor(rtmp[:, 0], q4[:, 0], cos, ALU.mult).then_inc(own_dve, own.one())
                V.tensor_tensor(rtmp[:, 1], q4[:, 1], sin, ALU.mult).then_inc(own_dve, own.one())
                V.tensor_tensor(rtmp[:, 2], q4[:, 0], sin, ALU.mult).then_inc(own_dve, own.one())
                V.tensor_tensor(rtmp[:, 3], q4[:, 1], cos, ALU.mult).then_inc(own_dve, own.one())
                dve.wait_ge(own_dve, own.at())
                V.tensor_tensor(q4[:, 0], rtmp[:, 0], rtmp[:, 1], ALU.subtract).then_inc(own_dve, own.one())
                V.tensor_tensor(q4[:, 1], rtmp[:, 2], rtmp[:, 3], ALU.add).then_inc(own_dve, own.one())
                dve.wait_ge(own_dve, own.at())
                with turns(dve, 6, {got: 2}) as i:
                    for s in range(2):
                        dve.wait_ge(filled[1], got.add(1))
                        V.tensor_copy(rg[:, 1, bass.ds(i * 2 * CH + s * CH, CH)], bank()).then_inc(took[1], 1)
                dve.wait_ge(took[0], mark["vg"] + 2)
                dve.wait_ge(took[1], got.at() + 2)
                told().then_inc(dve_act, 1)
                dve.wait_ge(pool_dve, from_pool.add(1))
                told().then_inc(dve_pe, 1)
                for h in range(RH):
                    dve.wait_ge(pool_dve, from_pool.add(1))
                    dve.wait_ge(filled[1], got.add(1))
                    o = bank()
                    b = rp[:, h % 2, :, :].rearrange("p a s -> p (a s)")
                    dd = dec[:, :, :].rearrange("p a s -> p (a s)")
                    V.scalar_tensor_tensor(out=b[:, 0:CH], in0=o, scalar=1.0 / 16.0, in1=dd[:, 0:CH],
                                                op0=ALU.mult, op1=ALU.mult).then_inc(own_dve, own.one())
                    V.scalar_tensor_tensor(out=b[:, CH:2 * CH], in0=o, scalar=1.0 / 16.0, in1=dd[:, CH:2 * CH],
                                                op0=ALU.mult, op1=ALU.mult).then_inc(took[1], 1)
                    dve.wait_ge(own_dve, own.at())
                    dve.wait_ge(took[1], got.at() + 2)
                    told().then_inc(dve_act, 1)
                    if h:
                        dve.wait_ge(act_dve, from_act.add(4))
                        combine(h - 1)
                    told().then_inc(dve_pe, 1)
                    for n in range(4):
                        dve.wait_ge(pe_dve, from_pe.add(1))
                        V.bn_stats(bns[:, n, :], pb[:, n, :]).then_inc(own_dve, own.one())
                    dve.wait_ge(own_dve, own.at())
                    for n in range(4):
                        V.bn_aggr(mv[:, n, :], bns[:, n, :]).then_inc(own_dve, own.one())
                    dve.wait_ge(own_dve, own.at())
                    V.tensor_scalar(st[:, 2:6], mv[:, :, 1], EPS, None, ALU.add).then_inc(dve_pool, 1)
                    dve.wait_ge(pool_dve, from_pool.add(1))
                    V.scalar_tensor_tensor(out=st[:, 12:16], in0=mv[:, :, 0], scalar=-1.0, in1=st[:, 8:12],
                                           op0=ALU.mult, op1=ALU.mult).then_inc(dve_act, 1)
                dve.wait_ge(act_dve, from_act.add(4))
                combine(RH - 1)
                told().then_inc(dve_pe, NT)
                for dst in (hT, xnT):
                    for c in (1, 3):
                        dve.wait_ge(filled[1], got.add(1))
                        V.tensor_copy(dst[:, 2 * c:2 * c + 2, :], two(bank())).then_inc(took[1], 1)
                dve.wait_ge(pe_dve, from_pe.add(1))
                post_norm(1.0)

            xnT = xn[:, :, :].rearrange("p t n -> p (t n)").rearrange("p (k s) -> p k s", k=KD)

            def combine(h):
                for t in range(NT):
                    f = rg[:, t, RV + h * CH:RV + (h + 1) * CH]
                    g = rg[:, t, 2 * RV + h * CH:2 * RV + (h + 1) * CH]
                    V.tensor_tensor(f, f, rn[:, t, :], ALU.mult).then_inc(own_dve, own.one())
                    V.tensor_tensor(g, g, rn[:, 2 + t, :], ALU.mult).then_inc(own_dve, own.one())
                    dve.wait_ge(own_dve, own.at())
                    V.tensor_tensor(f, f, g, ALU.add).then_inc(own_dve, own.one())
                    dve.wait_ge(own_dve, own.at())

            dve.sem_inc(took[1], 2)
            dve.sem_inc(u_used, RING)
            V.memset(zero[:], 0.0)
            V.memset(ones[:], 1.0)
            V.memset(junk[NBUCKET:NBUCKET + 1, 0:NG * AH], NEG).then_inc(dve_pe, 1)
            dve.wait_ge(tab_ready, 16)
            dve.wait_ge(par_ready, PAR)
            V.tensor_copy(posf[:], posi[:]).then_inc(own_dve, own.one())
            dve.wait_ge(own_dve, own.at())
            inv = tab[:, C_INV:C_INV + ROT]
            for t in range(NT):
                V.tensor_scalar(trig[:, 2, t, :], inv, posf[:, t:t + 1], None, ALU.mult).then_inc(own_dve, own.one())
            dve.wait_ge(own_dve, own.at())
            V.tensor_scalar(trig[:, 3], trig[:, 2], 1.0 / (2.0 * math.pi), None, ALU.mult).then_inc(own_dve, own.one())
            dve.wait_ge(own_dve, own.at())
            V.tensor_copy(kint[:], trig[:, 3]).then_inc(own_dve, own.one())
            dve.wait_ge(own_dve, own.at())
            V.tensor_copy(trig[:, 3], kint[:]).then_inc(own_dve, own.one())
            dve.wait_ge(own_dve, own.at())
            c1, c2 = 6.28125, float(np.float32(np.floor((2 * math.pi - 6.28125) * 2 ** 21) / 2 ** 21))
            for c in (c1, c2, 2 * math.pi - c1 - c2):
                V.scalar_tensor_tensor(out=trig[:, 2], in0=trig[:, 3], scalar=-c, in1=trig[:, 2],
                                            op0=ALU.mult, op1=ALU.add).then_inc(own_dve, own.one())
                dve.wait_ge(own_dve, own.at())
            V.tensor_scalar(trig[:, 2], trig[:, 2], 3.1415925, -3.1415925, ALU.min, ALU.max).then_inc(own_dve, own.one())
            dve.wait_ge(own_dve, own.at())
            told().then_inc(dve_act, 1)
            dve.wait_ge(act_dve, from_act.add(1))
            V.tensor_scalar(trig[:, 5], trig[:, 4], -1.0, math.pi / 2, ALU.mult, ALU.add).then_inc(dve_act, 1)
            dve.wait_ge(act_dve, from_act.add(1))
            for g in range(NG):
                dve.wait_ge(filled[1], got.add(1))
                V.tensor_copy(xnflat[0:AH, g * TOEPW:(g + 1) * TOEPW], bank()[0:AH, :]).then_inc(took[1], 1)
            dve.wait_ge(toep_stored, 16)
            dve.wait_ge(x_ready, 16)
            for stage, L in plan:
                if stage == "mixer":
                    mixer(L)
                elif stage == "experts":
                    experts(L)
                elif stage == "final":
                    norm(x, signal=False)
                else:
                    {"swiglu": swiglu, "dilated": dilated, "retention": retention}[stage]()
            told().then_inc(x_done, 1)

        @block.scalar
        def _(act):
            A = nc.scalar
            own = Tally()
            got = Tally()
            from_dve, from_pool, from_pe, diags = Tally(), Tally(), Tally(), Tally()
            posts = [0]

            def bank():
                return pb[:, 4 + 2 * ((got.n - 1) % 2), :]

            def two(b):
                return b.rearrange("p (a s) -> p a s", a=2)

            def hT_banks(dst):
                for c in (0, 2):
                    act.wait_ge(filled[0], got.add(1))
                    A.activation(dst[:, 2 * c:2 * c + 2, :], two(bank()), ACT.Copy).then_inc(took[0], 1)

            def squares():
                act.wait_ge(pe_dve, mark["sums"][posts[0]])
                posts[0] += 1
                for b in range(4):
                    ins = A.activation(xnflat[:, b * CH:(b + 1) * CH], pb[:, b, :], ACT.Square, accum_out=st[:, 8 + b:9 + b])
                ins.then_inc(act_dve, 1)

            def mixer(L):
                hT_banks(hT)
                with turns(act, 3, {got: 2}) as i:
                    for s in range(2):
                        act.wait_ge(filled[0], got.add(1))
                        A.activation(proj[:, 0, bass.ds(i * 2 * CH + s * CH, CH)], bank(), ACT.Copy).then_inc(took[0], 1)
                act.wait_ge(dve_act, from_dve.add(1))
                act.wait_ge(took[0], got.at() + 2)
                A.activation(sgr[:, :, :, :].rearrange("p t h e -> p t (h e)"), proj[:, :, COL_GR:COL_GR + SEQ], ACT.Silu)
                A.activation(qb[:], zg[:], ACT.Abs).then_inc(own_act, own.one())
                act.wait_ge(own_act, own.at())
                A.activation(qb[:], qb[:], ACT.Exp, scale=-1.0).then_inc(own_act, own.one())
                act.wait_ge(own_act, own.at())
                A.activation(qb[:], qb[:], ACT.Ln, bias=1.0).then_inc(act_dve, 1)
                for n in (0, 2, 4, 6):
                    act.wait_ge(filled[0], got.add(1))
                    A.activation(tT[:, 2 * n:2 * n + 2, :], two(bank()), ACT.Copy).then_inc(took[0], 1)
                act.wait_ge(dve_act, from_dve.add(1))
                A.activation(st[:, 20:22], st[:, 16:18], ACT.Exp).then_inc(act_dve, 1)
                act.wait_ge(dve_act, from_dve.add(1))
                for c in range(NCH):
                    s = slice(c * CHUNK, (c + 1) * CHUNK)
                    A.activation(kd[:, s], cb[:, s], ACT.Exp, bias=cb[:, (c + 1) * CHUNK - 1:(c + 1) * CHUNK], scale=-1.0)
                A.activation(eb[:], cb[:], ACT.Exp).then_inc(act_dve, 1)
                act.wait_ge(filled[0], got.add(1))
                A.activation(kdn[:], bank()[:, 0:NT * P].rearrange("p (t d) -> p t d", t=NT), ACT.Copy).then_inc(took[0], 1)
                for u in range(NT * QH):
                    t = u // QH
                    k = (t + 1) * P
                    act.wait_ge(dve_act, from_dve.add(1))
                    for m in range(2):
                        c = 26 + 4 * (u % 2) + m
                        o = 32 + 2 * (u % 2) + m
                        ins = A.activation(sS[:, u % 2, m, 0:k], sS[:, u % 2, m, 0:k], ACT.Exp,
                                           bias=st[:, c:c + 1], scale=QK ** -0.5, accum_out=st[:, o:o + 1])
                    ins.then_inc(act_dve, 1)
                    act.wait_ge(filled[0], got.add(1))
                    A.activation(aT[:, 0:k], bank()[:, 0:k], ACT.Copy).then_inc(took[0], 1)
                A.activation(ajunk[:, 0:1], st[:, 20:21], ACT.Copy).then_inc(act_pe, 1)
                with turns(act, NT, {from_pool: 2, from_pe: 1}) as t:
                    for c in range(2):
                        act.wait_ge(pool_act, from_pool.add(1))
                        ins = A.activation(M[:, c], M[:, c], ACT.Exp)
                    ins.then_inc(act_dve, 1)
                    act.wait_ge(pe_act, from_pe.add(1))
                    A.activation(atT[:, bass.ds(t, 1), :, :].rearrange("p t h i -> p (t h) i"),
                                 pb[:, 0, 0:CHUNK * GH].rearrange("p (i h) -> p h i", h=GH),
                                 ACT.Copy).then_inc(act_pe, 1)
                act.wait_ge(filled[0], got.add(1))
                A.activation(hT[:, 0:2, :], two(bank()), ACT.Copy).then_inc(took[0], 1)
                act.wait_ge(filled[0], got.add(1))
                A.activation(hT[:, 6:8, :], two(bank()), ACT.Copy).then_inc(took[0], 1)

            def experts(L):
                hT_banks(hT)
                act.wait_ge(filled[0], got.add(1))
                A.activation(keyT[:], bank()[:, 0:2 * P].rearrange("p (a d) -> p a d", a=2), ACT.Copy).then_inc(took[0], 1)
                with turns(act, 2, {got: 4}) as i:
                    for s in range(2):
                        for m in (0, 2):
                            act.wait_ge(filled[0], got.add(1))
                            A.activation(pq[:, bass.ds(i * 8 + s * 4 + m, 1), :], bank()[:, 0:SEQ].unsqueeze(1), ACT.Copy).then_inc(took[0], 1)
                for t in range(NT):
                    for g in (0, 2):
                        act.wait_ge(filled[0], got.add(1))
                        A.activation(score[:, t, 2 * g:2 * g + 2, :, :],
                                 bank().rearrange("p (h m n) -> p h m n", h=2, m=2), ACT.Copy).then_inc(took[0], 1)
                with turns(act, NT * 2, {from_dve: 8, diags: 4 * TOPK}):
                    for j in range(4):
                        act.wait_ge(dve_act, from_dve.add(1))
                        A.activation(gel[:, j, :], hdot[:, j, :], ACT.Gelu)
                        A.activation(gex[:, j, :], csc[:, j, :], ACT.Exp, bias=rsm[:, j, 0:1],
                                     accum_out=rsm[:, j, 1:2]).then_inc(act_dve, 1)
                        act.wait_ge(dve_act, from_dve.add(1))
                        for k in range(TOPK):
                            act.wait_ge(v_used, diags.add(1) + 4 * TOPK + 4)
                            A.activation(diag[:, k % 4, :], ident, ACT.Copy,
                                         scale=wgt[:, j, k:k + 1]).then_inc(diag_ready, 1)

            def swiglu():
                hT_banks(hT)

                def gates(j):
                    for m in range(2):
                        act.wait_ge(pe_act, from_pe.add(1))
                        A.activation(ffs[:, j % 2, m, :], pb[:, 4 + 2 * (j % 2) + m, 0:SEQ],
                                     ACT.Silu).then_inc(act_dve, 1)

                gates(0)
                with turns(act, (NPIECE - 1) // 2, {from_pe: 4}):
                    gates(1)
                    gates(2)
                squares()

            def dilated():
                def load_bias(h):
                    if h >= 2:
                        act.wait_ge(scores_read, NT * (h - 1))
                    act.dma_start(bias[:, h % 2, :, :],
                                  bass.AP(tensor=scratch.tensor, offset=h * NG * TOEPW,
                                          ap=[[1, P], [TOEPW, NG], [1, HANK]])).then_inc(bias_ready[h % 2], 16)

                hT_banks(hT)
                load_bias(0)
                load_bias(1)
                with turns(act, NG, {got: 10}) as g:
                    for dst, c0 in ((qT2, 0), (qT2, 4), (kT2, 0), (kT2, 4)):
                        for m in (0, 2):
                            act.wait_ge(filled[0], got.add(1))
                            A.activation(dst[:, bass.ds(g * KD + c0 + m, 1), :], bank()[:, 0:SEQ].unsqueeze(1), ACT.Copy).then_inc(took[0], 1)
                    for c in range(2):
                        act.wait_ge(filled[0], got.add(1))
                        A.activation(v2[:, 0, bass.ds(g * D + c * CH, CH)], bank(), ACT.Copy).then_inc(took[0], 1)
                for u in range(AH * NT):
                    h, t = divmod(u, NT)
                    act.wait_ge(dve_act, from_dve.add(1))
                    s = ssc[:, u % 2].rearrange("p g k -> p (g k)")
                    A.activation(s, s, ACT.Exp, bias=st[:, 58 + u % 2:59 + u % 2],
                                      accum_out=st[:, 60 + u % 2:61 + u % 2]).then_inc(own_act, own.one())
                    act.wait_ge(own_act, own.at())
                    A.activation(ajunk[:, 0:1], ones[:, 0:1], ACT.Copy).then_inc(act_pe, 1)
                    A.activation(ajunk[:, 1:2], ones[:, 0:1], ACT.Copy).then_inc(act_dve, 1)
                    if t == 1 and h + 2 < AH:
                        load_bias(h + 2)
                    act.wait_ge(filled[0], got.add(1))
                    A.activation(pT2[:, 0:4, :], bank().rearrange("p (j q) -> p j q", j=4), ACT.Copy).then_inc(took[0], 1)
                hT_banks(hT)
                squares()

            def retention():
                hT_banks(hT)
                act.wait_ge(rtab_ready, 32)
                A.activation(dlg[:, 1, :], dlg[:, 0, :], ACT.Exp).then_inc(act_dve, 1)
                act.wait_ge(dve_act, from_dve.add(1))
                A.activation(dlg[:, 5, :], dlg[:, 2, :], ACT.Ln).then_inc(act_dve, 1)
                act.wait_ge(dve_act, from_dve.add(1))
                for dst, c0 in ((rq, 0), (rq, 4), (rk, 0), (rk, 4)):
                    for m in (0, 2):
                        act.wait_ge(filled[0], got.add(1))
                        A.activation(dst[:, c0 + m, :], bank()[:, 0:SEQ], ACT.Copy).then_inc(took[0], 1)

                def decays(h):
                    d = dec[:, :, :].rearrange("p a s -> p (a s)")
                    for b, col in ((0, R_RELF), (1, R_RELB)):
                        ins = A.activation(d[:, b * CH:(b + 1) * CH], rtab[:, col:col + CH], ACT.Exp,
                                           scale=dlg[:, 6, b * RH + h:b * RH + h + 1])
                    ins.then_inc(act_pool, 1)

                decays(0)
                with turns(act, 6, {got: 2}) as i:
                    for s in range(2):
                        act.wait_ge(filled[0], got.add(1))
                        A.activation(rg[:, 0, bass.ds(i * 2 * CH + s * CH, CH)], bank(), ACT.Copy).then_inc(took[0], 1)
                act.wait_ge(dve_act, from_dve.add(1))
                act.wait_ge(took[0], got.at() + 2)
                A.activation(rg[:, :, RV:3 * RV], rg[:, :, RV:3 * RV], ACT.Silu).then_inc(own_act, own.one())
                act.wait_ge(own_act, own.at())
                for h in range(RH):
                    act.wait_ge(dve_act, from_dve.add(1))
                    if h + 1 < RH:
                        decays(h + 1)
                    act.wait_ge(dve_act, from_dve.add(1))
                    for n in range(4):
                        A.activation(rn[:, n, :], pb[:, n, :], ACT.Identity, bias=st[:, 12 + n:13 + n],
                                     scale=st[:, 8 + n:9 + n]).then_inc(act_dve, 1)
                hT_banks(hT)
                hT_banks(xnT)
                squares()

            act.sem_inc(took[0], 2)
            with nc.allow_non_contiguous_dma(reason="columns of small parameters"):
                for src, dst in params:
                    act.dma_start(dst, src, allow_slow_non_contiguous=True).then_inc(par_ready, 16)
                act.dma_start(hTflat[0:NBUCKET + 1, 0:NG * TOEPW], a["bucket_onehot"]).then_inc(onehot_ready, 16)
                act.dma_start(junk[0:NBUCKET, 0:NG * AH], a["rel_bias_2"].rearrange("h b -> b h"),
                              allow_slow_non_contiguous=True).then_inc(onehot_ready, 16)
            act.wait_ge(dve_act, from_dve.add(1))
            A.activation(trig[:, 1], trig[:, 2], ACT.Sin)
            A.activation(trig[:, 4], trig[:, 2], ACT.Abs).then_inc(act_dve, 1)
            act.wait_ge(dve_act, from_dve.add(1))
            A.activation(trig[:, 0], trig[:, 5], ACT.Sin).then_inc(act_dve, 1)
            act.wait_ge(took[1], NG + 2)
            act.dma_start(scratch, xnflat[0:AH, 0:NG * TOEPW]).then_inc(toep_stored, 16)
            for stage, L in plan:
                if stage in ("mixer", "experts"):
                    {"mixer": mixer, "experts": experts}[stage](L)
                elif stage != "final":
                    {"swiglu": swiglu, "dilated": dilated, "retention": retention}[stage]()

        @block.gpsimd
        def _(pool):
            G = nc.gpsimd
            own = Tally()
            from_dve, from_act = Tally(), Tally()
            us, vs = Tally(), Tally()
            rows = [0]

            def load_gains():
                n = rows[0]
                rows[0] += 1
                if n < n_norms:
                    pool.dma_start(grow[:, n % 2, :], gains[n].partition_broadcast(P)).then_inc(grow_ready[n % 2], 16)

            def root(dst, src, n):
                G.tensor_tensor(dst, src, mhalf[:, 0:n], ALU.pow).then_inc(pool_dve, 1)

            def norm():
                pool.wait_ge(dve_pool, from_dve.add(1))
                root(st[:, 4:6], st[:, 2:4], NT)
                load_gains()

            def mixer(L):
                norm()
                with turns(pool, NT, {from_dve: 2}):
                    for c in range(2):
                        pool.wait_ge(dve_pool, from_dve.add(1))
                        pool.sem_inc(passed, 1)
                        G.affine_select(out=M[:, c], in_=M[:, c], compare_op=ALU.is_ge, fill=masked, base=0,
                                        pattern=[[1, CHUNK], [-1, CHUNK]], channel_multiplier=0).then_inc(pool_act, 1)
                pool.wait_ge(dve_pool, from_dve.add(1))
                root(st[:, 40:56], st[:, 40:56], 16)

            def experts(L):
                norm()
                table_u = a["peer_u"].rearrange("l e d -> (l e) d")
                table_v = a["peer_v"].rearrange("l e d -> (l e) d")
                counts = {from_dve: 4, us: 4 * TOPK, vs: 4 * TOPK}
                with turns(pool, NT * 2, counts):
                    for j in range(4):
                        pool.wait_ge(dve_pool, from_dve.add(1))
                        pool.sem_inc(passed, 1)
                        for k in range(TOPK):
                            pool.wait_ge(u_used, us.add(1))
                            pool.sem_inc(passed, 1)
                            G.indirect_dma_start(
                                out=urow[:, k % RING, :], out_offset=None, in_=table_u,
                                in_offset=bass.IndirectOffsetOnAxis(ap=eid[:, j, k:k + 1], axis=0)
                            ).then_inc(u_ready[k % RING], 16)
                        for k in range(TOPK):
                            pool.wait_ge(v_used, vs.add(1) + 4 * TOPK)
                            pool.sem_inc(passed, 1)
                            G.indirect_dma_start(
                                out=vrow[:, k % RING, :], out_offset=None, in_=table_v,
                                in_offset=bass.IndirectOffsetOnAxis(ap=eid[:, j, k:k + 1], axis=0)
                            ).then_inc(v_ready[k % RING], 16)

            def retention():
                norm()
                pool.wait_ge(dve_pool, from_dve.add(1))
                k4 = rk[:, :, :].rearrange("p (h a) s -> p a h s", a=2)
                cos = rtab[:, R_COS:R_COS + SEQ].unsqueeze(1).broadcast_to([P, RH, SEQ])
                sin = rtab[:, R_SIN:R_SIN + SEQ].unsqueeze(1).broadcast_to([P, RH, SEQ])
                G.tensor_tensor(rtk[:, 0], k4[:, 0], cos, ALU.mult).then_inc(own_pool, own.one())
                G.tensor_tensor(rtk[:, 1], k4[:, 1], sin, ALU.mult).then_inc(own_pool, own.one())
                G.tensor_tensor(rtk[:, 2], k4[:, 0], sin, ALU.mult).then_inc(own_pool, own.one())
                G.tensor_tensor(rtk[:, 3], k4[:, 1], cos, ALU.mult).then_inc(own_pool, own.one())
                pool.wait_ge(own_pool, own.at())
                G.tensor_tensor(k4[:, 0], rtk[:, 0], rtk[:, 1], ALU.subtract).then_inc(own_pool, own.one())
                G.tensor_tensor(k4[:, 1], rtk[:, 2], rtk[:, 3], ALU.add).then_inc(pool_dve, 1)
                pool.wait_ge(own_pool, own.at())
                for h in range(RH):
                    pool.wait_ge(act_pool, from_act.add(1))
                    d = dec[:, :, :].rearrange("p a s -> p (a s)")
                    G.tensor_tensor(d[:, 0:CH], d[:, 0:CH], rtab[:, R_MF:R_MF + CH], ALU.mult).then_inc(own_pool, own.one())
                    G.tensor_tensor(d[:, CH:2 * CH], d[:, CH:2 * CH], rtab[:, R_MB:R_MB + CH], ALU.mult).then_inc(pool_dve, 1)
                    pool.wait_ge(dve_pool, from_dve.add(1))
                    root(st[:, 8:12], st[:, 2:6], 4)
                norm()

            masked = pool.to_reg(NEG)
            G.memset(mhalf[:], -0.5).then_inc(pool_set, 3)
            pool.wait_ge(pool_set, 3)
            pool.wait_ge(tab_ready, 16)
            load_gains()
            for stage, L in plan:
                if stage in ("mixer", "experts"):
                    {"mixer": mixer, "experts": experts}[stage](L)
                elif stage == "final":
                    norm()
                elif stage in ("swiglu", "dilated"):
                    norm()
                    norm()
                else:
                    retention()

        @block.sync
        def _(sp):
            slot, fills, downs = [0], [Tally(), Tally()], [Tally(), Tally()]

            def fill(parts):
                s = slot[0]
                slot[0] ^= 1
                n = fills[s].add(1)
                if not isinstance(n, int) or n > 1:
                    sp.wait_ge(w_free[s], n)
                for off, n, src in parts:
                    dst = w[:, s, off:off + n].rearrange("p (k n) -> p k n", k=src.shape[1])
                    sp.dma_start(dst, src).then_inc(w_ready[s], 16)

            def chunk(mat, col, row=0):
                v = mat[row:row + D, :].rearrange("(k p) n -> p k n", p=P)
                return [(0, KD * CH, v[:, :, bass.ds(col, CH)] if not isinstance(col, int) else v[:, :, col:col + CH])]

            def mixer(L):
                with turns(sp, 3, {fills[0]: 1, fills[1]: 1}) as i:
                    for s in range(2):
                        fill(chunk(a["w_in"][L], i * 2 * CH + s * CH))
                for c in range(2):
                    fill(chunk(a["w_out"][L], c * CH))

            def experts(L):
                with turns(sp, 2, {fills[0]: 1, fills[1]: 1}) as i:
                    for s in range(2):
                        fill(chunk(a["peer_w_q"][L], i * 2 * CH + s * CH))

            def swiglu(l, s):
                wg, wu = (a[n][l, s].rearrange("(k p) n -> p k n", p=P) for n in ("ffn_w_gate_2", "ffn_w_up_2"))
                wdn = a["ffn_w_down_2"][l, s].rearrange("(j m p) n -> p j m n", p=P, m=2)

                def piece(j, s):
                    n = KD * FP
                    c = bass.ds(j * FP, FP)
                    fill([(0, n, wg[:, :, c]), (n, n, wu[:, :, c])])
                    if not isinstance(j, int):
                        sp.wait_ge(wd_free[s], downs[s].add(1))
                    elif posts[0]:
                        sp.wait_ge(pe_dve, mark["sums"][posts[0] - 1])
                    sp.dma_start(wd[:, s, :, :], wdn[:, bass.ds(j, 1), :, :].rearrange("p j m n -> p (j m) n")
                                 ).then_inc(wd_ready[s], 16)

                piece(0, 0)
                with turns(sp, (NPIECE - 1) // 2, {fills[0]: 1, fills[1]: 1, downs[0]: 1, downs[1]: 1}) as i:
                    piece(i * 2 + 1, 1)
                    piece(i * 2 + 2, 0)

            def dilated():
                with turns(sp, NG, {fills[0]: 3, fills[1]: 3}) as g:
                    for c in range(6):
                        fill(chunk(a["attn_w_in_2"][0], g * 3 * D + c * CH))
                for c in range(2):
                    fill(chunk(a["attn_w_out_2"][0], c * CH))

            def retention():
                if posts[0]:
                    sp.wait_ge(pe_dve, mark["sums"][posts[0] - 1])
                sp.dma_start(rtab[:], a["ret_tables"]).then_inc(rtab_ready, 16)
                sp.dma_start(dlg[:, 0, :], a["ret_decay_logit_2"].rearrange("o d h -> (o d h)").partition_broadcast(P)).then_inc(rtab_ready, 16)
                with turns(sp, 8, {fills[0]: 1, fills[1]: 1}) as i:
                    for s in range(2):
                        fill(chunk(a["ret_w_in_2"][0], i * 2 * CH + s * CH))
                for r in range(2):
                    for c in range(2):
                        fill(chunk(a["ret_w_out_2"][0], c * CH, r * D))

            sp.dma_start(tab[:], a["tables"]).then_inc(tab_ready, 16)
            sp.dma_start(x[:, :, :], a["x"][0].rearrange("(t p) n -> p t n", p=P)).then_inc(x_ready, 16)
            sp.wait_ge(tab_ready, 16)
            posts = [0]
            for stage, L in plan:
                if stage == "mixer":
                    mixer(L)
                elif stage == "experts":
                    experts(L)
                elif stage == "swiglu":
                    swiglu(L // 2, L % 2)
                elif stage == "dilated":
                    dilated()
                elif stage == "retention":
                    retention()
                posts[0] += stage in ("swiglu", "dilated")
            sp.wait_ge(toep_stored, 16)
            sp.wait_ge(x_done, 1)
            sp.dma_start(out[0].rearrange("(t p) n -> p t n", p=P), x[:, :, :]).then_inc(stored, 16)
            sp.wait_ge(stored, 16)


INPUTS = ["x", "positions", "norm_mix", "w_in", "lam_q1", "lam_k1", "lam_q2", "lam_k2", "diff_norm", "conv_w",
          "gla_w_gate2", "gla_b_gate", "gla_norm", "w_out", "norm_ffn", "peer_w_q", "peer_keys1", "peer_keys2",
          "peer_u", "peer_v", "norm_final", "norm_gains_2", "ffn_w_gate_2", "ffn_w_up_2", "ffn_w_down_2",
          "attn_w_in_2", "attn_w_out_2", "rel_bias_2", "ret_w_in_2", "ret_w_out_2", "ret_decay_logit_2"]


def kernel(**inputs):
    import concourse.bacc as bacc
    from concourse.bass_utils import run_bass_kernel_spmd

    nc = bacc.Bacc("TRN2", target_bir_lowering=False, num_devices=1)
    arrays = {name: np.ascontiguousarray(inputs[name]) for name in INPUTS}
    arrays.update(constants())
    aps = {name: nc.dram_tensor(f"in_{name}", v.shape, mybir.dt.from_np(v.dtype), kind="ExternalInput").ap()
           for name, v in arrays.items()}
    scratch = nc.dram_tensor("bias_rows", (AH, NG * TOEPW), f32).ap()
    out = nc.dram_tensor("out", (1, SEQ, D), f32, kind="ExternalOutput").ap()
    program(nc, aps, out, scratch, PLAN)
    r = run_bass_kernel_spmd(nc, [{f"in_{k}": v for k, v in arrays.items()}], core_ids=[0])
    return r.results[0]["out"]
```

```python
import concourse.bass as bass
from concourse import mybir
from concourse.alu_op_type import AluOpType as ALU
from contextlib import ExitStack, contextmanager
import math
import numpy as np

f32 = mybir.dt.float32
u32 = mybir.dt.uint32
i32 = mybir.dt.int32
ACT = mybir.ActivationFunctionType
AX = mybir.AxisListType.X

P = 128
SEQ = 256
NT = SEQ // P
D = 1024
KD = D // P
DEPTH = 2
EPS = 1e-6

QH = 4
QK = 64
COL_Q, COL_K, COL_V, COL_B, COL_C, COL_H, COL_GQ, COL_GK, COL_GV, COL_GR, COL_LR = (
    0, 512, 1024, 1536, 1792, 2048, 2304, 2432, 2560, 2816, 3072)
IN_W = 3088
RANK = IN_W - COL_LR
ROT = 8
CHUNK = 64
NCH = SEQ // CHUNK
SUB = CHUNK // 2
GH, GDK, GDV = 4, 32, 64
PH = 8
NKEY = 128
TOPK = 16
RING = 8

FF = 2816
FP = 256
NPIECE = FF // FP
NG = 3
AH = 16
ADH = 64
DIL = (1, 4, 16)
RADIUS = 64
NEG = -1e30
NBUCKET = 32
RH = 4
RV = 2048

CH = 512
SLOT = KD * CH

C_ID, C_MASK, C_SEL, C_BD, C_IOTA, C_INV = 0, 128, 384, 388, 644, 660
C_N = 668
R_COS, R_SIN, R_RELF, R_MF, R_RELB, R_MB = 0, 256, 512, 1024, 1536, 2048
R_N = 2560
TOEP = 2 * SEQ - 1
TOEPW = 512
HANK = 3 * P


def constants():
    c = np.zeros((P, C_N), np.float32)
    c[:, C_ID:C_ID + P] = np.eye(P)
    q, k = np.arange(P)[:, None], np.arange(P)[None]
    c[:, C_MASK + P:C_MASK + 2 * P] = np.where(k <= q, 0.0, NEG)
    c[:, C_SEL:C_SEL + GH] = (q // GDK == np.arange(GH)[None]) * np.float32(GDK ** -0.5)
    c[:, C_BD:C_BD + SEQ] = (q // GDK == np.arange(GH * GDV)[None] // GDV)
    c[:, C_IOTA:C_IOTA + TOPK] = np.arange(TOPK)
    c[:, C_INV:C_INV + ROT] = np.float32(500000.0) ** (-np.arange(0, 2 * ROT, 2, dtype=np.float32) / np.float32(2 * ROT))
    r = np.zeros((P, R_N), np.float32)
    inv = (1.0 / (10000.0 ** np.linspace(0.0, 1.0, P, dtype=np.float32))).astype(np.float32)
    ang = inv[:, None] * np.arange(SEQ, dtype=np.float32)[None]
    r[:, R_COS:R_COS + SEQ] = np.cos(ang)
    r[:, R_SIN:R_SIN + SEQ] = np.sin(ang)
    for jt in range(NT):
        rel = np.arange(SEQ)[None] - (jt * P + np.arange(P)[:, None])
        s = slice(jt * SEQ, (jt + 1) * SEQ)
        r[:, R_RELF:R_MF][:, s] = np.maximum(rel, 0)
        r[:, R_MF:R_RELB][:, s] = rel >= 0
        r[:, R_RELB:R_MB][:, s] = np.maximum(-rel, 0)
        r[:, R_MB:R_N][:, s] = rel <= 0
    oh = np.zeros((NBUCKET + 1, NG, TOEPW), np.float32)
    for g, dil in enumerate(DIL):
        rel = SEQ - 1 - np.arange(TOEP)
        half, exact = NBUCKET // 2, NBUCKET // 4
        n = np.abs(rel)
        large = exact + (np.log(np.maximum(n, 1) / exact) / np.log(1024 / exact) * (half - exact)).astype(np.int64)
        large = np.minimum(large, half - 1)
        b = (rel > 0) * half + np.where(n < exact, n, large)
        b = np.where((rel % dil == 0) & (n <= RADIUS * dil), b, NBUCKET)
        oh[b, g, np.arange(TOEP)] = 1.0
    return {"tables": c, "ret_tables": r, "bucket_onehot": oh.reshape(NBUCKET + 1, NG * TOEPW)}


class Tally:

    def __init__(self, n=0):
        self.n, self.turns = n, []

    def at(self):
        v = self.n
        for reg, per in self.turns:
            v = reg * per + v
        return v

    def add(self, k=1):
        self.n += k
        return self.at()

    def one(self):
        self.n += 1
        return 1


@contextmanager
def turns(eng, trips, counted):
    with eng.Fori(0, trips) as i:
        before = {t: t.n for t in counted}
        for t, per in counted.items():
            t.turns.append((i, per))
        yield i
        for t, per in counted.items():
            assert t.n - before[t] == per, (t.n - before[t], per)
            t.turns.pop()
            t.n = before[t] + trips * per



PLAN = [("mixer", 0), ("experts", 0), ("mixer", 1), ("experts", 1), ("final", 0),
        ("swiglu", 0), ("dilated", 0), ("swiglu", 1), ("swiglu", 2), ("retention", 0), ("swiglu", 3)]

ATT_UNITS = [(t, h) for t in range(NT) for h in range(QH)]
GLA_EXPONENTIALS = {1: 0, 3: 1}
GLA_PRODUCTS = {2: 0, 4: 1}
GLA_CONTRACTIONS = {2: 0, 3: 1, 4: 2, 5: 3}
GLA_WEIGHTS = {4: 0, 6: 1}
GLA_STATES = 6

ROUTE_STEPS = 28


def program(nc, a, out, scratch, plan):
    ctx = ExitStack()
    with ctx:
        def sb(name, shape, dt=f32):
            return ctx.enter_context(nc.sbuf_tensor(name, shape, dt))

        def sem(name):
            return ctx.enter_context(nc.semaphore(name))

        x = sb("x", [P, NT, D])
        xn = sb("xn", [P, NT, D])
        hT = sb("hT", [P, KD, SEQ])
        w = sb("w", [P, 2, SLOT])
        wd = sb("wd", [P, 2, 2, D])
        grow = sb("grow", [P, 2, D])
        tab = sb("tab", [P, C_N])
        ident = tab[:, C_ID:C_ID + P]
        mask2 = tab[:, C_MASK:C_MASK + SEQ]
        zero = sb("zero", [1, CH])
        ones = sb("ones", [P, CHUNK])
        mhalf = sb("mhalf", [P, 16])
        st = sb("st", [P, 64])
        junk = sb("junk", [P, D])
        ARENA = 30240
        arena = sb("arena", [P, ARENA])
        pos = [0]

        def part(*shape, at=None):
            if at is not None:
                pos[0] = at
            n = math.prod(shape)
            v = arena[:, pos[0]:pos[0] + n]
            pos[0] += n
            assert pos[0] <= ARENA, pos
            if len(shape) == 1:
                return v
            names = "abcde"[:len(shape)]
            return v.rearrange(f"p ({' '.join(names)}) -> p {' '.join(names)}", **dict(zip(names, shape)))

        lamrow = part(DEPTH, 4, QK, at=0)
        gainrow = part(DEPTH, P)
        glarow = part(DEPTH, GDV)
        convw = part(DEPTH, 2, 3)
        gatew = part(DEPTH, P)
        gateb = part(DEPTH)
        keyn = part(DEPTH, 2, P)
        wtail = part(DEPTH, KD, RANK)
        keyT = part(2, P)
        trig = part(6, NT, ROT)
        posf = part(NT)
        posi = part(NT).bitcast(i32)
        kint = part(NT, ROT).bitcast(i32)
        lrT = part(SEQ)
        mixer = pos[0]
        proj = part(NT, COL_LR)
        tT = part(14, SEQ)
        stt = part(NCH, SEQ)
        rt = stt.rearrange("p a s -> p (a s)").rearrange("p (a t b e) -> p a t b e", a=4, t=NT, b=16)
        sS = part(3, 2, SEQ)
        aN = part(2, SEQ)
        aT = part(SEQ)
        oda = part(NT, QH, P)
        og = part(NT, GH, GDV)
        sgr = part(NT, GH, GDV)
        zg, lg, cb, eb, qb, kd = (part(SEQ) for _ in range(6))
        M = part(NT, 4, SUB, SUB)
        qsel = part(SEQ, GH)
        atT = part(NT, GH, CHUNK)
        kdn = part(NT, P)
        stu = part(SEQ)
        cy = part(SEQ)
        mid = junk[:, P:2 * P + P].rearrange("p (a c i) -> p a c i", a=2, c=NCH)
        qmid = junk[:, CH:2 * CH].rearrange("p (c i h) -> p (c i) h", c=NCH, h=GH)
        score = part(NT, PH, 2, NKEY, at=mixer)
        urow = part(RING, D)
        vrow = part(RING, D)
        xcur = part(D)
        junk2 = part(D)
        diag = part(4, P)
        rsv = part(2, NKEY)
        rs2 = part(2, NKEY)
        rv = part(2, TOPK)
        rif = part(2, TOPK)
        cand = part(TOPK, TOPK)
        cand2 = part(TOPK * TOPK)
        csc = part(4, TOPK)
        caf = part(2, TOPK)
        oh = part(2, TOPK, TOPK)
        ef = part(2, TOPK)
        eidf = part(TOPK)
        hdot = part(4, TOPK)
        gel = part(4, TOPK)
        gex = part(4, TOPK)
        wgt = part(4, TOPK)
        rsm = part(4, 4)
        ri = part(2, TOPK).bitcast(u32)
        ci = part(TOPK).bitcast(u32)
        cab = part(2, TOPK).bitcast(u32)
        eid = part(4, TOPK).bitcast(u32)
        pq = part(4, SEQ)

        ptmp = part(2, CH, at=0)
        second = pos[0]
        ffh = part(2, 2, SEQ)
        ffs = part(2, 2, SEQ)
        qT2 = part(3 * KD, SEQ, at=second)
        kT2 = part(3 * KD, SEQ)
        v2 = part(NT, NG * D)
        bias = part(2, NG, HANK)
        ssc = part(3, NG, SEQ)
        pT2 = part(NG * NT, P)
        o2 = part(NT, D)
        onehot = o2.rearrange("p t n -> p (t n)")[:, 0:NG * TOEPW]
        buckets = pT2.rearrange("p j q -> p (j q)")[:, 0:NG * AH]
        rtab = part(R_N, at=second)
        rq = part(KD, SEQ)
        rk = part(KD, SEQ)
        rg = part(NT, 3 * RV)
        dlg = part(8, 2 * RH)
        bns = part(4, 6)
        mv = part(4, 2)
        dec = part(4, SEQ)
        rotating = pos[0]
        rtmp = part(4, RH, SEQ)
        rtk = part(4, RH, SEQ)
        rn = part(2, 4, CH, at=rotating)
        rp = part(2, 4, SEQ, at=rotating + 4 * RH * SEQ)
        xnflat = xn[:, :, :].rearrange("p t n -> p (t n)")
        xnT = xnflat.rearrange("p (k s) -> p k s", k=KD)
        cells = sb("cells", [P, 4])

        pb = ctx.enter_context(nc.psum_tensor("pb", [P, 8, CH], f32))
        pflat = pb[:, :, :].rearrange("p b n -> p (b n)")

        filled = [sem("bank_filled_for_act"), sem("bank_filled_for_dve")]
        took = [sem("bank_taken_by_act"), sem("bank_taken_by_dve")]
        w_ready = [sem("weights_ready_0"), sem("weights_ready_1")]
        w_free = [sem("weights_free_0"), sem("weights_free_1")]
        wd_ready = [sem("down_weights_ready_0"), sem("down_weights_ready_1")]
        wd_free = [sem("down_weights_free_0"), sem("down_weights_free_1")]
        tab_ready, x_ready, par_ready = sem("tables_ready"), sem("x_ready"), sem("parameters_ready")
        grow_ready = [sem("gains_ready_0"), sem("gains_ready_1")]
        onehot_ready, toep_stored, rtab_ready = sem("onehot_ready"), sem("bias_rows_stored"), sem("ret_tables_ready")
        dve_pe, act_pe = sem("dve_wrote_for_pe"), sem("act_wrote_for_pe")
        dve_act, act_dve = sem("dve_wrote_for_act"), sem("act_wrote_for_dve")
        dve_pool, pool_dve = sem("dve_wrote_for_pool"), sem("pool_wrote_for_dve")
        pool_act, act_pool = sem("pool_wrote_for_act"), sem("act_wrote_for_pool")
        pe_dve, pe_act = sem("pe_summed_for_dve"), sem("pe_summed_for_act")
        pool_set = sem("pool_set_constants")
        own_dve, own_act, own_pool = sem("own_dve"), sem("own_act"), sem("own_pool")
        u_ready = [sem(f"u_row_ready_{r}") for r in range(RING)]
        v_ready = [sem(f"v_row_ready_{r}") for r in range(RING)]
        u_used, v_used, diag_ready = sem("u_rows_used"), sem("v_rows_used"), sem("diagonals_ready")
        bias_ready = [sem("bias_ready_0"), sem("bias_ready_1")]
        bias_first = sem("bias_of_first_heads_ready")
        maps_read = sem("attention_scores_read")
        decays_ready = sem("gla_decays_ready")
        outputs_copied = sem("retention_outputs_copied")
        scores_read = sem("scores_read_by_dve")
        x_done = sem("x_done")
        stored = sem("output_stored")
        mark = {}

        block = ctx.enter_context(nc.Block())

        passed = sem("waits_passed")

        def window(h):
            return bass.AP(tensor=scratch.tensor, offset=h * NG * TOEPW, ap=[[1, P], [TOEPW, NG], [1, HANK]])

        gains = []
        for stage, n in plan:
            g2 = a["norm_gains_2"]
            gains += {
                "mixer": lambda: [a["norm_mix"][n]], "experts": lambda: [a["norm_ffn"][n]],
                "final": lambda: [a["norm_final"]],
                "swiglu": lambda: [g2[n // 2, 4 * (n % 2)], g2[n // 2, 4 * (n % 2) + 1]],
                "dilated": lambda: [g2[0, 2], g2[0, 3]], "retention": lambda: [g2[1, 2], g2[1, 3]],
            }[stage]()
        n_norms = len(gains)
        params = [(a["positions"].rearrange("o (t p) -> p (o t)", p=P), posi)]
        for l in range(DEPTH):
            for n, name in enumerate(("lam_q1", "lam_k1", "lam_q2", "lam_k2")):
                params.append((a[name][l].partition_broadcast(P), lamrow[:, l, n, :]))
            params += [
                (a["diff_norm"][l].partition_broadcast(P), gainrow[:, l, :]),
                (a["gla_norm"][l].partition_broadcast(P), glarow[:, l, :]),
                (a["gla_w_gate2"][l], gatew[0:RANK, l, :]),
                (a["gla_b_gate"][l].rearrange("(p o) -> p o", o=1), gateb[:, l:l + 1]),
                (a["peer_keys1"][l], keyn[:, l, 0, :]),
                (a["peer_keys2"][l], keyn[:, l, 1, :]),
                (a["w_in"][l].rearrange("(k p) n -> p k n", p=P)[:, :, COL_LR:IN_W], wtail[:, l, :, :]),
            ]
            for b in range(2):
                params.append((a["conv_w"][l][:, b * P:(b + 1) * P].rearrange("j p -> p j"), convw[:, l, b, :]))
        PAR = 16 * len(params)

        @block.tensor
        def _(pe):
            given = [Tally(), Tally()]
            from_dve, from_act = Tally(), Tally()
            filledw = [Tally(), Tally()]
            slot, spent = [0], [1]

            def ring(e):
                return pb[:, 4 + e + 2 * ((given[e].n - 1) % 2), :]

            def next_slot():
                slot[0] ^= 1
                return slot[0] ^ 1

            def release(ins):
                if spent[0] is not None:
                    ins.then_inc(w_free[spent[0]], 1)
                    spent[0] = None

            def chunk_natural(src, readers, banks=None, first=True, last=True):
                s = next_slot()
                pe.wait_ge(w_ready[s], filledw[s].add(16))
                wk = w[:, s, :].rearrange("p (k n) -> p k n", k=KD)
                for t in range(NT):
                    if banks is None:
                        pe.wait_ge(took[readers[t]], given[readers[t]].add(1))
                        o = ring(readers[t])
                    else:
                        o = pb[:, banks[t], :]
                    for k in range(KD):
                        ins = nc.tensor.matmul(o, src[:, k, t * P:(t + 1) * P], wk[:, k, :],
                                               start=first and k == 0, stop=last and k == KD - 1)
                        if t == 0 and k == 0:
                            release(ins)
                    if banks is None:
                        ins.then_inc(filled[readers[t]], 1)
                spent[0] = s
                return ins

            def chunk_transposed(readers=(0, 1)):
                s = next_slot()
                pe.wait_ge(w_ready[s], filledw[s].add(16))
                wk = w[:, s, :].rearrange("p (k n) -> p k n", k=KD)
                for m in range(CH // P):
                    e = readers[m % 2]
                    pe.wait_ge(took[e], given[e].add(1))
                    o = ring(e)
                    for k in range(KD):
                        ins = nc.tensor.matmul(o[:, 0:SEQ], wk[:, k, m * P:(m + 1) * P], hT[:, k, :],
                                               start=k == 0, stop=k == KD - 1)
                        if m == 0 and k == 0:
                            release(ins)
                    ins.then_inc(filled[e], 1)
                spent[0] = s

            maps = Tally()
            sums, filledwd = Tally(), [Tally(), Tally()]

            def transpose_into(e, ins_):
                pe.wait_ge(took[e], given[e].add(1))
                o = ring(e)
                for j, tile in enumerate(ins_):
                    ins = nc.tensor.transpose(o[:, j * P:(j + 1) * P], tile, ident)
                ins.then_inc(filled[e], 1)

            def natural_to_hT(src):
                banks = []
                for c in range(KD // 2):
                    pe.wait_ge(took[c % 2], given[c % 2].add(1))
                    banks.append(ring(c % 2))
                for t in range(NT):
                    pe.wait_ge(dve_pe, from_dve.add(1))
                    for b in range(KD):
                        j = b % 2 * NT + t
                        ins = nc.tensor.transpose(banks[b // 2][:, j * P:(j + 1) * P], src[:, t, b * P:(b + 1) * P], ident)
                        if t == NT - 1 and b % 2:
                            ins.then_inc(filled[b // 2 % 2], 1)
                pe.wait_ge(took[0], given[0].at() + 2)
                pe.wait_ge(took[1], given[1].at() + 2)

            def mixer(L):
                natural_to_hT(xn)
                pe.wait_ge(par_ready, PAR)
                pe.wait_ge(took[1], given[1].add(1))
                o = ring(1)
                for k in range(KD):
                    ins = nc.tensor.matmul(o[0:RANK, 0:SEQ], wtail[:, L, k, :], hT[:, k, :],
                                           start=k == 0, stop=k == KD - 1)
                ins.then_inc(filled[1], 1)
                with turns(pe, 3, {given[0]: 2, given[1]: 2, filledw[0]: 16, filledw[1]: 16}):
                    for _ in range(2):
                        chunk_natural(hT, (0, 1))
                pe.wait_ge(took[0], given[0].at() + 2)
                pe.wait_ge(took[1], given[1].at() + 2)
                mark["proj", L] = given[0].n
                pe.wait_ge(took[1], given[1].add(1))
                o = ring(1)
                nc.tensor.matmul(o[:, 0:SEQ], gatew[0:RANK, L, :], lrT[0:RANK, :],
                                 start=True, stop=True).then_inc(filled[1], 1)
                cols = [COL_GQ, COL_GK] + [COL_Q + P * b for b in range(4)] + [COL_K + P * b for b in range(4)]
                cols += [COL_B, COL_B + P, COL_C, COL_C + P]
                for n in range(7):
                    if n == 1:
                        pe.wait_ge(dve_pe, from_dve.add(1))
                    transpose_into(n % 2, [proj[:, t, cols[2 * n + b]:cols[2 * n + b] + P]
                                           for b in range(2) for t in range(NT)])
                mark["tT", L] = given[0].n
                pe.wait_ge(took[0], given[0].at() + 2)
                pe.wait_ge(took[1], given[1].at() + 2)

                def scores(u):
                    t, h = ATT_UNITS[u]
                    if u:
                        pe.wait_ge(maps_read, maps.add(2))
                    elif maps.n:
                        maps.add(2)
                    for m in range(2):
                        r = slice(m * QK, (m + 1) * QK)
                        ins = nc.tensor.matmul(pb[:, 2 + m, 0:(t + 1) * P],
                                               tT[r, 2 + h, t * P:(t + 1) * P], tT[r, 6 + h, 0:(t + 1) * P],
                                               start=True, stop=True)
                    ins.then_inc(pe_dve, sums.one())

                scores(0)
                scores(1)
                pe.wait_ge(dve_pe, from_dve.add(1))
                transpose_into(0, [kd[:, t * P:(t + 1) * P] for t in range(NT)])
                for u, (t, h) in enumerate(ATT_UNITS):
                    pe.wait_ge(dve_pe, from_dve.add(1))
                    transpose_into(0, [aN[:, u % 2, j * P:(j + 1) * P] for j in range(t + 1)])
                    if u + 2 < len(ATT_UNITS):
                        scores(u + 2)
                    pe.wait_ge(took[0], given[0].at() + 2)
                    pe.wait_ge(took[1], given[1].add(1))
                    o = ring(1)
                    for j in range(t + 1):
                        ins = nc.tensor.matmul(o[:, 0:P], aT[:, j * P:(j + 1) * P],
                                               proj[:, j, COL_V + h * P:COL_V + (h + 1) * P],
                                               start=j == 0, stop=j == t)
                    ins.then_inc(filled[1], 1)
                    if u in GLA_CONTRACTIONS:
                        c = GLA_CONTRACTIONS[u]
                        if c % 2 == 0:
                            pe.wait_ge(dve_pe, from_dve.add(1))
                        for a in range(2):
                            rows = slice(c % 2 * CHUNK + a * SUB, c % 2 * CHUNK + (a + 1) * SUB)
                            for i in range(SUB):
                                ins = nc.tensor.matmul(pb[rows, c // 2, (a * SUB + i) * GH:(a * SUB + i + 1) * GH],
                                                       M[:, c // 2, c % 2 * 2 + a, i, :],
                                                       qsel[:, c * CHUNK + a * SUB + i, :], start=True, stop=True)
                        rows = slice(c % 2 * CHUNK, c % 2 * CHUNK + SUB)
                        ins = nc.tensor.matmul(pb[rows, c // 2, SUB * GH:CHUNK * GH], mid[:, 0, c, :],
                                               qmid[:, c * SUB:(c + 1) * SUB, :].rearrange("p i h -> p (i h)"),
                                               start=True, stop=True)
                        if c % 2:
                            ins.then_inc(pe_act, 1)
                    if u == GLA_STATES:
                        for c in range(NCH - 1):
                            t, r = c // 2, slice((c % 2) * CHUNK, (c % 2 + 1) * CHUNK)
                            pe.wait_ge(took[1], given[1].add(1))
                            nc.tensor.matmul(ring(1)[:, 0:SEQ], kdn[r, t, :], proj[r, t, COL_GV:COL_GV + SEQ],
                                             start=True, stop=True).then_inc(filled[1], 1)
                pe.wait_ge(act_pe, from_act.add(NT))
                for t in range(NT):
                    pe.wait_ge(took[1], given[1].add(1))
                    o = ring(1)
                    for c in (2 * t, 2 * t + 1):
                        r = slice((c % 2) * CHUNK, (c % 2 + 1) * CHUNK)
                        for h in range(GH):
                            ins = nc.tensor.matmul(o[r, h * GDV:(h + 1) * GDV], atT[r, t, h, :],
                                                   proj[r, t, COL_GV + h * GDV:COL_GV + (h + 1) * GDV],
                                                   start=True, stop=True)
                    ins.then_inc(filled[1], 1)
                for t in range(NT):
                    pe.wait_ge(took[1], given[1].add(1))
                    o = ring(1)
                    for c in (2 * t, 2 * t + 1):
                        r = slice((c % 2) * CHUNK, (c % 2 + 1) * CHUNK)
                        ins = nc.tensor.matmul(o[r, 0:SEQ], qb[:, c * CHUNK:(c + 1) * CHUNK], stt[:, c, :],
                                               start=True, stop=True)
                    ins.then_inc(filled[1], 1)

                outs = [oda[:, :, h, :] for h in range(QH)] + [
                    og[:, :, 2 * b:2 * b + 2, :].rearrange("p t h e -> p t (h e)") for b in range(2)]
                for n in range(3):
                    if n != 1:
                        pe.wait_ge(dve_pe, from_dve.add(1))
                    transpose_into(n % 2, [outs[2 * n + b][:, t, :] for b in range(2) for t in range(NT)])
                pe.wait_ge(took[0], given[0].at() + 2)
                pe.wait_ge(took[1], given[1].at() + 2)
                for _ in range(2):
                    chunk_natural(hT, (1, 1))

            def experts(L):
                natural_to_hT(xn)
                transpose_into(0, [keyn[:, L, b, :] for b in range(2)])
                for c in range(4):
                    chunk_transposed(readers=(0, 0))
                    pe.wait_ge(took[0], given[0].at() + 2)
                    for t in range(NT):
                        pe.wait_ge(took[0], given[0].add(1))
                        o = ring(0)
                        for b in range(4):
                            ins = nc.tensor.matmul(o[:, b * P:(b + 1) * P], pq[:, b, t * P:(t + 1) * P],
                                                   keyT[:, b % 2, :], start=True, stop=True)
                        ins.then_inc(filled[0], 1)
                    if c == 0:
                        mark["score", L] = given[0].n
                for b in range(4):
                    nc.tensor.matmul(pb[:, b, :], zero[0:1, 0:P], zero[0:1, :], start=True, stop=False)
                with turns(pe, NT, {diags: 8 * TOPK, **{vrows[r]: 16 * 16 for r in range(RING)}}) as t:
                    with turns(pe, 2, {diags: 4 * TOPK, **{vrows[r]: 16 * 8 for r in range(RING)}}):
                        for u in range(4):
                            for k in range(TOPK):
                                pe.wait_ge(diag_ready, diags.add(1))
                                pe.wait_ge(v_ready[k % RING], vrows[k % RING].add(16))
                                for half in range(2):
                                    ins = nc.tensor.matmul(pflat[:, bass.ds(t * D + half * CH, CH)],
                                                           diag[:, k % 4, :],
                                                           vrow[:, k % RING, half * CH:(half + 1) * CH],
                                                           start=False, stop=False, skip_group_check=True)
                                ins.then_inc(v_used, 1)
                for b in range(4):
                    ins = nc.tensor.matmul(pb[:, b, :], zero[0:1, 0:P], zero[0:1, :], start=False, stop=True)
                ins.then_inc(pe_dve, sums.one())

            diags, vrows = Tally(), [Tally() for _ in range(RING)]

            def swiglu():
                natural_to_hT(xn)
                def gate_up(j):
                    s = next_slot()
                    pe.wait_ge(w_ready[s], filledw[s].add(32))
                    wk = w[:, s, :].rearrange("p (a k n) -> p a k n", a=2, k=KD)
                    for m in range(2):
                        o = pb[:, 4 + 2 * (j % 2) + m, :]
                        for g in range(2):
                            for k in range(KD):
                                ins = nc.tensor.matmul(o[:, g * SEQ:(g + 1) * SEQ],
                                                       wk[:, g, k, m * P:(m + 1) * P], hT[:, k, :],
                                                       start=k == 0, stop=k == KD - 1)
                                if m == 0 and g == 0 and k == 0:
                                    release(ins)
                        ins.then_inc(pe_act, 1)
                    spent[0] = s

                def down(j, free_w=True, last=False):
                    s = j % 2
                    pe.wait_ge(wd_ready[s], filledwd[s].add(16))
                    pe.wait_ge(dve_pe, from_dve.add(2))
                    for m in range(2):
                        for t in range(NT):
                            for half in range(2):
                                ins = nc.tensor.matmul(pb[:, 2 * t + half, :], ffh[:, s, m, t * P:(t + 1) * P],
                                                       wd[:, s, m, half * CH:(half + 1) * CH],
                                                       start=j == 0 and m == 0, stop=last and m == 1,
                                                       skip_group_check=True)
                                if free_w:
                                    release(ins)
                    if last:
                        ins.then_inc(pe_dve, sums.one())
                        mark.setdefault("sums", []).append(sums.n)
                    else:
                        ins.then_inc(wd_free[s], 1)

                gate_up(0)
                gate_up(1)
                down(0)
                with turns(pe, (NPIECE - 3) // 2, {filledw[0]: 32, filledw[1]: 32, filledwd[0]: 16, filledwd[1]: 16,
                                                   from_dve: 4}):
                    gate_up(2)
                    down(1)
                    gate_up(3)
                    down(2)
                gate_up(NPIECE - 1)
                down(NPIECE - 2, free_w=False)
                down(NPIECE - 1, free_w=False, last=True)

            def dilated():
                natural_to_hT(xn)
                pe.wait_ge(onehot_ready, 32)
                for g in range(NG):
                    pe.wait_ge(took[1], given[1].add(1))
                    nc.tensor.matmul(ring(1)[0:AH, :], buckets[0:NBUCKET + 1, g * AH:(g + 1) * AH],
                                     onehot[0:NBUCKET + 1, g * TOEPW:(g + 1) * TOEPW],
                                     start=True, stop=True).then_inc(filled[1], 1)
                mark["bias"] = given[1].n
                with turns(pe, NG, {given[0]: 10, given[1]: 10, filledw[0]: 48, filledw[1]: 48}):
                    for _ in range(4):
                        chunk_transposed()
                    for _ in range(2):
                        chunk_natural(hT, (0, 1))
                pe.wait_ge(took[0], given[0].at() + 2)
                pe.wait_ge(took[1], given[1].at() + 2)
                units = [(h, t) for h in range(AH) for t in range(NT)]

                def scores(u):
                    h, t = units[u]
                    r = slice((h % 2) * ADH, (h % 2 + 1) * ADH)
                    if u >= 2:
                        pe.wait_ge(scores_read, u - 1)
                    for g in range(NG):
                        o = pflat[:, (u % 2) * D + g * SEQ:(u % 2) * D + (g + 1) * SEQ]
                        ins = nc.tensor.matmul(o, qT2[r, g * KD + h // 2, t * P:(t + 1) * P],
                                               kT2[r, g * KD + h // 2, :], start=True, stop=True)
                    ins.then_inc(pe_dve, sums.one())

                scores(0)
                scores(1)
                for u, (h, t) in enumerate(units):
                    pe.wait_ge(act_pe, from_act.add(1))
                    flat = ssc[:, u % 3, :, :].rearrange("p g k -> p (g k)")
                    transpose_into(0, [flat[:, j * P:(j + 1) * P] for j in range(4)])
                    transpose_into(1, [flat[:, j * P:(j + 1) * P] for j in range(4, 6)])
                    if u + 2 < len(units):
                        scores(u + 2)
                    pe.wait_ge(took[0], given[0].at() + 2)
                    pe.wait_ge(took[1], given[1].at() + 2)
                    pe.wait_ge(took[1], given[1].add(1))
                    o = ring(1)
                    for j in range(6):
                        g, kt = j // 2, j % 2
                        ins = nc.tensor.matmul(o[:, 0:ADH], pT2[:, j, :],
                                               v2[:, kt, g * D + h * ADH:g * D + (h + 1) * ADH],
                                               start=j == 0, stop=j == 5)
                    ins.then_inc(filled[1], 1)
                natural_to_hT(o2)
                for c in range(2):
                    ins = chunk_natural(hT, None, banks=(c, 2 + c))
                ins.then_inc(pe_dve, sums.one())
                mark.setdefault("sums", []).append(sums.n)

            def retention():
                natural_to_hT(xn)
                for _ in range(4):
                    chunk_transposed()
                mark["qk"] = given[0].n
                with turns(pe, 6, {given[0]: 2, given[1]: 2, filledw[0]: 16, filledw[1]: 16}):
                    for _ in range(2):
                        chunk_natural(hT, (0, 1))
                pe.wait_ge(took[0], given[0].at() + 2)
                pe.wait_ge(took[1], given[1].at() + 2)
                mark["vg"] = given[0].n
                pe.wait_ge(dve_pe, from_dve.add(1))

                def scores(h):
                    pe.wait_ge(took[1], given[1].add(1))
                    o = ring(1)
                    for jt in range(NT):
                        for kt in range(2):
                            ins = nc.tensor.matmul(o[:, jt * SEQ:(jt + 1) * SEQ],
                                                   rk[:, 2 * h + kt, jt * P:(jt + 1) * P], rq[:, 2 * h + kt, :],
                                                   start=kt == 0, stop=kt == 1)
                    ins.then_inc(filled[1], 1)

                scores(0)
                for h in range(RH):
                    if h + 1 < RH:
                        scores(h + 1)
                    pe.wait_ge(dve_pe, from_dve.add(1))
                    if h:
                        pe.wait_ge(outputs_copied, 4 * h)
                    for d, t in ((0, 0), (0, 1), (1, 0), (1, 1)):
                        js = range(t + 1) if d == 0 else range(t, NT)
                        for j in js:
                            ins = nc.tensor.matmul(pb[:, 2 * d + t, :], rp[:, h % 2, 2 * d + j, t * P:(t + 1) * P],
                                                   rg[:, j, h * CH:(h + 1) * CH],
                                                   start=j == js[0], stop=j == js[-1])
                        ins.then_inc(pe_act, 1)
                pe.wait_ge(dve_pe, from_dve.add(2))
                for r, dst in enumerate((hT, xn)):
                    for c in range(KD // 2):
                        base = RV + r * D + 2 * c * P
                        transpose_into(c % 2, [rg[:, t, base + b * P:base + (b + 1) * P]
                                               for b in range(2) for t in range(NT)])
                pe.wait_ge(took[0], given[0].at() + 2)
                pe.wait_ge(took[1], given[1].at() + 2)
                for r, src in enumerate((hT, xnT)):
                    for c in range(2):
                        ins = chunk_natural(src, None, banks=(c, 2 + c), first=r == 0, last=r == 1)
                ins.then_inc(pe_dve, sums.one())
                mark.setdefault("sums", []).append(sums.n)

            pe.sem_inc(w_free[0], 1)
            pe.sem_inc(wd_free[1], 1)
            pe.sem_inc(v_used, 4 * TOPK + RING)
            pe.wait_ge(tab_ready, 16)
            pe.wait_ge(dve_pe, from_dve.add(1))
            for stage, L in plan:
                {"mixer": mixer, "experts": experts}[stage](L) if stage in ("mixer", "experts") else \
                    {"swiglu": swiglu, "dilated": dilated, "retention": retention, "final": lambda: None}[stage]()

        @block.vector
        def _(dve):
            V = nc.vector
            own = Tally()
            got = Tally()
            from_act, from_pool, from_pe = Tally(), Tally(), Tally()
            norms, cell = [0], [0]

            def bank():
                return pb[:, 5 + 2 * ((got.n - 1) % 2), :]

            def told():
                cell[0] = (cell[0] + 1) % 4
                return V.tensor_copy(cells[:, cell[0]:cell[0] + 1], tab[:, 0:1])

            def gains_row():
                n = norms[0]
                norms[0] += 1
                dve.wait_ge(grow_ready[n % 2], 16 * (n // 2 + 1))
                return grow[:, n % 2, :]

            def norm(dst=None, signal=True):
                if not x_told[0]:
                    told().then_inc(dve_act, 1)
                x_told[0] = False
                V.tensor_tensor_reduce(out=xn[:, 1, :], in0=x[:, 1, :], in1=x[:, 1, :], scale=1.0, scalar=0.0,
                                       op0=ALU.mult, op1=ALU.add, accum_out=st[:, 1:2]).then_inc(own_dve, own.one())
                dve.wait_ge(own_dve, own.at())
                dve.wait_ge(act_dve, from_act.add(1))
                V.tensor_scalar(st[:, 2:4], st[:, 0:2], 1.0 / D, EPS, ALU.mult, ALU.add).then_inc(dve_pool, 1)
                g = gains_row()
                dve.wait_ge(pool_dve, from_pool.add(1))
                for t in range(NT):
                    ins = V.scalar_tensor_tensor(out=(xn if dst is None else dst)[:, t, :], in0=x[:, t, :],
                                                 scalar=st[:, 4 + t:5 + t], in1=g, op0=ALU.mult, op1=ALU.mult)
                    if signal:
                        ins.then_inc(dve_pe, 1)
                    else:
                        ins.then_inc(own_dve, own.one())
                        dve.wait_ge(own_dve, own.at())

            def hT_banks():
                for c in (1, 3):
                    dve.wait_ge(filled[1], got.add(1))
                    V.tensor_copy(hT[:, 2 * c:2 * c + 2, :], two(bank())).then_inc(took[1], 1)

            def two(b):
                return b.rearrange("p (a s) -> p a s", a=2)

            def post_norm(factor):
                g = gains_row()
                for t in range(NT):
                    for h in range(2):
                        cols = slice(h * CH, (h + 1) * CH)
                        dve.wait_ge(act_dve, from_act.add(1))
                        V.scalar_tensor_tensor(out=xn[:, t, cols], in0=pb[:, 2 * t + h, :], scalar=factor,
                                               in1=g[:, cols], op0=ALU.mult, op1=ALU.mult).then_inc(own_dve, own.one())
                halves = st[:, 8:12].rearrange("p (t h) -> p t h", t=2)
                V.tensor_tensor(st[:, 12:14], halves[:, :, 0], halves[:, :, 1], ALU.add).then_inc(own_dve, own.one())
                dve.wait_ge(own_dve, own.at())
                V.tensor_scalar(st[:, 2:4], st[:, 12:14], 1.0 / D, EPS, ALU.mult, ALU.add).then_inc(dve_pool, 1)
                dve.wait_ge(pool_dve, from_pool.add(1))
                for t in range(NT):
                    ins = V.scalar_tensor_tensor(out=x[:, t, :], in0=xn[:, t, :], scalar=st[:, 4 + t:5 + t],
                                                 in1=x[:, t, :], op0=ALU.mult, op1=ALU.add)
                    if t == 0:
                        ins.then_inc(dve_act, 1)
                    else:
                        ins.then_inc(own_dve, own.one())
                dve.wait_ge(own_dve, own.at())
                x_told[0] = True

            x_told = [False]

            def rotation_tables():
                dve.wait_ge(par_ready, PAR)
                V.tensor_copy(posf[:], posi[:]).then_inc(own_dve, own.one())
                dve.wait_ge(own_dve, own.at())
                inv = tab[:, C_INV:C_INV + ROT]
                for t in range(NT):
                    V.tensor_scalar(trig[:, 2, t, :], inv, posf[:, t:t + 1], None, ALU.mult).then_inc(own_dve, own.one())
                dve.wait_ge(own_dve, own.at())
                V.tensor_scalar(trig[:, 3], trig[:, 2], 1.0 / (2.0 * math.pi), None, ALU.mult).then_inc(own_dve, own.one())
                dve.wait_ge(own_dve, own.at())
                V.tensor_copy(kint[:], trig[:, 3]).then_inc(own_dve, own.one())
                dve.wait_ge(own_dve, own.at())
                V.tensor_copy(trig[:, 3], kint[:]).then_inc(own_dve, own.one())
                dve.wait_ge(own_dve, own.at())
                c1, c2 = 6.28125, float(np.float32(np.floor((2 * math.pi - 6.28125) * 2 ** 21) / 2 ** 21))
                for c in (c1, c2, 2 * math.pi - c1 - c2):
                    V.scalar_tensor_tensor(out=trig[:, 2], in0=trig[:, 3], scalar=-c, in1=trig[:, 2],
                                                op0=ALU.mult, op1=ALU.add).then_inc(own_dve, own.one())
                    dve.wait_ge(own_dve, own.at())
                V.tensor_scalar(trig[:, 2], trig[:, 2], 3.1415925, -3.1415925, ALU.min, ALU.max).then_inc(own_dve, own.one())
                dve.wait_ge(own_dve, own.at())
                told().then_inc(dve_act, 1)
                dve.wait_ge(act_dve, from_act.add(1))
                V.tensor_scalar(trig[:, 5], trig[:, 4], -1.0, math.pi / 2, ALU.mult, ALU.add).then_inc(dve_act, 1)
                dve.wait_ge(act_dve, from_act.add(1))

            def mixer(L):
                lam_init = 0.8 - 0.6 * math.exp(-0.3 * L)

                def scores(u):
                    t, h = ATT_UNITS[u]
                    k = (t + 1) * P
                    s = sS[:, u % 3, :, 0:k]
                    dve.wait_ge(pe_dve, from_pe.add(1))
                    for m in range(2):
                        V.tensor_tensor(s[:, m, :], pb[:, 2 + m, 0:k], mask2[:, SEQ - k:SEQ],
                                        ALU.add).then_inc(maps_read, maps.one())
                    dve.wait_ge(maps_read, maps.at())
                    c = 24 + 4 * (u % 3)
                    V.reduce_max(st[:, c:c + 2], s, AX).then_inc(own_dve, own.one())
                    dve.wait_ge(own_dve, own.at())
                    V.tensor_scalar(st[:, c + 2:c + 4], st[:, c:c + 2], -QK ** -0.5, None,
                                    ALU.mult).then_inc(dve_act, 1)

                sel = tab[:, C_SEL:C_SEL + GH].unsqueeze(1)

                def convolution(b):
                    z, y = tT[:, 12 + b, :], cy[:]
                    cw = convw[:, L, b, :]
                    V.tensor_scalar(y, z, cw[:, 2:3], None, ALU.mult).then_inc(own_dve, own.one())
                    dve.wait_ge(own_dve, own.at())
                    for j in (1, 0):
                        d = 2 - j
                        V.scalar_tensor_tensor(out=y[:, d:SEQ], in0=z[:, 0:SEQ - d], scalar=cw[:, j:j + 1],
                                               in1=y[:, d:SEQ], op0=ALU.mult, op1=ALU.add).then_inc(own_dve, own.one())
                        dve.wait_ge(own_dve, own.at())
                    V.tensor_tensor(hT[:, 4 + b, :], y, tT[:, 10 + b, :], ALU.mult).then_inc(own_dve, own.one())
                    dve.wait_ge(own_dve, own.at())

                sg8 = sgr[:, :, :, :].rearrange("p t h e -> p (t h) e")

                def differences(t):
                    b = cb[:, t * P:(t + 1) * P].rearrange("p (a i) -> p a i", a=4)
                    bi = b.unsqueeze(3).broadcast_to([P, 4, SUB, SUB])
                    bj = b.unsqueeze(2).broadcast_to([P, 4, SUB, SUB])
                    V.tensor_tensor(M[:, t], bi, bj, ALU.subtract).then_inc(dve_pool, 1)

                norm()
                hT_banks()
                if L == 0:
                    rotation_tables()
                dve.wait_ge(filled[1], got.add(1))
                V.tensor_copy(lrT[0:RANK, :], bank()[0:RANK, 0:SEQ]).then_inc(took[1], 1)
                with turns(dve, 3, {got: 2}) as i:
                    for s in range(2):
                        dve.wait_ge(filled[1], got.add(1))
                        V.tensor_copy(proj[:, 1, bass.ds(i * 2 * CH + s * CH, CH)], bank()).then_inc(took[1], 1)
                dve.wait_ge(filled[1], got.add(1))
                V.tensor_scalar(zg[:], bank()[:, 0:SEQ], gateb[:, L:L + 1], None, ALU.add).then_inc(took[1], 1)
                dve.wait_ge(took[0], mark["proj", L] + 2)
                dve.wait_ge(took[1], got.at() + 2)
                V.tensor_scalar(lg[:], zg[:], 0.0, None, ALU.min).then_inc(dve_act, 1)
                qk = proj[:, :, 0:2 * CH].rearrange("p t (b e) -> p t b e", b=16)
                for t in range(NT):
                    r1, r2 = qk[:, t, :, 0:ROT], qk[:, t, :, ROT:2 * ROT]
                    c = trig[:, 0, t, :].unsqueeze(1).broadcast_to([P, 16, ROT])
                    s = trig[:, 1, t, :].unsqueeze(1).broadcast_to([P, 16, ROT])
                    V.tensor_tensor(rt[:, 0, t], r1, c, ALU.mult).then_inc(own_dve, own.one())
                    V.tensor_tensor(rt[:, 1, t], r2, s, ALU.mult).then_inc(own_dve, own.one())
                    V.tensor_tensor(rt[:, 2, t], r1, s, ALU.mult).then_inc(own_dve, own.one())
                    V.tensor_tensor(rt[:, 3, t], r2, c, ALU.mult).then_inc(own_dve, own.one())
                    dve.wait_ge(own_dve, own.at())
                    V.tensor_tensor(r1, rt[:, 0, t], rt[:, 1, t], ALU.subtract).then_inc(own_dve, own.one())
                    V.tensor_tensor(r2, rt[:, 2, t], rt[:, 3, t], ALU.add).then_inc(own_dve, own.one())
                V.tensor_tensor(proj[:, :, COL_C:COL_C + SEQ], proj[:, :, COL_C:COL_C + SEQ],
                                     proj[:, :, COL_H:COL_H + SEQ], ALU.mult).then_inc(own_dve, own.one())
                dve.wait_ge(own_dve, own.at())
                told().then_inc(dve_pe, 1)
                for n in (1, 3, 5):
                    dve.wait_ge(filled[1], got.add(1))
                    V.tensor_copy(tT[:, 2 * n:2 * n + 2, :], two(bank())).then_inc(took[1], 1)
                for m in range(2):
                    V.tensor_tensor_reduce(out=junk[:, m * QK:(m + 1) * QK], in0=lamrow[:, L, 2 * m, :],
                                                in1=lamrow[:, L, 2 * m + 1, :], scale=1.0, scalar=0.0,
                                                op0=ALU.mult, op1=ALU.add, accum_out=st[:, 16 + m:17 + m]).then_inc(own_dve, own.one())
                dve.wait_ge(own_dve, own.at())
                told().then_inc(dve_act, 1)
                dve.wait_ge(act_dve, from_act.add(1))
                V.tensor_tensor(lg[:], lg[:], qb[:], ALU.subtract).then_inc(own_dve, own.one())
                dve.wait_ge(own_dve, own.at())
                for c in range(NCH):
                    s = slice(c * CHUNK, (c + 1) * CHUNK)
                    V.tensor_tensor_scan(out=zg[:, s], data0=ones[:], data1=lg[:, s], initial=0.0,
                                              op0=ALU.mult, op1=ALU.add).then_inc(own_dve, own.one())
                dve.wait_ge(own_dve, own.at())
                V.tensor_scalar(cb[:], zg[:], 1.0 / 16.0, None, ALU.mult).then_inc(own_dve, own.one())
                dve.wait_ge(own_dve, own.at())
                cb4 = cb[:, :].rearrange("p (c a i) -> p c a i", c=NCH, a=2)
                edge = cb4[:, :, 0, SUB - 1:SUB].broadcast_to([P, NCH, SUB])
                V.tensor_tensor(mid[:, 0], edge, cb4[:, :, 0, :], ALU.subtract).then_inc(own_dve, own.one())
                V.tensor_tensor(mid[:, 1], cb4[:, :, 1, :], edge, ALU.subtract).then_inc(own_dve, own.one())
                qi = tT[:, 0, :].unsqueeze(2).broadcast_to([P, SEQ, GH])
                dve.wait_ge(took[0], mark["tT", L] + 2)
                V.tensor_tensor(qsel[:], qi, sel.broadcast_to([P, SEQ, GH]), ALU.mult).then_inc(own_dve, own.one())
                V.memset(atT[:], 0.0).then_inc(own_dve, own.one())
                dve.wait_ge(own_dve, own.at())
                told().then_inc(dve_act, 1)
                dve.wait_ge(act_dve, from_act.add(1))
                V.tensor_tensor(st[:, 22:23], st[:, 21:22], st[:, 20:21], ALU.subtract).then_inc(own_dve, own.one())
                dve.wait_ge(own_dve, own.at())
                V.tensor_scalar(st[:, 23:24], st[:, 22:23], lam_init, None, ALU.subtract).then_inc(own_dve, own.one())
                dve.wait_ge(own_dve, own.at())
                dve.wait_ge(took[1], got.at() + 2)
                scores(0)
                scores(1)
                differences(0)
                dve.wait_ge(act_dve, from_act.add(1))
                kq = tT[:, 0:2, :].rearrange("p n (c a i) -> p n c a i", c=NCH, a=2)
                V.tensor_tensor(mid[:, 0], mid[:, 0], kq[:, 1, :, 0, :], ALU.mult).then_inc(own_dve, own.one())
                V.tensor_tensor(mid[:, 1], mid[:, 1], kq[:, 0, :, 1, :], ALU.mult).then_inc(own_dve, own.one())
                dve.wait_ge(own_dve, own.at())
                V.tensor_tensor(qmid, mid[:, 1].rearrange("p c i -> p (c i)").unsqueeze(2).broadcast_to([P, P, GH]),
                                sel.broadcast_to([P, P, GH]), ALU.mult).then_inc(own_dve, own.one())
                V.scalar_tensor_tensor(out=qb[:], in0=tT[:, 0, :], scalar=GDK ** -0.5, in1=eb[:],
                                            op0=ALU.mult, op1=ALU.mult).then_inc(own_dve, own.one())
                V.tensor_tensor(kd[:], kd[:], tT[:, 1, :], ALU.mult).then_inc(own_dve, own.one())
                dve.wait_ge(own_dve, own.at())
                told().then_inc(dve_pe, 1)

                for u, (t, h) in enumerate(ATT_UNITS):
                    dve.wait_ge(act_dve, from_act.add(1))
                    k = (t + 1) * P
                    c = 36 + 2 * (u % 3)
                    V.reciprocal(st[:, 42:44], st[:, c:c + 2]).then_inc(own_dve, own.one())
                    dve.wait_ge(own_dve, own.at())
                    V.tensor_scalar(st[:, 44:45], st[:, 43:44], st[:, 23:24], None, ALU.mult).then_inc(own_dve, own.one())
                    V.tensor_scalar(sS[:, u % 3, 0, 0:k], sS[:, u % 3, 0, 0:k], st[:, 42:43], None,
                                    ALU.mult).then_inc(own_dve, own.one())
                    dve.wait_ge(own_dve, own.at())
                    V.scalar_tensor_tensor(out=aN[:, u % 2, 0:k], in0=sS[:, u % 3, 1, 0:k], scalar=st[:, 44:45],
                                           in1=sS[:, u % 3, 0, 0:k], op0=ALU.mult,
                                           op1=ALU.add).then_inc(dve_pe, 1)
                    if u + 2 < len(ATT_UNITS):
                        scores(u + 2)
                    dve.wait_ge(filled[1], got.add(1))
                    V.tensor_copy(oda[:, t, h, :], bank()[:, 0:P]).then_inc(took[1], 1)
                    if u == 0:
                        differences(1)
                    if u in (1, 3):
                        convolution(u // 2)
                    if u == 6:
                        V.tensor_scalar(junk[:, 0:P], gainrow[:, L, :], 1.0 - lam_init, None, ALU.mult).then_inc(own_dve, own.one())
                        V.tensor_tensor(sg8, sg8, glarow[:, L, :].unsqueeze(1).broadcast_to([P, 8, GDV]),
                                        ALU.mult).then_inc(own_dve, own.one())
                        dve.wait_ge(own_dve, own.at())
                    if u in GLA_PRODUCTS:
                        g = GLA_PRODUCTS[u]
                        kj = tT[:, 1, g * P:(g + 1) * P].rearrange("p (a j) -> p a j", a=4).unsqueeze(2)
                        dve.wait_ge(decays_ready, decays.add(1))
                        V.tensor_tensor(M[:, g], M[:, g], kj.broadcast_to([P, 4, SUB, SUB]),
                                        ALU.mult).then_inc(dve_pe, 1)
                    if u == GLA_STATES:
                        V.memset(stt[:, 0, :], 0.0).then_inc(own_dve, own.one())
                        for c in range(NCH - 1):
                            dve.wait_ge(filled[1], got.add(1))
                            V.tensor_tensor(stu[:], bank()[:, 0:SEQ], tab[:, C_BD:C_BD + SEQ],
                                            ALU.mult).then_inc(took[1], 1)
                            dve.wait_ge(took[1], got.at() + 2)
                            e = eb[:, (c + 1) * CHUNK - 1:(c + 1) * CHUNK]
                            if c == 0:
                                V.tensor_copy(stt[:, 1, :], stu[:]).then_inc(own_dve, own.one())
                            else:
                                V.scalar_tensor_tensor(out=stt[:, c + 1, :], in0=stt[:, c, :], scalar=e, in1=stu[:],
                                                       op0=ALU.mult, op1=ALU.add).then_inc(own_dve, own.one())
                            dve.wait_ge(own_dve, own.at())
                dve.wait_ge(took[1], got.at() + 2)
                told().then_inc(dve_act, 1)
                for t in range(NT):
                    dve.wait_ge(filled[1], got.add(1))
                    V.tensor_copy(og[:, t].rearrange("p h e -> p (h e)"), bank()[:, 0:SEQ]).then_inc(took[1], 1)
                dve.wait_ge(took[1], got.at() + 2)
                for t in range(NT):
                    o = og[:, t].rearrange("p h e -> p (h e)")
                    dve.wait_ge(filled[1], got.add(1))
                    V.tensor_tensor(o, bank()[:, 0:SEQ], o, ALU.add).then_inc(took[1], 1)
                dve.wait_ge(act_dve, from_act.add(1))
                V.tensor_scalar(st[:, 40:48], st[:, 40:48], 1.0 / P, EPS, ALU.mult, ALU.add).then_inc(dve_pool, 1)
                dve.wait_ge(took[1], got.at() + 2)
                sq = sS[:, 2, :, :].rearrange("p m k -> p (m k)")
                ogf = og[:, :, :, :].rearrange("p t h e -> p (t h e)")
                V.tensor_tensor(sq, ogf, ogf, ALU.mult).then_inc(own_dve, own.one())
                dve.wait_ge(own_dve, own.at())
                V.reduce_sum(st[:, 48:56], sq.rearrange("p (b e) -> p b e", b=8), AX).then_inc(own_dve, own.one())
                dve.wait_ge(own_dve, own.at())
                V.tensor_scalar(st[:, 48:56], st[:, 48:56], 1.0 / GDV, EPS, ALU.mult, ALU.add).then_inc(dve_pool, 1)
                oda8 = oda[:, :, :, :].rearrange("p t h e -> p (t h) e")
                og8 = og[:, :, :, :].rearrange("p t h e -> p (t h) e")
                V.tensor_tensor(oda8, oda8, junk[:, 0:P].unsqueeze(1).broadcast_to([P, 8, P]), ALU.mult).then_inc(own_dve, own.one())
                dve.wait_ge(own_dve, own.at())
                dve.wait_ge(pool_dve, from_pool.add(1))
                V.tensor_tensor(oda8, oda8, st[:, 40:48].unsqueeze(2).broadcast_to([P, 8, P]), ALU.mult).then_inc(dve_pe, 1)
                dve.wait_ge(pool_dve, from_pool.add(1))
                V.tensor_tensor(og8, og8, st[:, 48:56].unsqueeze(2).broadcast_to([P, 8, GDV]), ALU.mult).then_inc(own_dve, own.one())
                dve.wait_ge(own_dve, own.at())
                V.tensor_tensor(og8, og8, sg8, ALU.mult).then_inc(dve_pe, 1)
                dve.wait_ge(filled[1], got.add(1))
                V.tensor_copy(hT[:, 2:4, :], two(bank())).then_inc(took[1], 1)
                for c in range(2):
                    for t in range(NT):
                        s = slice(c * CH, (c + 1) * CH)
                        dve.wait_ge(filled[1], got.add(1))
                        V.tensor_tensor(x[:, t, s], bank(), x[:, t, s], ALU.add).then_inc(took[1], 1)
                dve.wait_ge(took[1], got.at() + 2)

            def experts(L):
                norm()
                hT_banks()
                sflat = score[:, :, :, :, :].rearrange("p t h m n -> p (t h) m n")
                iota_k = tab[:, C_IOTA:C_IOTA + TOPK].unsqueeze(1).broadcast_to([P, TOPK, TOPK])

                def route(s, j, used_v):
                    dve.wait_ge(v_used, used_v + (j + 1) * TOPK + RING)
                    dve.sem_inc(passed, 1)
                    V.tensor_copy(rsv[:].unsqueeze(1), sflat[:, s]).then_inc(own_dve, own.one())
                    dve.wait_ge(own_dve, own.at())
                    dve.sem_inc(passed, 1)
                    for m in range(2):
                        V.max(rv[:, m, 0:8], rsv[:, m, :]).then_inc(own_dve, own.one())
                        dve.wait_ge(own_dve, own.at())
                        dve.sem_inc(passed, 1)
                        V.max_index(ri[:, m, 0:8], rv[:, m, 0:8], rsv[:, m, :]).then_inc(own_dve, own.one())
                        V.match_replace(rs2[:, m, :], rv[:, m, 0:8], rsv[:, m, :], -3e38).then_inc(own_dve, own.one())
                        dve.wait_ge(own_dve, own.at())
                        dve.sem_inc(passed, 1)
                        V.max(rv[:, m, 8:16], rs2[:, m, :]).then_inc(own_dve, own.one())
                        dve.wait_ge(own_dve, own.at())
                        dve.sem_inc(passed, 1)
                        V.max_index(ri[:, m, 8:16], rv[:, m, 8:16], rs2[:, m, :]).then_inc(own_dve, own.one())
                    dve.wait_ge(own_dve, own.at())
                    dve.sem_inc(passed, 1)
                    V.tensor_tensor(cand[:], rv[:, 0, :].unsqueeze(2).broadcast_to([P, TOPK, TOPK]),
                                         rv[:, 1, :].unsqueeze(1).broadcast_to([P, TOPK, TOPK]), ALU.add).then_inc(own_dve, own.one())
                    V.tensor_copy(rif[:], ri[:]).then_inc(own_dve, own.one())
                    dve.wait_ge(own_dve, own.at())
                    dve.sem_inc(passed, 1)
                    cf = cand[:, :, :].rearrange("p a b -> p (a b)")
                    V.max(csc[:, j, 0:8], cf).then_inc(own_dve, own.one())
                    dve.wait_ge(own_dve, own.at())
                    dve.sem_inc(passed, 1)
                    V.max_index(ci[:, 0:8], csc[:, j, 0:8], cf).then_inc(own_dve, own.one())
                    V.match_replace(cand2[:], csc[:, j, 0:8], cf, -3e38).then_inc(own_dve, own.one())
                    dve.wait_ge(own_dve, own.at())
                    dve.sem_inc(passed, 1)
                    V.max(csc[:, j, 8:16], cand2[:]).then_inc(own_dve, own.one())
                    dve.wait_ge(own_dve, own.at())
                    dve.sem_inc(passed, 1)
                    V.max_index(ci[:, 8:16], csc[:, j, 8:16], cand2[:]).then_inc(own_dve, own.one())
                    dve.wait_ge(own_dve, own.at())
                    dve.sem_inc(passed, 1)
                    V.tensor_single_scalar(cab[:, 0, :], ci[:], 4, ALU.logical_shift_right).then_inc(own_dve, own.one())
                    V.tensor_single_scalar(cab[:, 1, :], ci[:], 15, ALU.bitwise_and).then_inc(own_dve, own.one())
                    dve.wait_ge(own_dve, own.at())
                    dve.sem_inc(passed, 1)
                    V.tensor_copy(caf[:], cab[:]).then_inc(own_dve, own.one())
                    dve.wait_ge(own_dve, own.at())
                    dve.sem_inc(passed, 1)
                    for m in range(2):
                        V.tensor_tensor(oh[:, m], caf[:, m, :].unsqueeze(2).broadcast_to([P, TOPK, TOPK]),
                                             iota_k, ALU.is_equal).then_inc(own_dve, own.one())
                    dve.wait_ge(own_dve, own.at())
                    dve.sem_inc(passed, 1)
                    for m in range(2):
                        V.tensor_tensor(oh[:, m], oh[:, m], rif[:, m, :].unsqueeze(1).broadcast_to([P, TOPK, TOPK]),
                                             ALU.mult).then_inc(own_dve, own.one())
                    dve.wait_ge(own_dve, own.at())
                    dve.sem_inc(passed, 1)
                    V.reduce_sum(ef[:], oh[:], AX).then_inc(own_dve, own.one())
                    dve.wait_ge(own_dve, own.at())
                    dve.sem_inc(passed, 1)
                    V.scalar_tensor_tensor(out=eidf[:], in0=ef[:, 0, :], scalar=float(NKEY), in1=ef[:, 1, :],
                                                op0=ALU.mult, op1=ALU.add).then_inc(own_dve, own.one())
                    dve.wait_ge(own_dve, own.at())
                    dve.sem_inc(passed, 1)
                    V.tensor_scalar(rsm[:, j, 0:1], csc[:, j, 0:1], -1.0, None, ALU.mult).then_inc(own_dve, own.one())
                    V.tensor_scalar(eid[:, j, :], eidf[:], float(L * NKEY * NKEY), None,
                                    ALU.add).then_inc(dve_pool, 1)

                junks = (junk[:], junk2[:])

                def dots(j):
                    for k in range(TOPK):
                        dve.wait_ge(u_ready[k % RING], urows[k % RING].add(16))
                        dve.wait_ge(u_used, used.at() + k - 1 + RING)
                        V.tensor_tensor_reduce(out=junks[k % 2], in0=urow[:, k % RING, :], in1=xcur[:], scale=1.0,
                                               scalar=0.0, op0=ALU.mult, op1=ALU.add,
                                               accum_out=hdot[:, j, k:k + 1]).then_inc(u_used, 1)
                    used.add(TOPK)
                    dve.wait_ge(u_used, used.at() + RING)
                    V.tensor_copy(rsm[:, j, 3:4], rsm[:, j, 0:1]).then_inc(dve_act, 1)
                    dve.wait_ge(act_dve, from_act.add(1))
                    V.reciprocal(rsm[:, j, 2:3], rsm[:, j, 1:2]).then_inc(own_dve, own.one())
                    dve.wait_ge(own_dve, own.at())
                    V.scalar_tensor_tensor(out=wgt[:, j, :], in0=gel[:, j, :], scalar=rsm[:, j, 2:3],
                                           in1=gex[:, j, :], op0=ALU.mult, op1=ALU.mult).then_inc(dve_act, 1)

                def group(g, last=False):
                    tile = xn[:, bass.ds(g // 2, 1), :] if not last else xn[:, NT - 1:NT, :]
                    V.tensor_copy(xcur[:].unsqueeze(1), tile).then_inc(own_dve, own.one())
                    dve.wait_ge(own_dve, own.at())
                    dve.sem_inc(passed, 1)
                    for j in range(4):
                        dots(j)
                        if j < 2:
                            route(bass.ds(g * 4 + j + 2, 1), j + 2, groups.at())
                        elif not last:
                            route(bass.ds(g * 4 + j + 2, 1), j - 2, groups.at() + 4 * TOPK)
                    groups.add(4 * TOPK)

                dve.wait_ge(took[0], mark["score", L] + 2)
                route(slice(0, 1), 0, groups.at())
                route(slice(1, 2), 1, groups.at())
                per = {own: ROUTE_STEPS * 4 + 5, used: 4 * TOPK, groups: 4 * TOPK, from_act: 4,
                       **{urows[r]: 8 * 16 for r in range(RING)}}
                with turns(dve, NT * 2 - 1, per) as g:
                    group(g)
                group(NT * 2 - 1, last=True)
                dve.wait_ge(pe_dve, from_pe.add(1))
                for t in range(NT):
                    for h in range(2):
                        s = slice(h * CH, (h + 1) * CH)
                        V.tensor_tensor(x[:, t, s], pb[:, 2 * t + h, :], x[:, t, s], ALU.add).then_inc(own_dve, own.one())
                dve.wait_ge(own_dve, own.at())

            urows, used, groups = [Tally() for _ in range(RING)], Tally(), Tally()
            maps, decays = Tally(), Tally()

            def swiglu():
                norm()
                hT_banks()

                def hidden(j):
                    for m in range(2):
                        dve.wait_ge(act_dve, from_act.add(1))
                        V.tensor_tensor(ffh[:, j % 2, m, :], ffs[:, j % 2, m, :],
                                        pb[:, 4 + 2 * (j % 2) + m, SEQ:2 * SEQ], ALU.mult).then_inc(dve_pe, 1)

                hidden(0)
                with turns(dve, (NPIECE - 1) // 2, {from_act: 4}):
                    hidden(1)
                    hidden(2)
                dve.wait_ge(pe_dve, from_pe.add(1))
                post_norm(0.5)

            def dilated():
                V.memset(buckets[NBUCKET:NBUCKET + 1, :], NEG).then_inc(own_dve, own.one())
                dve.wait_ge(own_dve, own.at())
                norm()
                hT_banks()
                for g in range(NG):
                    dve.wait_ge(filled[1], got.add(1))
                    V.tensor_copy(xnflat[0:AH, g * TOEPW:(g + 1) * TOEPW], bank()[0:AH, :]).then_inc(took[1], 1)
                with turns(dve, NG, {got: 10}) as g:
                    for dst, c0 in ((qT2, 0), (qT2, 4), (kT2, 0), (kT2, 4)):
                        for m in (1, 3):
                            dve.wait_ge(filled[1], got.add(1))
                            V.tensor_copy(dst[:, bass.ds(g * KD + c0 + m, 1), :], bank()[:, 0:SEQ].unsqueeze(1)).then_inc(took[1], 1)
                    for c in range(2):
                        dve.wait_ge(filled[1], got.add(1))
                        V.tensor_copy(v2[:, 1, bass.ds(g * D + c * CH, CH)], bank()).then_inc(took[1], 1)
                units = [(h, t) for h in range(AH) for t in range(NT)]

                def scores(u):
                    h, t = units[u]
                    if t == 0 and h >= 2:
                        dve.wait_ge(bias_ready[h % 2], 16 * (h // 2))
                    dve.wait_ge(pe_dve, from_pe.add(1))
                    s = ssc[:, u % 3]
                    o = pflat[:, (u % 2) * D:(u % 2) * D + NG * SEQ].rearrange("p (g k) -> p g k", g=NG)
                    c0 = P * t
                    V.scalar_tensor_tensor(out=s, in0=o, scalar=ADH ** -0.5, in1=bias[:, h % 2, :, c0:c0 + SEQ][:, :, ::-1],
                                           op0=ALU.mult, op1=ALU.add).then_inc(scores_read, 1)
                    dve.wait_ge(scores_read, u + 1)
                    c = 16 + u % 3
                    V.reduce_max(st[:, c:c + 1], s.rearrange("p g k -> p (g k)"), AX).then_inc(own_dve, own.one())
                    dve.wait_ge(own_dve, own.at())
                    V.tensor_scalar(st[:, c + 4:c + 5], st[:, c:c + 1], -1.0, None, ALU.mult).then_inc(dve_act, 1)

                dve.wait_ge(bias_first, 32)
                scores(0)
                scores(1)
                for u, (h, t) in enumerate(units):
                    dve.wait_ge(filled[1], got.add(1))
                    V.tensor_copy(pT2[:, 4:6, :], bank()[:, 0:2 * P].rearrange("p (j q) -> p j q", j=2)).then_inc(took[1], 1)
                    r = st[:, 28 + u % 3:29 + u % 3]
                    V.reciprocal(r, st[:, 24 + u % 3:25 + u % 3]).then_inc(own_dve, own.one())
                    if u + 2 < len(units):
                        scores(u + 2)
                    dve.wait_ge(own_dve, own.at())
                    dve.wait_ge(filled[1], got.add(1))
                    V.tensor_scalar(o2[:, t, h * ADH:(h + 1) * ADH], bank()[:, 0:ADH], r, None, ALU.mult).then_inc(took[1], 1)
                dve.wait_ge(took[1], got.at() + 2)
                told().then_inc(dve_pe, NT)
                hT_banks()
                dve.wait_ge(pe_dve, from_pe.add(1))
                post_norm(1.0)

            def retention():
                norm()
                hT_banks()
                dve.wait_ge(rtab_ready, 32)
                dve.wait_ge(act_dve, from_act.add(1))
                V.tensor_scalar(dlg[:, 2, :], dlg[:, 1, :], -1.0, 1.0, ALU.mult, ALU.add).then_inc(own_dve, own.one())
                dve.wait_ge(own_dve, own.at())
                told().then_inc(dve_act, 1)
                V.tensor_scalar(dlg[:, 3, :], dlg[:, 2, :], 1.0, None, ALU.subtract).then_inc(own_dve, own.one())
                dve.wait_ge(own_dve, own.at())
                V.tensor_scalar(dlg[:, 4, :], dlg[:, 3, :], 0.0, None, ALU.is_equal).then_inc(own_dve, own.one())
                dve.wait_ge(own_dve, own.at())
                V.tensor_tensor(dlg[:, 3, :], dlg[:, 3, :], dlg[:, 4, :], ALU.add).then_inc(own_dve, own.one())
                dve.wait_ge(own_dve, own.at())
                V.reciprocal(dlg[:, 3, :], dlg[:, 3, :]).then_inc(own_dve, own.one())
                dve.wait_ge(own_dve, own.at())
                dve.wait_ge(act_dve, from_act.add(1))
                V.tensor_tensor(dlg[:, 5, :], dlg[:, 5, :], dlg[:, 4, :], ALU.add).then_inc(own_dve, own.one())
                dve.wait_ge(own_dve, own.at())
                V.tensor_tensor(dlg[:, 5, :], dlg[:, 5, :], dlg[:, 3, :], ALU.mult).then_inc(own_dve, own.one())
                dve.wait_ge(own_dve, own.at())
                V.tensor_tensor(dlg[:, 5, :], dlg[:, 5, :], dlg[:, 1, :], ALU.mult).then_inc(own_dve, own.one())
                dve.wait_ge(own_dve, own.at())
                V.tensor_scalar(dlg[:, 6, :], dlg[:, 5, :], -1.0, None, ALU.mult).then_inc(dve_act, 1)
                for dst, c0 in ((rq, 0), (rq, 4), (rk, 0), (rk, 4)):
                    for m in (1, 3):
                        dve.wait_ge(filled[1], got.add(1))
                        V.tensor_copy(dst[:, c0 + m, :], bank()[:, 0:SEQ]).then_inc(took[1], 1)
                dve.wait_ge(took[0], mark["qk"] + 2)
                dve.wait_ge(took[1], got.at() + 2)
                told().then_inc(dve_pool, 1)
                q4 = rq[:, :, :].rearrange("p (h a) s -> p a h s", a=2)
                cos = rtab[:, R_COS:R_COS + SEQ].unsqueeze(1).broadcast_to([P, RH, SEQ])
                sin = rtab[:, R_SIN:R_SIN + SEQ].unsqueeze(1).broadcast_to([P, RH, SEQ])
                V.tensor_tensor(rtmp[:, 0], q4[:, 0], cos, ALU.mult).then_inc(own_dve, own.one())
                V.tensor_tensor(rtmp[:, 1], q4[:, 1], sin, ALU.mult).then_inc(own_dve, own.one())
                V.tensor_tensor(rtmp[:, 2], q4[:, 0], sin, ALU.mult).then_inc(own_dve, own.one())
                V.tensor_tensor(rtmp[:, 3], q4[:, 1], cos, ALU.mult).then_inc(own_dve, own.one())
                dve.wait_ge(own_dve, own.at())
                V.tensor_tensor(q4[:, 0], rtmp[:, 0], rtmp[:, 1], ALU.subtract).then_inc(own_dve, own.one())
                V.tensor_tensor(q4[:, 1], rtmp[:, 2], rtmp[:, 3], ALU.add).then_inc(own_dve, own.one())
                dve.wait_ge(own_dve, own.at())
                with turns(dve, 6, {got: 2}) as i:
                    for s in range(2):
                        dve.wait_ge(filled[1], got.add(1))
                        V.tensor_copy(rg[:, 1, bass.ds(i * 2 * CH + s * CH, CH)], bank()).then_inc(took[1], 1)
                dve.wait_ge(took[0], mark["vg"] + 2)
                dve.wait_ge(took[1], got.at() + 2)
                told().then_inc(dve_act, 1)
                dve.wait_ge(pool_dve, from_pool.add(1))
                told().then_inc(dve_pe, 1)

                def decayed(h):
                    dve.wait_ge(pool_dve, from_pool.add(1))
                    dve.wait_ge(filled[1], got.add(1))
                    o = bank()
                    b = rp[:, h % 2, :, :].rearrange("p a s -> p (a s)")
                    dd = dec[:, :, :].rearrange("p a s -> p (a s)")
                    V.scalar_tensor_tensor(out=b[:, 0:CH], in0=o, scalar=1.0 / 16.0, in1=dd[:, 0:CH],
                                           op0=ALU.mult, op1=ALU.mult).then_inc(own_dve, own.one())
                    V.scalar_tensor_tensor(out=b[:, CH:2 * CH], in0=o, scalar=1.0 / 16.0, in1=dd[:, CH:2 * CH],
                                           op0=ALU.mult, op1=ALU.mult).then_inc(took[1], 1)
                    dve.wait_ge(own_dve, own.at())
                    dve.wait_ge(took[1], got.at() + 2)
                    told().then_inc(dve_act, 1)
                    told().then_inc(dve_pe, 1)

                decayed(0)
                for h in range(RH):
                    if h + 1 < RH:
                        decayed(h + 1)
                    if h:
                        combine(h - 1)
                    for n in range(4):
                        dve.wait_ge(outputs_copied, 4 * h + n + 1)
                        V.bn_stats(bns[:, n, :], rn[:, h % 2, n, :]).then_inc(own_dve, own.one())
                    dve.wait_ge(own_dve, own.at())
                    for n in range(4):
                        V.bn_aggr(mv[:, n, :], bns[:, n, :]).then_inc(own_dve, own.one())
                    dve.wait_ge(own_dve, own.at())
                    V.tensor_scalar(st[:, 2:6], mv[:, :, 1], EPS, None, ALU.add).then_inc(dve_pool, 1)
                    dve.wait_ge(pool_dve, from_pool.add(1))
                    V.scalar_tensor_tensor(out=st[:, 12:16], in0=mv[:, :, 0], scalar=-1.0, in1=st[:, 8:12],
                                           op0=ALU.mult, op1=ALU.mult).then_inc(dve_act, 1)
                combine(RH - 1)
                told().then_inc(dve_pe, NT)
                for dst in (hT, xnT):
                    for c in (1, 3):
                        dve.wait_ge(filled[1], got.add(1))
                        V.tensor_copy(dst[:, 2 * c:2 * c + 2, :], two(bank())).then_inc(took[1], 1)
                dve.wait_ge(pe_dve, from_pe.add(1))
                post_norm(1.0)

            def combine(h):
                dve.wait_ge(act_dve, from_act.add(4))
                for t in range(NT):
                    f = rg[:, t, RV + h * CH:RV + (h + 1) * CH]
                    g = rg[:, t, 2 * RV + h * CH:2 * RV + (h + 1) * CH]
                    V.tensor_tensor(f, f, rn[:, h % 2, t, :], ALU.mult).then_inc(own_dve, own.one())
                    V.tensor_tensor(g, g, rn[:, h % 2, 2 + t, :], ALU.mult).then_inc(own_dve, own.one())
                    dve.wait_ge(own_dve, own.at())
                    V.tensor_tensor(f, f, g, ALU.add).then_inc(own_dve, own.one())
                    dve.wait_ge(own_dve, own.at())

            dve.sem_inc(took[1], 2)
            dve.sem_inc(u_used, RING)
            V.memset(zero[:], 0.0)
            V.memset(ones[:], 1.0).then_inc(dve_pe, 1)
            dve.wait_ge(tab_ready, 16)
            dve.wait_ge(x_ready, 16)
            for stage, L in plan:
                if stage == "mixer":
                    mixer(L)
                elif stage == "experts":
                    experts(L)
                elif stage == "final":
                    norm(x, signal=False)
                else:
                    {"swiglu": swiglu, "dilated": dilated, "retention": retention}[stage]()
            told().then_inc(x_done, 1)

        @block.scalar
        def _(act):
            A = nc.scalar
            own = Tally()
            got = Tally()
            from_dve, from_pool, from_pe, diags = Tally(), Tally(), Tally(), Tally()
            posts = [0]

            def bank():
                return pb[:, 4 + 2 * ((got.n - 1) % 2), :]

            def two(b):
                return b.rearrange("p (a s) -> p a s", a=2)

            def hT_banks(dst):
                for c in (0, 2):
                    act.wait_ge(filled[0], got.add(1))
                    A.activation(dst[:, 2 * c:2 * c + 2, :], two(bank()), ACT.Copy).then_inc(took[0], 1)

            rest = [junk[:, 0:CH], junk[:, CH:D], ptmp[:, 0, :], ptmp[:, 1, :]]

            def norm():
                act.wait_ge(dve_act, from_dve.add(1))
                A.activation(xn[:, 0, :], x[:, 0, :], ACT.Square, accum_out=st[:, 0:1]).then_inc(act_dve, 1)

            def squares():
                act.wait_ge(pe_dve, mark["sums"][posts[0]])
                posts[0] += 1
                for b in range(4):
                    A.activation(rest[b], pb[:, b, :], ACT.Square, accum_out=st[:, 8 + b:9 + b]).then_inc(act_dve, 1)

            def rotation_tables():
                act.wait_ge(dve_act, from_dve.add(1))
                A.activation(trig[:, 1], trig[:, 2], ACT.Sin)
                A.activation(trig[:, 4], trig[:, 2], ACT.Abs).then_inc(act_dve, 1)
                act.wait_ge(dve_act, from_dve.add(1))
                A.activation(trig[:, 0], trig[:, 5], ACT.Sin).then_inc(act_dve, 1)

            def mixer(L):
                norm()
                hT_banks(hT)
                if L == 0:
                    rotation_tables()
                with turns(act, 3, {got: 2}) as i:
                    for s in range(2):
                        act.wait_ge(filled[0], got.add(1))
                        A.activation(proj[:, 0, bass.ds(i * 2 * CH + s * CH, CH)], bank(), ACT.Copy).then_inc(took[0], 1)
                act.wait_ge(dve_act, from_dve.add(1))
                act.wait_ge(took[0], got.at() + 2)
                A.activation(sgr[:, :, :, :].rearrange("p t h e -> p t (h e)"), proj[:, :, COL_GR:COL_GR + SEQ], ACT.Silu)
                A.activation(qb[:], zg[:], ACT.Abs).then_inc(own_act, own.one())
                act.wait_ge(own_act, own.at())
                A.activation(qb[:], qb[:], ACT.Exp, scale=-1.0).then_inc(own_act, own.one())
                act.wait_ge(own_act, own.at())
                A.activation(qb[:], qb[:], ACT.Ln, bias=1.0).then_inc(act_dve, 1)
                for n in (0, 2, 4, 6):
                    act.wait_ge(filled[0], got.add(1))
                    A.activation(tT[:, 2 * n:2 * n + 2, :], two(bank()), ACT.Copy).then_inc(took[0], 1)
                act.wait_ge(dve_act, from_dve.add(1))
                A.activation(st[:, 20:22], st[:, 16:18], ACT.Exp).then_inc(act_dve, 1)
                act.wait_ge(dve_act, from_dve.add(1))
                for c in range(NCH):
                    s = slice(c * CHUNK, (c + 1) * CHUNK)
                    A.activation(kd[:, s], cb[:, s], ACT.Exp, bias=cb[:, (c + 1) * CHUNK - 1:(c + 1) * CHUNK], scale=-1.0)
                A.activation(mid[:, :, :, :], mid[:, :, :, :], ACT.Exp)
                A.activation(eb[:], cb[:], ACT.Exp).then_inc(act_dve, 1)

                def exponentials(u):
                    t, h = ATT_UNITS[u]
                    k = (t + 1) * P
                    act.wait_ge(dve_act, from_dve.add(1))
                    for m in range(2):
                        c = 26 + 4 * (u % 3) + m
                        o = 36 + 2 * (u % 3) + m
                        ins = A.activation(sS[:, u % 3, m, 0:k], sS[:, u % 3, m, 0:k], ACT.Exp,
                                           bias=st[:, c:c + 1], scale=QK ** -0.5, accum_out=st[:, o:o + 1])
                    ins.then_inc(act_dve, 1)

                def weights(t):
                    act.wait_ge(pe_act, from_pe.add(1))
                    o = pb[:, t, 0:CHUNK * GH].rearrange("p (i h) -> p h i", h=GH)
                    for r in (slice(0, SUB), slice(CHUNK, CHUNK + SUB)):
                        A.activation(atT[r, t, :, 0:SUB], o[r, :, 0:SUB], ACT.Copy)
                    A.activation(atT[:, t, :, SUB:CHUNK], o[:, :, SUB:CHUNK], ACT.Copy).then_inc(act_pe, 1)

                exponentials(0)
                exponentials(1)
                act.wait_ge(filled[0], got.add(1))
                A.activation(kdn[:], bank()[:, 0:NT * P].rearrange("p (t d) -> p t d", t=NT), ACT.Copy).then_inc(took[0], 1)

                for u, (t, h) in enumerate(ATT_UNITS):
                    k = (t + 1) * P
                    act.wait_ge(filled[0], got.add(1))
                    A.activation(aT[:, 0:k], bank()[:, 0:k], ACT.Copy).then_inc(took[0], 1)
                    if u + 2 < len(ATT_UNITS):
                        exponentials(u + 2)
                    if u in GLA_EXPONENTIALS:
                        act.wait_ge(pool_act, from_pool.add(1))
                        g = GLA_EXPONENTIALS[u]
                        A.activation(M[:, g], M[:, g], ACT.Exp).then_inc(decays_ready, 1)
                    if u in GLA_WEIGHTS:
                        weights(GLA_WEIGHTS[u])
                act.wait_ge(dve_act, from_dve.add(1))
                for n, (t, h) in enumerate(ATT_UNITS):
                    ins = A.activation(sS[:, n // 4, n // 2 % 2, n % 2 * P:(n % 2 + 1) * P], oda[:, t, h, :], ACT.Square,
                                       accum_out=st[:, 40 + n:41 + n])
                ins.then_inc(act_dve, 1)
                act.wait_ge(filled[0], got.add(1))
                A.activation(hT[:, 0:2, :], two(bank()), ACT.Copy).then_inc(took[0], 1)
                act.wait_ge(filled[0], got.add(1))
                A.activation(hT[:, 6:8, :], two(bank()), ACT.Copy).then_inc(took[0], 1)

            def experts(L):
                norm()
                hT_banks(hT)
                act.wait_ge(filled[0], got.add(1))
                A.activation(keyT[:], bank()[:, 0:2 * P].rearrange("p (a d) -> p a d", a=2), ACT.Copy).then_inc(took[0], 1)
                for c in range(4):
                    for b in range(4):
                        act.wait_ge(filled[0], got.add(1))
                        A.activation(pq[:, b, :], bank()[:, 0:SEQ], ACT.Copy).then_inc(took[0], 1)
                    for t in range(NT):
                        act.wait_ge(filled[0], got.add(1))
                        A.activation(score[:, t, 2 * c:2 * c + 2, :, :],
                                     bank().rearrange("p (h m n) -> p h m n", h=2, m=2), ACT.Copy).then_inc(took[0], 1)
                act.wait_ge(took[0], got.at() + 2)
                with turns(act, NT * 2, {from_dve: 8, diags: 4 * TOPK}):
                    for j in range(4):
                        act.wait_ge(dve_act, from_dve.add(1))
                        A.activation(gel[:, j, :], hdot[:, j, :], ACT.Gelu)
                        A.activation(gex[:, j, :], csc[:, j, :], ACT.Exp, bias=rsm[:, j, 0:1],
                                     accum_out=rsm[:, j, 1:2]).then_inc(act_dve, 1)
                        act.wait_ge(dve_act, from_dve.add(1))
                        for k in range(TOPK):
                            act.wait_ge(v_used, diags.add(1) + 4 * TOPK + 4)
                            A.activation(diag[:, k % 4, :], ident, ACT.Copy,
                                         scale=wgt[:, j, k:k + 1]).then_inc(diag_ready, 1)

            def swiglu():
                norm()
                hT_banks(hT)

                def gates(j):
                    for m in range(2):
                        act.wait_ge(pe_act, from_pe.add(1))
                        A.activation(ffs[:, j % 2, m, :], pb[:, 4 + 2 * (j % 2) + m, 0:SEQ],
                                     ACT.Silu).then_inc(act_dve, 1)

                gates(0)
                with turns(act, (NPIECE - 1) // 2, {from_pe: 4}):
                    gates(1)
                    gates(2)
                squares()

            def dilated():
                def load_bias(h):
                    act.wait_ge(scores_read, NT * (h - 1))
                    act.dma_start(bias[:, h % 2, :, :], window(h)).then_inc(bias_ready[h % 2], 16)

                act.dma_start(onehot[0:NBUCKET + 1, :], a["bucket_onehot"]).then_inc(onehot_ready, 16)
                with nc.allow_non_contiguous_dma(reason="a small transposed table"):
                    act.dma_start(buckets[0:NBUCKET, :], a["rel_bias_2"].rearrange("h b -> b h"),
                                  allow_slow_non_contiguous=True).then_inc(onehot_ready, 16)
                norm()
                hT_banks(hT)
                with turns(act, NG, {got: 10}) as g:
                    for dst, c0 in ((qT2, 0), (qT2, 4), (kT2, 0), (kT2, 4)):
                        for m in (0, 2):
                            act.wait_ge(filled[0], got.add(1))
                            A.activation(dst[:, bass.ds(g * KD + c0 + m, 1), :], bank()[:, 0:SEQ].unsqueeze(1), ACT.Copy).then_inc(took[0], 1)
                    for c in range(2):
                        act.wait_ge(filled[0], got.add(1))
                        A.activation(v2[:, 0, bass.ds(g * D + c * CH, CH)], bank(), ACT.Copy).then_inc(took[0], 1)
                for u in range(AH * NT):
                    h, t = divmod(u, NT)
                    act.wait_ge(dve_act, from_dve.add(1))
                    s = ssc[:, u % 3].rearrange("p g k -> p (g k)")
                    A.activation(s, s, ACT.Exp, bias=st[:, 20 + u % 3:21 + u % 3],
                                 accum_out=st[:, 24 + u % 3:25 + u % 3]).then_inc(act_pe, 1)
                    if t == 0 and 0 < h < AH - 1:
                        load_bias(h + 1)
                    act.wait_ge(filled[0], got.add(1))
                    A.activation(pT2[:, 0:4, :], bank().rearrange("p (j q) -> p j q", j=4), ACT.Copy).then_inc(took[0], 1)
                hT_banks(hT)
                squares()

            def retention():
                norm()
                hT_banks(hT)
                act.wait_ge(rtab_ready, 32)
                A.activation(dlg[:, 1, :], dlg[:, 0, :], ACT.Exp).then_inc(act_dve, 1)
                act.wait_ge(dve_act, from_dve.add(1))
                A.activation(dlg[:, 5, :], dlg[:, 2, :], ACT.Ln).then_inc(act_dve, 1)
                act.wait_ge(dve_act, from_dve.add(1))
                for dst, c0 in ((rq, 0), (rq, 4), (rk, 0), (rk, 4)):
                    for m in (0, 2):
                        act.wait_ge(filled[0], got.add(1))
                        A.activation(dst[:, c0 + m, :], bank()[:, 0:SEQ], ACT.Copy).then_inc(took[0], 1)

                def decays(h):
                    d = dec[:, :, :].rearrange("p a s -> p (a s)")
                    for b, col in ((0, R_RELF), (1, R_RELB)):
                        ins = A.activation(d[:, b * CH:(b + 1) * CH], rtab[:, col:col + CH], ACT.Exp,
                                           scale=dlg[:, 6, b * RH + h:b * RH + h + 1])
                    ins.then_inc(act_pool, 1)

                decays(0)
                with turns(act, 6, {got: 2}) as i:
                    for s in range(2):
                        act.wait_ge(filled[0], got.add(1))
                        A.activation(rg[:, 0, bass.ds(i * 2 * CH + s * CH, CH)], bank(), ACT.Copy).then_inc(took[0], 1)
                act.wait_ge(dve_act, from_dve.add(1))
                act.wait_ge(took[0], got.at() + 2)
                A.activation(rg[:, :, RV:3 * RV], rg[:, :, RV:3 * RV], ACT.Silu).then_inc(own_act, own.one())
                act.wait_ge(own_act, own.at())
                act.wait_ge(dve_act, from_dve.add(1))
                decays(1)
                for h in range(RH):
                    if h + 1 < RH:
                        act.wait_ge(dve_act, from_dve.add(1))
                    if h + 2 < RH:
                        decays(h + 2)
                    for n in range(4):
                        act.wait_ge(pe_act, from_pe.add(1))
                        A.activation(rn[:, h % 2, n, :], pb[:, n, :], ACT.Copy).then_inc(outputs_copied, 1)
                    act.wait_ge(dve_act, from_dve.add(1))
                    for n in range(4):
                        A.activation(rn[:, h % 2, n, :], rn[:, h % 2, n, :], ACT.Identity, bias=st[:, 12 + n:13 + n],
                                     scale=st[:, 8 + n:9 + n]).then_inc(act_dve, 1)
                hT_banks(hT)
                hT_banks(xnT)
                squares()

            act.sem_inc(took[0], 2)
            with nc.allow_non_contiguous_dma(reason="columns of small parameters"):
                for src, dst in params:
                    act.dma_start(dst, src, allow_slow_non_contiguous=True).then_inc(par_ready, 16)
            for stage, L in plan:
                if stage in ("mixer", "experts"):
                    {"mixer": mixer, "experts": experts}[stage](L)
                elif stage == "final":
                    norm()
                else:
                    {"swiglu": swiglu, "dilated": dilated, "retention": retention}[stage]()

        @block.gpsimd
        def _(pool):
            G = nc.gpsimd
            own = Tally()
            from_dve, from_act = Tally(), Tally()
            us, vs = Tally(), Tally()
            rows = [0]

            def load_gains():
                n = rows[0]
                rows[0] += 1
                if n < n_norms:
                    pool.dma_start(grow[:, n % 2, :], gains[n].partition_broadcast(P)).then_inc(grow_ready[n % 2], 16)

            def root(dst, src, n):
                G.tensor_tensor(dst, src, mhalf[:, 0:n], ALU.pow).then_inc(pool_dve, 1)

            def norm():
                pool.wait_ge(dve_pool, from_dve.add(1))
                root(st[:, 4:6], st[:, 2:4], NT)
                load_gains()

            def mixer(L):
                norm()
                for t in range(NT):
                    pool.wait_ge(dve_pool, from_dve.add(1))
                    G.affine_select(out=M[:, t], in_=M[:, t], compare_op=ALU.is_ge, fill=masked, base=0,
                                    pattern=[[0, 4], [1, SUB], [-1, SUB]], channel_multiplier=0).then_inc(pool_act, 1)
                for c in (40, 48):
                    pool.wait_ge(dve_pool, from_dve.add(1))
                    root(st[:, c:c + 8], st[:, c:c + 8], 8)

            def experts(L):
                norm()
                table_u = a["peer_u"].rearrange("l e d -> (l e) d")
                table_v = a["peer_v"].rearrange("l e d -> (l e) d")
                counts = {from_dve: 4, us: 4 * TOPK, vs: 4 * TOPK}
                with turns(pool, NT * 2, counts):
                    for j in range(4):
                        pool.wait_ge(dve_pool, from_dve.add(1))
                        pool.sem_inc(passed, 1)
                        for k in range(TOPK):
                            pool.wait_ge(u_used, us.add(1))
                            pool.sem_inc(passed, 1)
                            G.indirect_dma_start(
                                out=urow[:, k % RING, :], out_offset=None, in_=table_u,
                                in_offset=bass.IndirectOffsetOnAxis(ap=eid[:, j, k:k + 1], axis=0)
                            ).then_inc(u_ready[k % RING], 16)
                        for k in range(TOPK):
                            pool.wait_ge(v_used, vs.add(1) + 4 * TOPK)
                            pool.sem_inc(passed, 1)
                            G.indirect_dma_start(
                                out=vrow[:, k % RING, :], out_offset=None, in_=table_v,
                                in_offset=bass.IndirectOffsetOnAxis(ap=eid[:, j, k:k + 1], axis=0)
                            ).then_inc(v_ready[k % RING], 16)

            def dilated():
                norm()
                pool.wait_ge(took[1], mark["bias"] + 2)
                pool.dma_start(scratch, xnflat[0:AH, 0:NG * TOEPW]).then_inc(toep_stored, 16)
                pool.wait_ge(toep_stored, 16)
                for h in range(2):
                    pool.dma_start(bias[:, h, :, :], window(h)).then_inc(bias_first, 16)
                norm()

            def retention():
                norm()
                pool.dma_start(rtab[:], a["ret_tables"]).then_inc(rtab_ready, 16)
                pool.dma_start(dlg[:, 0, :], a["ret_decay_logit_2"].rearrange("o d h -> (o d h)").partition_broadcast(P)
                               ).then_inc(rtab_ready, 16)
                pool.wait_ge(dve_pool, from_dve.add(1))
                k4 = rk[:, :, :].rearrange("p (h a) s -> p a h s", a=2)
                cos = rtab[:, R_COS:R_COS + SEQ].unsqueeze(1).broadcast_to([P, RH, SEQ])
                sin = rtab[:, R_SIN:R_SIN + SEQ].unsqueeze(1).broadcast_to([P, RH, SEQ])
                G.tensor_tensor(rtk[:, 0], k4[:, 0], cos, ALU.mult).then_inc(own_pool, own.one())
                G.tensor_tensor(rtk[:, 1], k4[:, 1], sin, ALU.mult).then_inc(own_pool, own.one())
                G.tensor_tensor(rtk[:, 2], k4[:, 0], sin, ALU.mult).then_inc(own_pool, own.one())
                G.tensor_tensor(rtk[:, 3], k4[:, 1], cos, ALU.mult).then_inc(own_pool, own.one())
                pool.wait_ge(own_pool, own.at())
                G.tensor_tensor(k4[:, 0], rtk[:, 0], rtk[:, 1], ALU.subtract).then_inc(own_pool, own.one())
                G.tensor_tensor(k4[:, 1], rtk[:, 2], rtk[:, 3], ALU.add).then_inc(pool_dve, 1)
                pool.wait_ge(own_pool, own.at())

                def mask(h):
                    pool.wait_ge(act_pool, from_act.add(1))
                    d = dec[:, :, :].rearrange("p a s -> p (a s)")
                    G.tensor_tensor(d[:, 0:CH], d[:, 0:CH], rtab[:, R_MF:R_MF + CH], ALU.mult).then_inc(own_pool, own.one())
                    G.tensor_tensor(d[:, CH:2 * CH], d[:, CH:2 * CH], rtab[:, R_MB:R_MB + CH],
                                    ALU.mult).then_inc(pool_dve, 1)

                mask(0)
                for h in range(RH):
                    if h + 1 < RH:
                        mask(h + 1)
                    pool.wait_ge(dve_pool, from_dve.add(1))
                    root(st[:, 8:12], st[:, 2:6], 4)
                norm()

            masked = pool.to_reg(NEG)
            G.memset(mhalf[:], -0.5).then_inc(pool_set, 3)
            pool.wait_ge(pool_set, 3)
            pool.wait_ge(tab_ready, 16)
            load_gains()
            for stage, L in plan:
                if stage in ("mixer", "experts"):
                    {"mixer": mixer, "experts": experts}[stage](L)
                elif stage == "final":
                    norm()
                elif stage == "swiglu":
                    norm()
                    norm()
                elif stage == "dilated":
                    dilated()
                else:
                    retention()

        @block.sync
        def _(sp):
            slot, fills, downs = [0], [Tally(), Tally()], [Tally(), Tally()]

            def fill(parts):
                s = slot[0]
                slot[0] ^= 1
                n = fills[s].add(1)
                if not isinstance(n, int) or n > 1:
                    sp.wait_ge(w_free[s], n)
                for off, n, src in parts:
                    dst = w[:, s, off:off + n].rearrange("p (k n) -> p k n", k=src.shape[1])
                    sp.dma_start(dst, src).then_inc(w_ready[s], 16)

            def chunk(mat, col, row=0):
                v = mat[row:row + D, :].rearrange("(k p) n -> p k n", p=P)
                return [(0, KD * CH, v[:, :, bass.ds(col, CH)] if not isinstance(col, int) else v[:, :, col:col + CH])]

            def mixer(L):
                with turns(sp, 3, {fills[0]: 1, fills[1]: 1}) as i:
                    for s in range(2):
                        fill(chunk(a["w_in"][L], i * 2 * CH + s * CH))
                for c in range(2):
                    fill(chunk(a["w_out"][L], c * CH))

            def experts(L):
                with turns(sp, 2, {fills[0]: 1, fills[1]: 1}) as i:
                    for s in range(2):
                        fill(chunk(a["peer_w_q"][L], i * 2 * CH + s * CH))

            def swiglu(l, s):
                wg, wu = (a[n][l, s].rearrange("(k p) n -> p k n", p=P) for n in ("ffn_w_gate_2", "ffn_w_up_2"))
                wdn = a["ffn_w_down_2"][l, s].rearrange("(j m p) n -> p j m n", p=P, m=2)

                def piece(j, s):
                    n = KD * FP
                    c = bass.ds(j * FP, FP)
                    fill([(0, n, wg[:, :, c]), (n, n, wu[:, :, c])])
                    if not isinstance(j, int):
                        sp.wait_ge(wd_free[s], downs[s].add(1))
                    elif posts[0]:
                        sp.wait_ge(pe_dve, mark["sums"][posts[0] - 1])
                    sp.dma_start(wd[:, s, :, :], wdn[:, bass.ds(j, 1), :, :].rearrange("p j m n -> p (j m) n")
                                 ).then_inc(wd_ready[s], 16)

                piece(0, 0)
                with turns(sp, (NPIECE - 1) // 2, {fills[0]: 1, fills[1]: 1, downs[0]: 1, downs[1]: 1}) as i:
                    piece(i * 2 + 1, 1)
                    piece(i * 2 + 2, 0)

            def dilated():
                with turns(sp, NG, {fills[0]: 3, fills[1]: 3}) as g:
                    for c in range(6):
                        fill(chunk(a["attn_w_in_2"][0], g * 3 * D + c * CH))
                for c in range(2):
                    fill(chunk(a["attn_w_out_2"][0], c * CH))

            def retention():
                with turns(sp, 8, {fills[0]: 1, fills[1]: 1}) as i:
                    for s in range(2):
                        fill(chunk(a["ret_w_in_2"][0], i * 2 * CH + s * CH))
                for r in range(2):
                    for c in range(2):
                        fill(chunk(a["ret_w_out_2"][0], c * CH, r * D))

            sp.dma_start(x[:, :, :], a["x"][0].rearrange("(t p) n -> p t n", p=P)).then_inc(x_ready, 16)
            sp.dma_start(tab[:], a["tables"]).then_inc(tab_ready, 16)
            posts = [0]
            for stage, L in plan:
                if stage == "mixer":
                    mixer(L)
                elif stage == "experts":
                    experts(L)
                elif stage == "swiglu":
                    swiglu(L // 2, L % 2)
                elif stage == "dilated":
                    dilated()
                elif stage == "retention":
                    retention()
                posts[0] += stage in ("swiglu", "dilated")
            sp.wait_ge(tab_ready, 16)
            if ("dilated", 0) in plan:
                sp.wait_ge(toep_stored, 16)
            sp.wait_ge(x_done, 1)
            sp.dma_start(out[0].rearrange("(t p) n -> p t n", p=P), x[:, :, :]).then_inc(stored, 16)
            sp.wait_ge(stored, 16)


INPUTS = ["x", "positions", "norm_mix", "w_in", "lam_q1", "lam_k1", "lam_q2", "lam_k2", "diff_norm", "conv_w",
          "gla_w_gate2", "gla_b_gate", "gla_norm", "w_out", "norm_ffn", "peer_w_q", "peer_keys1", "peer_keys2",
          "peer_u", "peer_v", "norm_final", "norm_gains_2", "ffn_w_gate_2", "ffn_w_up_2", "ffn_w_down_2",
          "attn_w_in_2", "attn_w_out_2", "rel_bias_2", "ret_w_in_2", "ret_w_out_2", "ret_decay_logit_2"]


def kernel(**inputs):
    import concourse.bacc as bacc
    from concourse.bass_utils import run_bass_kernel_spmd

    nc = bacc.Bacc("TRN2", target_bir_lowering=False, num_devices=1)
    arrays = {name: np.ascontiguousarray(inputs[name]) for name in INPUTS}
    arrays.update(constants())
    aps = {name: nc.dram_tensor(f"in_{name}", v.shape, mybir.dt.from_np(v.dtype), kind="ExternalInput").ap()
           for name, v in arrays.items()}
    scratch = nc.dram_tensor("bias_rows", (AH, NG * TOEPW), f32).ap()
    out = nc.dram_tensor("out", (1, SEQ, D), f32, kind="ExternalOutput").ap()
    program(nc, aps, out, scratch, PLAN)
    r = run_bass_kernel_spmd(nc, [{f"in_{k}": v for k, v in arrays.items()}], core_ids=[0])
    return r.results[0]["out"]
```
